# Optimizing a Trainium2 kernel written in Bass

```python
import jax, jax.numpy as jnp
from jax import lax
import numpy as np
import math

D_MODEL = 1024
BATCH = 1
SEQ = 512
DEPTH = 2

N_A_LAYERS = DEPTH // 2
N_B_LAYERS = DEPTH - N_A_LAYERS
CONV_WIDTH = 3
D_FF = 2816
N_HEADS = 8
QK_NOPE_DIM = 128
QK_ROPE_DIM = 64
V_HEAD_DIM = 128
Q_LORA_RANK = 512
KV_LORA_RANK = 256
ROPE_THETA = 10000.0
RMS_EPS = 1e-6
Q_BLOCK = 128


def rms_norm(x, g):
    xf = x.astype(jnp.float32)
    y = xf * lax.rsqrt(jnp.mean(xf * xf, axis=-1, keepdims=True) + RMS_EPS)
    return (y * g.astype(jnp.float32)).astype(x.dtype)

def causal_dwconv(x, w):
    c = x.shape[-1]
    return lax.conv_general_dilated(
        x, w[:, None, :].astype(x.dtype), window_strides=(1,),
        padding=((CONV_WIDTH - 1, 0),), dimension_numbers=("NWC", "WIO", "NWC"),
        feature_group_count=c)

def rope_tables(seq, dtype):
    inv = 1.0 / (ROPE_THETA ** (jnp.arange(0, QK_ROPE_DIM, 2, dtype=jnp.float32) / QK_ROPE_DIM))
    ang = jnp.arange(seq, dtype=jnp.float32)[:, None] * inv[None, :]
    return jnp.cos(ang).astype(dtype), jnp.sin(ang).astype(dtype)

def apply_rope(x, cos, sin):
    x1, x2 = jnp.split(x, 2, axis=-1)
    return jnp.concatenate([x1 * cos - x2 * sin, x1 * sin + x2 * cos], axis=-1)

def short_conv_mixer(x_n, w_in, conv_w, w_out):
    b, c, h = jnp.split(x_n @ w_in, 3, axis=-1)
    return (b * causal_dwconv(c * h, conv_w)) @ w_out

def conv_ffn(x_n, w_up, conv_w, w_down):
    g, u = jnp.split(causal_dwconv(x_n @ w_up, conv_w), 2, axis=-1)
    return (jax.nn.silu(g) * u) @ w_down

def shared_latent_kv(h, kv_in_norm, w_dkv, kv_norm, w_ukv, cos, sin):
    bsz, seq, _ = h.shape
    ckv = rms_norm(h, kv_in_norm) @ w_dkv
    c_kv, k_rope = ckv[..., :KV_LORA_RANK], ckv[..., KV_LORA_RANK:]
    k_rope = apply_rope(k_rope, cos, sin)
    kv = (rms_norm(c_kv, kv_norm) @ w_ukv).reshape(bsz, seq, N_HEADS, QK_NOPE_DIM + V_HEAD_DIM)
    return kv[..., :QK_NOPE_DIM], kv[..., QK_NOPE_DIM:], k_rope

def mla_attention(x_n, w_dq, q_norm, w_uq, w_o, k_nope, v, k_rope, cos, sin):
    bsz, seq, _ = x_n.shape
    q = (rms_norm(x_n @ w_dq, q_norm) @ w_uq).reshape(bsz, seq, N_HEADS, QK_NOPE_DIM + QK_ROPE_DIM)
    q_nope = q[..., :QK_NOPE_DIM]
    q_rope = apply_rope(q[..., QK_NOPE_DIM:], cos[:, None, :], sin[:, None, :])
    n_blk = seq // Q_BLOCK

    def to_blocks(t):
        return jnp.moveaxis(t.reshape(bsz, n_blk, Q_BLOCK, *t.shape[2:]), 1, 0)

    k_pos = jnp.arange(seq)
    scale = (QK_NOPE_DIM + QK_ROPE_DIM) ** -0.5

    def attend_block(args):
        qn, qr, blk = args
        s = (jnp.einsum('bqhd,bkhd->bhqk', qn, k_nope)
             + jnp.einsum('bqhr,bkr->bhqk', qr, k_rope)).astype(jnp.float32) * scale
        q_pos = blk * Q_BLOCK + jnp.arange(Q_BLOCK)
        s = jnp.where(k_pos[None, :] <= q_pos[:, None], s, -jnp.inf)
        p = jax.nn.softmax(s, axis=-1).astype(v.dtype)
        return jnp.einsum('bhqk,bkhd->bqhd', p, v)

    o = lax.map(attend_block, (to_blocks(q_nope), to_blocks(q_rope), jnp.arange(n_blk)))
    o = jnp.moveaxis(o, 0, 1).reshape(bsz, seq, N_HEADS * V_HEAD_DIM)
    return o @ w_o

def first_inputs(seed: int = 0) -> dict:
    key = jax.random.key(seed)
    ks = jax.random.split(key, 24)
    f32 = jnp.float32

    def w(k, shape, fan_in):
        return jax.random.normal(k, shape, f32) * (fan_in ** -0.5)

    def gain(k, shape):
        return 1.0 + 0.02 * jax.random.normal(k, shape, f32)

    return {
        "x": jax.random.normal(ks[0], (BATCH, SEQ, D_MODEL), f32),
        "a_mix_norm": gain(ks[1], (N_A_LAYERS, D_MODEL)),
        "a_w_in": w(ks[2], (N_A_LAYERS, D_MODEL, 3 * D_MODEL), D_MODEL),
        "a_conv": w(ks[3], (N_A_LAYERS, CONV_WIDTH, D_MODEL), CONV_WIDTH),
        "a_w_out": w(ks[4], (N_A_LAYERS, D_MODEL, D_MODEL), D_MODEL),
        "b_mix_norm": gain(ks[5], (N_B_LAYERS, D_MODEL)),
        "b_w_dq": w(ks[6], (N_B_LAYERS, D_MODEL, Q_LORA_RANK), D_MODEL),
        "b_q_norm": gain(ks[7], (N_B_LAYERS, Q_LORA_RANK)),
        "b_w_uq": w(ks[8], (N_B_LAYERS, Q_LORA_RANK, N_HEADS * (QK_NOPE_DIM + QK_ROPE_DIM)), Q_LORA_RANK),
        "b_w_o": w(ks[9], (N_B_LAYERS, N_HEADS * V_HEAD_DIM, D_MODEL), N_HEADS * V_HEAD_DIM),
        "kv_in_norm": gain(ks[10], (D_MODEL,)),
        "w_dkv": w(ks[11], (D_MODEL, KV_LORA_RANK + QK_ROPE_DIM), D_MODEL),
        "kv_norm": gain(ks[12], (KV_LORA_RANK,)),
        "w_ukv": w(ks[13], (KV_LORA_RANK, N_HEADS * (QK_NOPE_DIM + V_HEAD_DIM)), KV_LORA_RANK),
        "ffn_norm": gain(ks[14], (DEPTH, D_MODEL)),
        "ffn_w_up": w(ks[15], (DEPTH, D_MODEL, 2 * D_FF), D_MODEL),
        "ffn_conv": w(ks[16], (DEPTH, CONV_WIDTH, 2 * D_FF), CONV_WIDTH),
        "ffn_w_down": w(ks[17], (DEPTH, D_FF, D_MODEL), D_FF),
        "final_norm": gain(ks[18], (D_MODEL,)),
    }

def first_block(x, a_mix_norm, a_w_in, a_conv, a_w_out, b_mix_norm, b_w_dq, b_q_norm, b_w_uq, b_w_o,
              kv_in_norm, w_dkv, kv_norm, w_ukv, ffn_norm, ffn_w_up, ffn_conv, ffn_w_down, final_norm):
    cos, sin = rope_tables(x.shape[1], x.dtype)
    h = x
    shared = None
    for layer in range(DEPTH):
        if layer < N_A_LAYERS:
            h = h + short_conv_mixer(rms_norm(h, a_mix_norm[layer]), a_w_in[layer],
                                     a_conv[layer], a_w_out[layer])
        else:
            j = layer - N_A_LAYERS
            k_nope, v, k_rope = shared
            h = h + mla_attention(rms_norm(h, b_mix_norm[j]), b_w_dq[j], b_q_norm[j], b_w_uq[j],
                                  b_w_o[j], k_nope, v, k_rope, cos, sin)
        h = h + conv_ffn(rms_norm(h, ffn_norm[layer]), ffn_w_up[layer], ffn_conv[layer], ffn_w_down[layer])
        if layer == N_A_LAYERS - 1:
            shared = shared_latent_kv(h, kv_in_norm, w_dkv, kv_norm, w_ukv, cos, sin)
    return rms_norm(h, final_norm)


DEPTH_2 = 1

HEAD_DIM = 64
A_GROUPS = 4
A_WIDTH = A_GROUPS * HEAD_DIM
CHUNK = 128
B_HEADS = 6
B_WIDTH = B_HEADS * HEAD_DIM
DIL_PAIRS = ((128, 1), (512, 4), (2048, 16))
C_HEADS_PER_GROUP = 2
C_GROUPS = len(DIL_PAIRS)
C_HEADS = C_GROUPS * C_HEADS_PER_GROUP
C_WIDTH = C_HEADS * HEAD_DIM
C_DILATIONS = tuple(d for (w, d) in DIL_PAIRS for _ in range(C_HEADS_PER_GROUP))
N_OFFSETS = DIL_PAIRS[0][0] // DIL_PAIRS[0][1] + 1
MIX_WIDTH = A_WIDTH + B_WIDTH + C_WIDTH
IN_WIDTH = 2 * A_WIDTH + 3 * B_WIDTH + 3 * C_WIDTH
EPS = 1e-6
N_MOD = 6


def _rmsnorm(x, g):
    x32 = x.astype(jnp.float32)
    y = x32 * lax.rsqrt(jnp.mean(x32 * x32, axis=-1, keepdims=True) + EPS)
    return (y * g.astype(jnp.float32)).astype(x.dtype)

def _rope_tables(positions):
    inv_freq = ROPE_THETA ** (-jnp.arange(0, HEAD_DIM, 2, dtype=jnp.float32) / HEAD_DIM)
    ang = positions.astype(jnp.float32)[..., None] * inv_freq
    return jnp.cos(ang)[:, :, None, :], jnp.sin(ang)[:, :, None, :]

def _rope(x, cos, sin):
    x32 = x.astype(jnp.float32)
    x1, x2 = jnp.split(x32, 2, axis=-1)
    return jnp.concatenate([x1 * cos - x2 * sin, x2 * cos + x1 * sin], axis=-1).astype(x.dtype)

def _spatial_gating(u, v, g_sgu, w_sp, b_sp):
    bsz, seq, _ = u.shape
    n_chunks = seq // CHUNK
    u = jax.nn.gelu(u)
    v = jax.nn.gelu(v).reshape(bsz, n_chunks, CHUNK, A_GROUPS, HEAD_DIM)
    v = _rmsnorm(v, g_sgu.reshape(A_GROUPS, HEAD_DIM))
    causal = jnp.tril(jnp.ones((CHUNK, CHUNK), dtype=bool))
    w_causal = jnp.where(causal[None], w_sp, 0.0).astype(v.dtype)
    mixed = jnp.einsum('gts,bnsgc->bntgc', w_causal, v) + b_sp.T[:, :, None].astype(v.dtype)
    return u * mixed.reshape(bsz, seq, A_WIDTH)

def _stick_breaking(q, k, v):
    bsz, seq, n_heads, dh = q.shape
    n_blocks = seq // Q_BLOCK
    scale = dh ** -0.5
    k_pos = jnp.arange(seq)
    q_blocks = q.reshape(bsz, n_blocks, Q_BLOCK, n_heads, dh).transpose(1, 0, 2, 3, 4)

    def one_block(args):
        q_blk, blk = args
        q_pos = blk * Q_BLOCK + jnp.arange(Q_BLOCK)
        before = (k_pos[None, :] < q_pos[:, None])[None, None]
        z = jnp.einsum('bqhd,bkhd->bhqk', q_blk, k).astype(jnp.float32) * scale
        log_beta = jax.nn.log_sigmoid(z)
        log_stay = jnp.where(before, jax.nn.log_sigmoid(-z), 0.0)
        tail = lax.cumsum(log_stay, axis=3, reverse=True) - log_stay
        weight = jnp.where(before, jnp.exp(log_beta + tail), 0.0)
        return jnp.einsum('bhqk,bkhd->bqhd', weight.astype(v.dtype), v)

    out = lax.map(one_block, (q_blocks, jnp.arange(n_blocks)))
    return out.transpose(1, 0, 2, 3, 4).reshape(bsz, seq, n_heads * dh)

def _dilated_window(q, k, v):
    bsz, seq, n_heads, dh = q.shape
    n_blocks = seq // Q_BLOCK
    scale = dh ** -0.5
    dil = jnp.array(C_DILATIONS, dtype=jnp.int32)
    offsets = jnp.arange(N_OFFSETS, dtype=jnp.int32)
    head_idx = jnp.arange(n_heads)[None, None, :]
    q_blocks = q.reshape(bsz, n_blocks, Q_BLOCK, n_heads, dh).transpose(1, 0, 2, 3, 4)

    def one_block(args):
        q_blk, blk = args
        q_pos = blk * Q_BLOCK + jnp.arange(Q_BLOCK, dtype=jnp.int32)
        idx = q_pos[:, None, None] - offsets[None, :, None] * dil[None, None, :]
        valid = idx >= 0
        idx = jnp.maximum(idx, 0)
        k_g = k[:, idx, head_idx, :]
        v_g = v[:, idx, head_idx, :]
        z = jnp.einsum('bqhd,bqmhd->bqhm', q_blk, k_g).astype(jnp.float32) * scale
        z = jnp.where(valid.transpose(0, 2, 1)[None], z, -jnp.inf)
        z_max = jnp.max(z, axis=-1, keepdims=True)
        p = jnp.exp(z - z_max)
        denom = jnp.sum(p, axis=-1)
        o = jnp.einsum('bqhm,bqmhd->bqhd', p.astype(v.dtype), v_g) / denom[..., None]
        return o.astype(q.dtype), z_max[..., 0] + jnp.log(denom)

    o, lse = lax.map(one_block, (q_blocks, jnp.arange(n_blocks)))
    o = o.transpose(1, 0, 2, 3, 4).reshape(bsz, seq, C_GROUPS, C_HEADS_PER_GROUP, dh)
    lse = lse.transpose(1, 0, 2, 3).reshape(bsz, seq, C_GROUPS, C_HEADS_PER_GROUP)
    alpha = jax.nn.softmax(lse, axis=2)
    return (o * alpha[..., None].astype(o.dtype)).reshape(bsz, seq, n_heads * dh)

def _causal_dwconv(h, w, b):
    seq = h.shape[1]
    hp = jnp.pad(h, ((0, 0), (CONV_WIDTH - 1, 0), (0, 0)))
    out = b.astype(h.dtype)
    for i in range(CONV_WIDTH):
        out = out + w[i].astype(h.dtype) * hp[:, i:i + seq]
    return out

def second_inputs(seed: int = 0) -> dict:
    key = jax.random.key(seed)
    ks = jax.random.split(key, 17)
    f32 = jnp.float32

    def nrm(k, shape, s):
        return jax.random.normal(k, shape, f32) * s

    x = nrm(ks[0], (BATCH, SEQ, D_MODEL), 1.0)
    c = nrm(ks[1], (BATCH, D_MODEL), 1.0)
    offset = jax.random.randint(ks[2], (BATCH, 1), 0, 1024, dtype=jnp.int32)
    positions = jnp.arange(SEQ, dtype=jnp.int32)[None, :] + offset
    w_ada = nrm(ks[3], (DEPTH_2, D_MODEL, N_MOD * D_MODEL), 0.2 * D_MODEL ** -0.5)
    b_ada = nrm(ks[4], (DEPTH_2, N_MOD * D_MODEL), 0.02)
    g_mix = 1.0 + nrm(ks[5], (DEPTH_2, D_MODEL), 0.05)
    w_in = nrm(ks[6], (DEPTH_2, D_MODEL, IN_WIDTH), D_MODEL ** -0.5)
    g_sgu = 1.0 + nrm(ks[7], (DEPTH_2, A_WIDTH), 0.05)
    w_sp = nrm(ks[8], (DEPTH_2, A_GROUPS, CHUNK, CHUNK), CHUNK ** -0.5)
    b_sp = 1.0 + nrm(ks[9], (DEPTH_2, A_GROUPS, CHUNK), 0.1)
    w_out = nrm(ks[10], (DEPTH_2, MIX_WIDTH, D_MODEL), MIX_WIDTH ** -0.5)
    g_ffn = 1.0 + nrm(ks[11], (DEPTH_2, D_MODEL), 0.05)
    w_up = nrm(ks[12], (DEPTH_2, D_MODEL, 2 * D_FF), D_MODEL ** -0.5)
    conv_w = nrm(ks[13], (DEPTH_2, CONV_WIDTH, 2 * D_FF), CONV_WIDTH ** -0.5)
    conv_b = nrm(ks[14], (DEPTH_2, 2 * D_FF), 0.02)
    w_down = nrm(ks[15], (DEPTH_2, D_FF, D_MODEL), D_FF ** -0.5)
    g_final = 1.0 + nrm(ks[16], (D_MODEL,), 0.05)
    return {'x': x, 'c': c, 'positions': positions, 'w_ada': w_ada, 'b_ada': b_ada,
            'g_mix': g_mix, 'w_in': w_in, 'g_sgu': g_sgu, 'w_sp': w_sp, 'b_sp': b_sp,
            'w_out': w_out, 'g_ffn': g_ffn, 'w_up': w_up, 'conv_w': conv_w,
            'conv_b': conv_b, 'w_down': w_down, 'g_final': g_final}

def second_block(x, c, positions, w_ada, b_ada, g_mix, w_in, g_sgu, w_sp, b_sp, w_out,
              g_ffn, w_up, conv_w, conv_b, w_down, g_final):
    bsz, seq, _ = x.shape
    cos, sin = _rope_tables(positions)
    splits = np.cumsum([A_WIDTH, A_WIDTH, B_WIDTH, B_WIDTH, B_WIDTH, C_WIDTH, C_WIDTH]).tolist()
    c_act = jax.nn.silu(c)
    for l in range(DEPTH_2):
        mod = (c_act @ w_ada[l] + b_ada[l])[:, None, :]
        shift1, scale1, gate1, shift2, scale2, gate2 = jnp.split(mod, N_MOD, axis=-1)
        h = _rmsnorm(x, g_mix[l]) * (1.0 + scale1) + shift1
        proj = h @ w_in[l]
        a_u, a_v, b_q, b_k, b_v, c_q, c_k, c_v = jnp.split(proj, splits, axis=-1)
        y_a = _spatial_gating(a_u, a_v, g_sgu[l], w_sp[l], b_sp[l])
        y_b = _stick_breaking(b_q.reshape(bsz, seq, B_HEADS, HEAD_DIM),
                              b_k.reshape(bsz, seq, B_HEADS, HEAD_DIM),
                              b_v.reshape(bsz, seq, B_HEADS, HEAD_DIM))
        y_c = _dilated_window(_rope(c_q.reshape(bsz, seq, C_HEADS, HEAD_DIM), cos, sin),
                              _rope(c_k.reshape(bsz, seq, C_HEADS, HEAD_DIM), cos, sin),
                              c_v.reshape(bsz, seq, C_HEADS, HEAD_DIM))
        y = jnp.concatenate([y_a, y_b, y_c], axis=-1) @ w_out[l]
        x = x + (1.0 + gate1) * y
        h = _rmsnorm(x, g_ffn[l]) * (1.0 + scale2) + shift2
        up = _causal_dwconv(h @ w_up[l], conv_w[l], conv_b[l])
        gate, val = jnp.split(up, 2, axis=-1)
        x = x + (1.0 + gate2) * ((jax.nn.silu(gate) * val) @ w_down[l])
    return _rmsnorm(x, g_final)


def setup_inputs(seed=0):
    out = dict(first_inputs(seed))
    for name, value in second_inputs(seed + 1).items():
        if name != "x":
            out[name + "_2"] = value
    return out


def reference(
    x, a_mix_norm, a_w_in, a_conv, a_w_out, b_mix_norm, b_w_dq, b_q_norm, b_w_uq, b_w_o,
    kv_in_norm, w_dkv, kv_norm, w_ukv, ffn_norm, ffn_w_up, ffn_conv, ffn_w_down, final_norm,
    c_2, positions_2, w_ada_2, b_ada_2, g_mix_2, w_in_2, g_sgu_2, w_sp_2, b_sp_2, w_out_2,
    g_ffn_2, w_up_2, conv_w_2, conv_b_2, w_down_2, g_final_2,
):
    x = first_block(
        x, a_mix_norm, a_w_in, a_conv, a_w_out, b_mix_norm, b_w_dq, b_q_norm, b_w_uq, b_w_o,
        kv_in_norm, w_dkv, kv_norm, w_ukv, ffn_norm, ffn_w_up, ffn_conv, ffn_w_down, final_norm,
    )
    return second_block(
        x, c_2, positions_2, w_ada_2, b_ada_2, g_mix_2, w_in_2, g_sgu_2, w_sp_2, b_sp_2,
        w_out_2, g_ffn_2, w_up_2, conv_w_2, conv_b_2, w_down_2, g_final_2,
    )


_drawn_inputs = setup_inputs


def setup_inputs(seed=0):
    import zlib

    import numpy as np

    out = dict(_drawn_inputs(seed))
    spreads = {}
    factors = {'b_mix_norm': 8.0,
     'b_q_norm': 8.0,
     'kv_in_norm': 8.0,
     'kv_norm': 8.0,
     'ffn_norm': 2.939,
     'g_sgu_2': 5.374,
     'conv_b_2': 4.281,
     'b_sp_2': 2.811}
    for name, (base, spread) in spreads.items():
        noise = np.random.default_rng([zlib.crc32(name.encode()), seed]).standard_normal(out[name].shape)
        drawn = base * np.exp(spread * noise) if base else spread * noise
        out[name] = __import__('jax').numpy.asarray(drawn.astype(out[name].dtype))
    for name, factor in factors.items():
        out[name] = (out[name] * factor).astype(out[name].dtype)
    return out
```

```python
from contextlib import ExitStack

import numpy as np
import concourse.bass as bass
from concourse import mybir

F32 = mybir.dt.float32
F32R = mybir.dt.float32r
I32 = mybir.dt.int32
BF16 = mybir.dt.bfloat16
ACT = mybir.ActivationFunctionType
ALU = mybir.AluOpType
AX_X = mybir.AxisListType.X

P = 128
D = 1024
KD = D // P
S = 512
D_FF = 2816
FF = D_FF // P
HEADS = 8
NOPE, ROPE, VD = 128, 64, 128
Q_LORA, KV_LORA = 512, 256
KQ, KKV = Q_LORA // P, KV_LORA // P
THETA = 10000.0
EPS = 1e-6
MLA_SCALE = float((NOPE + ROPE) ** -0.5)
HD = 64
A_W, B_W, C_W = 256, 384, 384
GROUPS = A_W // HD
B_HEADS = B_W // HD
QK_SCALE = HD ** -0.5
N_OFFSETS = 129
NEG = -1.0e30
BLK = 8
TILE = BLK * P
RAW = 4
SPL = 2
CONV = 3


def vec_layout():
    at, out = 0, {}
    for name, n in (("a_mix", KD), ("a_conv", CONV * KD), ("b_mix", KD), ("q_norm", KQ), ("kv_in", KD),
                    ("kv_norm", KKV), ("ffn_norm0", KD), ("ffn_norm1", KD), ("ffn_conv0", CONV * 2 * FF),
                    ("ffn_conv1", CONV * 2 * FF), ("final", KD), ("b_ada", 6 * KD), ("g_mix", KD),
                    ("g_ffn", KD), ("ffn_conv2", CONV * 2 * FF), ("conv_b", 2 * FF), ("g_final", KD),
                    ("b_sp", GROUPS), ("inv_freq", 1), ("sin_sign", 1)):
        out[name] = (at, n)
        at += n
    out["width"] = at
    return out


def const_layout():
    at, out = 0, {}
    for name, n in (("ident", P), ("swap", P), ("ones", P), ("tri", P), ("causal_neg", P), ("strict", P),
                    ("strict_neg", P)):
        out[name] = (at, n)
        at += n
    out["width"] = at
    return out


PHASES = (
    ("A_CH", 16, [1]), ("A_B", 8, [1]), ("A_OUT", 8, [1]),
    ("UP0", 2 * FF, [1]), ("DN0", 24, [0, 0, 1]),
    ("DKV", 3, [1]), ("DQ", 4, [1]), ("UKV", 4, [4]), ("UQ", 6, [2]), ("WO", 8, [1]),
    ("UP1", 2 * FF, [1]), ("DN1", 24, [0, 0, 1]),
    ("IN2", 22, [1]), ("OUT2", 8, [1]), ("UP2", 2 * FF, [1]), ("DN2", 24, [0, 0, 1]),
)


def schedule():
    t0, m0, done_t, done_m, steps = {}, {}, [], [], 0
    for name, tiles, ends in PHASES:
        t0[name], m0[name] = len(done_t), len(done_m)
        for i in range(tiles):
            n = ends[i % len(ends)]
            for _ in range(n):
                steps += 1
                done_m.append(steps)
            steps += n == 0
            done_t.append(steps)
    return t0, m0, done_t, done_m


def build(nc, w_tiles, ada_tiles, c_in, x_in, vec_in, const_in, rope_in, mask1_in, mask2_in, gsgu_in, wsp_in, pos_in, out):
    T0, M0, DONE_T, DONE_M = schedule()
    NT = len(DONE_T)
    V = vec_layout()
    C = const_layout()
    ctx = ExitStack()
    with ctx:
        def sb(name, shape, dt=F32, stack=ctx):
            return stack.enter_context(nc.sbuf_tensor(name, shape, dt))

        def sem(name):
            return ctx.enter_context(nc.semaphore(name))

        X = sb("X", [P, KD, S])
        XH = sb("XH", [P, KD, S], F32R)
        XL = sb("XL", [P, KD, S], F32R)
        raw = sb("raw", [P, RAW, TILE])
        WH = [sb(f"WH{i}", [P, TILE], F32R) for i in range(SPL)]
        WL = [sb(f"WL{i}", [P, TILE], F32R) for i in range(SPL)]
        vec = sb("vec", [P, V["width"]])
        cst = sb("cst", [P, C["width"]])
        cos_t = sb("cos_t", [P, S])
        sin_t = sb("sin_t", [P, S])
        rb = sb("rb", [P, S])
        rbl = sb("rbl", [P, S])
        acc = sb("acc", [P, S])
        SQ = sb("SQ", [P, 2, S])
        AT = sb("AT", [P, 2, S])
        RA = sb("RA", [P, S])
        RB = sb("RB", [P, S])
        mask16 = sb("mask16", [P, 2, P], BF16)
        mod = sb("mod", [P, 6 * KD])
        gm = sb("gm", [P, 4, KD])
        epsc = sb("epsc", [P, 1])
        gsgu = sb("gsgu", [P, A_W])

        st = ExitStack()
        CV = sb("CV", [P, KD, S], F32, st)
        MH = sb("MH", [P, KD, S], F32R, st)
        ML = sb("ML", [P, KD, S], F32R, st)
        ada = sb("ada", [P, 2, D], F32, st)
        crow = sb("crow", [P, D], F32, st)
        st.close()
        st = ExitStack()
        HH = sb("HH", [P, FF, S], F32R, st)
        HL = sb("HL", [P, FF, S], F32R, st)
        TG = sb("TG", [P, S + 2], F32, st)
        TU = sb("TU", [P, S + 2], F32, st)
        CG = sb("CG", [P, S], F32, st)
        CU = sb("CU", [P, S], F32, st)
        st.close()
        st = ExitStack()
        QXH = sb("QXH", [P, KD, S], F32R, st)
        QXL = sb("QXL", [P, KD, S], F32R, st)
        st.close()
        st = ExitStack()
        KN = sb("KN", [P, HEADS, S], F32, st)
        VT = sb("VT", [P, HEADS, S], F32, st)
        KR = sb("KR", [P, S], F32, st)
        QN = sb("QN", [P, HEADS, S], F32, st)
        QR = sb("QR", [P, HEADS // 2, S], F32, st)
        stat = sb("stat", [P, 4, 4 * HEADS], F32, st)
        st2 = ExitStack()
        CL = sb("CL", [P, KKV, S], F32, st2)
        CLH = sb("CLH", [P, KKV, S], F32R, st2)
        CLL = sb("CLL", [P, KKV, S], F32R, st2)
        QL = sb("QL", [P, KQ, S], F32, st2)
        st2.close()
        OH = sb("OH", [P, HEADS, S], F32R, st)
        OL = sb("OL", [P, HEADS, S], F32R, st)
        st.close()
        st = ExitStack()
        FT = sb("FT", [P, 12, S], F32, st)
        BV = sb("BV", [P, 4, B_W], F32, st)
        CV0 = sb("CV0", [P, 4, P], F32, st)
        CV12 = sb("CV12", [P, 4, 2 * P], F32, st)
        WS = sb("WS", [P, GROUPS, P], F32, st)
        MK1 = sb("MK1", [P, 4, S], F32, st)
        MK2 = sb("MK2", [P, 2 * P], F32, st)
        posi = sb("posi", [P, S], I32, st)
        st2 = ExitStack()
        U = sb("U", [P, 4, A_W], F32, st2)
        VV = sb("VV", [P, 4, A_W], F32, st2)
        VN = sb("VN", [P, 4, A_W], F32, st2)
        YA = sb("YA", [P, 4, A_W], F32, st2)
        vst = sb("vst", [P, 3, 4 * GROUPS], F32, st2)
        st2.close()
        st2 = ExitStack()
        ZB = [sb(f"ZB{i}", [P, S], F32, st2) for i in range(2)]
        EB = [sb(f"EB{i}", [P, S], F32, st2) for i in range(2)]
        SP = sb("SP", [P, 4, S], F32, st2)
        WT = [sb(f"WT{i}", [P, S], F32, st2) for i in range(2)]
        st2.close()
        st2 = ExitStack()
        ZC = [sb(f"ZC{i}", [P, S + 2 * P], F32, st2) for i in range(2)]
        PC = [sb(f"PC{i}", [P, S + 2 * P], F32, st2) for i in range(2)]
        PCT = [sb(f"PCT{i}", [P, S + 2 * P], F32, st2) for i in range(2)]
        cstat = sb("cstat", [P, 4, 8], F32, st2)
        st2.close()
        st.close()

        PB = [SQ[:, 0, :], SQ[:, 1, :], RA[:, :], RB[:, :]]
        SB = (4, 5, 2, 3)

        ps = [ctx.enter_context(nc.psum_tensor(f"ps{i}", [P, S], F32)) for i in range(8)]

        s_in = {n: sem(f"s_in_{n}") for n in ("x0", "x1", "x2", "x3", "c", "vec", "const", "rope", "gsgu", "wsp", "mask", "pos")}
        s_raw = [sem(f"s_raw{i}") for i in range(RAW)]
        s_hi = sem("s_hi")
        s_lo = sem("s_lo")
        s_pe = sem("s_pe")
        s_ev = sem("s_ev")
        s_ada_in = [sem(f"s_ada_in{i}") for i in range(2)]
        s_ada = sem("s_ada")
        s_cact = sem("s_cact")
        s_set = sem("s_set")
        s_x = sem("s_x")
        s_sq = sem("s_sq")
        s_acc = sem("s_acc")
        s_sq2 = sem("s_sq2")
        s_acc2 = sem("s_acc2")
        s_ms = sem("s_ms")
        s_ssum = sem("s_ssum")
        s_root = sem("s_root")
        s_rb = sem("s_rb")
        s_xh = sem("s_xh")
        s_xl = sem("s_xl")
        s_nb = sem("s_nb")
        s_dve = sem("s_dve")
        s_act = sem("s_act")
        s_gc = sem("s_gc")
        s_sg = sem("s_sg")
        s_h = sem("s_h")
        s_hh = sem("s_hh")
        s_hl = sem("s_hl")
        s_y = sem("s_y")
        s_yh = sem("s_yh")
        s_yl = sem("s_yl")
        s_aux = sem("s_aux")
        s_auxev = sem("s_auxev")
        s_lh = sem("s_lh")
        s_ll = sem("s_ll")
        s_qk = sem("s_qk")
        s_m16 = sem("s_m16")
        s_s = sem("s_s")
        s_mx = sem("s_mx")
        s_p = sem("s_p")
        s_rs = sem("s_rs")
        s_pn = sem("s_pn")
        s_pt = sem("s_pt")
        s_ptc = sem("s_ptc")
        s_pv = sem("s_pv")
        s_oh = sem("s_oh")
        s_ol = sem("s_ol")
        s_ws = sem("s_ws")
        s_arg = sem("s_arg")
        s_trig = sem("s_trig")
        s_gelu = sem("s_gelu")
        s_vs = sem("s_vs")
        s_vr = sem("s_vr")
        s_vn = sem("s_vn")
        s_mixed = sem("s_mixed")
        s_ya = sem("s_ya")
        s_y2h = sem("s_y2h")
        s_y2l = sem("s_y2l")
        s_z = sem("s_z")
        s_zb = sem("s_zb")
        s_ln = sem("s_ln")
        s_sp = sem("s_sp")
        s_r = sem("s_r")
        s_wa = sem("s_wa")
        s_w = sem("s_w")
        s_bo = sem("s_bo")
        s_cz = sem("s_cz")
        s_cm = sem("s_cm")
        s_cp = sem("s_cp")
        s_cn = sem("s_cn")
        s_ct = sem("s_ct")
        s_cc = sem("s_cc")
        s_co = sem("s_co")
        s_fin = sem("s_fin")
        s_out = sem("s_out")

        block = ctx.enter_context(nc.Block())

        def vcol(name, i):
            first = V[name][0]
            return vec[:, first + i:first + i + 1] if isinstance(i, int) else vec[:, bass.ds(i + first, 1)]

        def cc(name):
            return cst[:, C[name][0]:C[name][0] + C[name][1]]

        def at(t, i):
            return t[:, i, :] if isinstance(i, int) else t[:, bass.ds(i, 1), :].rearrange("p a b -> p (a b)")

        def f32(ap):
            return ap.bitcast(F32)

        ADA_AT = ((0, 1), (2,), (3, 4), (5,))
        NORM_CHUNKS = [KD, KD, KD, KKV, KQ, KD, KD, KD, KD]
        N_A, N_F0, N_KV, N_LK, N_LQ, N_F1, N_FIN, N_F2, N_END = range(9)
        SQ0 = [sum(NORM_CHUNKS[:i]) for i in range(10)]
        E_A, E_F0, E_KV, E_Q, E_F1, E_M2, E_F2 = range(7)
        NB_KV, NB_Q, NB_M2, NB_F2 = 0, KKV, KKV + KQ, KKV + KQ + KD
        AUX_KR, AUX_V, AUX_QR = 0, 1, 1 + HEADS
        AUX_2 = AUX_QR + HEADS // 2
        N_TOK = 2 * (A_W // P) + C_W // P + B_W // P
        AUX_YA = AUX_2 + N_TOK + 2 * (C_W // P)
        BLOCKS_A = 4 * HEADS
        BLOCKS_B = 4 * B_HEADS

        class Chain:

            def __init__(self, eng, s):
                self.eng, self.s, self.n, self.i, self.per = eng, s, 0, None, 0

            def enter(self, i, per):
                self.i, self.per, self.base = i, per, self.n

            def leave(self):
                assert self.n - self.base == self.per, (self.n - self.base, self.per)
                self.n, self.i = self.base, None

            def step(self, ins):
                ins.then_inc(self.s, 1)
                self.n += 1

            def wait(self):
                self.eng.wait_ge(self.s, self.n if self.i is None else self.i * self.per + self.n)

            def link(self, ins):
                self.step(ins)
                self.wait()

        def repeat(eng, times, body, chain=None, per=0, peel=0):
            def one(i):
                if chain:
                    chain.enter(i, per)
                body(i)
                if chain:
                    chain.leave()
            for i in range(peel):
                one(i)
            if times > peel:
                with eng.Fori(peel, times) as i:
                    one(i)
            if chain:
                chain.n += times * per

        @block.sync
        def _(sp):
            def load(t, slot, first=False):
                if not first:
                    sp.wait_ge(s_lo, t - (RAW - 1))
                src = w_tiles[t] if isinstance(t, int) else \
                    w_tiles[bass.ds(t, 1), :, :].rearrange("a p n -> p (a n)")
                sp.dma_start(raw[:, slot, :], src).then_inc(s_raw[slot], 16)

            def load_ada(a, slot, first=False):
                if not first:
                    sp.wait_ge(s_ada, a - 1)
                src = ada_tiles[a] if isinstance(a, int) else \
                    ada_tiles[bass.ds(a, 1), :, :].rearrange("a p n -> p (a n)")
                sp.dma_start(ada[:, slot, :], src).then_inc(s_ada_in[slot], 16)

            for k in range(RAW):
                load(k, k, True)

            def with_ada(i):
                for k in range(RAW):
                    load(i * RAW + (RAW + k), k)
                    for q in ADA_AT[k]:
                        load_ada(i * 6 + q, q % 2, isinstance(i, int) and q < 2)
            n_ada = 6 * KD // 6
            repeat(sp, n_ada, with_ada, peel=1)

            def four(i):
                for k in range(RAW):
                    load(i * RAW + ((n_ada + 1) * RAW + k), k)
            repeat(sp, NT // RAW - n_ada - 1, four)
            for t in range(NT // RAW * RAW, NT):
                load(t, t % RAW)
            for m in range(KD):
                sp.wait_ge(s_fin, m + 1)
                sp.dma_start(out[:, m, :], X[:, m, :]).then_inc(s_out, 16)
            sp.wait_ge(s_out, 16 * KD)

        @block.gpsimd
        def _(pool):
            def lo(t, k):
                pool.wait_ge(s_hi, t + 1)
                nc.gpsimd.tensor_tensor(WL[k % SPL][:, :], raw[:, k, :], f32(WH[k % SPL][:, :]),
                                        ALU.subtract).then_inc(s_lo, 1)

            cut = (T0["IN2"] + RAW) // RAW

            def before(i):
                for k in range(RAW):
                    lo(i * RAW + k, k)
            repeat(pool, cut, before)
            pool.wait_ge(s_in["wsp"], 16)
            nc.gpsimd.affine_select(out=WS[:, :, :], in_=WS[:, :, :], compare_op=ALU.is_ge, fill=0.0, base=0,
                                    pattern=[[0, GROUPS], [1, P]], channel_multiplier=-1).then_inc(s_ws, 1)

            def after(i):
                for k in range(RAW):
                    lo(i * RAW + (cut * RAW + k), k)
            repeat(pool, NT // RAW - cut, after)
            for t in range(NT // RAW * RAW, NT):
                lo(t, t % RAW)

        @block.scalar
        def _(act):
            ch = Chain(act, s_act)
            act.dma_start(vec[:, :], vec_in).then_inc(s_in["vec"], 16)
            for m in range(4):
                act.dma_start(X[:, 2 * m:2 * m + 2, :], x_in[:, 2 * m:2 * m + 2, :]).then_inc(s_in[f"x{m}"], 16)
            act.dma_start(crow[:, :], c_in).then_inc(s_in["c"], 16)
            act.dma_start(cst[:, :], const_in).then_inc(s_in["const"], 16)
            act.dma_start(cos_t[:, :], rope_in[0]).then_inc(s_in["rope"], 16)
            act.dma_start(sin_t[:, :], rope_in[1]).then_inc(s_in["rope"], 16)
            act.dma_start(gsgu[:, :], gsgu_in).then_inc(s_in["gsgu"], 16)

            def hi(t, i=0, per=0):
                slot = t % RAW
                act.wait_ge(s_raw[slot], i * (16 * per // RAW) + 16 * (t // RAW + 1))
                nc.scalar.activation(WH[t % SPL][:, :], raw[:, slot, :], ACT.Copy).then_inc(s_hi, 1)

            def ahead(t, i=0, per=0):
                if not isinstance(i, int) or t + i * per + SPL < NT:
                    act.wait_ge(s_pe, i * per + DONE_T[t])
                    hi(t + SPL, i, per)

            def apart():
                act.wait_ge(s_set, 1)

            def square(n, m, k, src):
                act.wait_ge(s_acc, m + (SQ0[n] - 1))
                nc.scalar.activation(SQ[:, k % 2, :], src, ACT.Square).then_inc(s_sq, 1)

            def root(n, dim, dst):
                act.wait_ge(s_ssum, n + 1 + (n > N_FIN))
                nc.scalar.activation(dst[:, :], ps[4][:, :], ACT.Sqrt, bias=epsc[:, :], scale=1.0 / dim)\
                    .then_inc(s_root, 1)

            def residual(phase, tiles_per_m, gname, n, second=False):
                per = 4 * tiles_per_m

                def body(i):
                    for k in range(4):
                        for j in range(tiles_per_m):
                            ahead(T0[phase] + k * tiles_per_m + j, i, per)
                        m = i * 4 + k
                        act.wait_ge(s_acc, m + (SQ0[n] - 1))
                        act.wait_ge(s_ev, m + (M0[phase] + 1))
                        apart()
                        if gname:
                            nc.scalar.activation(at(XH, m), at(X, m), ACT.Copy, scale=vcol(gname, m))\
                                .then_inc(s_xh, 1)
                        nc.scalar.activation(SQ[:, k % 2, :], at(X, m), ACT.Square).then_inc(s_sq, 1)
                        if second:
                            act.wait_ge(s_acc2, m + 1)
                            apart()
                            nc.scalar.activation(AT[:, k % 2, :], at(X, m), ACT.Square, scale=vcol("final", m))\
                                .then_inc(s_sq2, 1)
                repeat(act, KD // 4, body, peel=KD // 4 if phase == PHASES[-1][0] else 0)

            def up(f, phase, bias):
                def body(i):
                    for j in range(2):
                        t, jj = T0[phase] + 2 * j, i * 2 + j
                        ahead(t, i, 4)
                        act.wait_ge(s_gc, jj + (FF * f + 1))
                        apart()
                        nc.scalar.activation(CG[:, :], CG[:, :], ACT.Silu, bias=vcol("conv_b", jj) if bias else 0.0)\
                            .then_inc(s_sg, 1)
                        ahead(t + 1, i, 4)
                        act.wait_ge(s_h, jj + (FF * f + 1))
                        apart()
                        nc.scalar.activation(at(HH, jj), CU[:, :], ACT.Copy).then_inc(s_hh, 1)
                repeat(act, FF // 2, body)

            act.wait_ge(s_in["vec"], 16)
            for m in range(KD):
                if m % 2 == 0:
                    act.wait_ge(s_in[f"x{m // 2}"], 16)
                nc.scalar.activation(XH[:, m, :], X[:, m, :], ACT.Copy, scale=vcol("a_mix", m)).then_inc(s_xh, 1)
                if m % 2 == 1 and m < 4:
                    hi(m // 2)
            for m in range(KD):
                if m >= 2:
                    act.wait_ge(s_acc, m - 1)
                nc.scalar.activation(SQ[:, m % 2, :], X[:, m, :], ACT.Square).then_inc(s_sq, 1)
            act.wait_ge(s_in["c"], 16)
            nc.scalar.activation(crow[:, :], crow[:, :], ACT.Silu).then_inc(s_cact, 1)
            act.wait_ge(s_set, 1)
            root(N_A, D, rb)

            def a_ch(i):
                for k in range(4):
                    ahead(T0["A_CH"] + k, i, 4)
            repeat(act, 4, a_ch)

            def a_b(i):
                for k in range(4):
                    ahead(T0["A_B"] + k, i, 4)
                    act.wait_ge(s_y, i * 4 + (k + 1))
                    apart()
                    nc.scalar.activation(at(MH, i * 4 + k), CU[:, :], ACT.Copy).then_inc(s_yh, 1)
            repeat(act, 2, a_b)
            residual("A_OUT", 1, "ffn_norm0", N_F0)

            root(N_F0, D, rb)
            up(0, "UP0", False)
            residual("DN0", 3, "kv_in", N_KV)

            root(N_KV, D, rb)
            for m in range(KD):
                nc.scalar.activation(QXH[:, m, :], X[:, m, :], ACT.Copy, scale=vcol("b_mix", m)).then_inc(s_xh, 1)
            for k in range(3):
                ahead(T0["DKV"] + k)
                if k < KKV:
                    act.wait_ge(s_ev, M0["DKV"] + k + 1)
                    square(N_LK, k, k, CL[:, k, :])
            ahead(T0["DQ"])
            root(N_LK, KV_LORA, rbl)
            for m in range(KKV):
                act.wait_ge(s_nb, NB_KV + m + 1)
                nc.scalar.activation(CLH[:, m, :], CL[:, m, :], ACT.Copy, scale=vcol("kv_norm", m)).then_inc(s_lh, 1)
            for k in range(KQ):
                if k > 0:
                    ahead(T0["DQ"] + k)
                act.wait_ge(s_ev, M0["DQ"] + k + 1)
                square(N_LQ, k, k, QL[:, k, :])
            ahead(T0["UKV"])
            root(N_LQ, Q_LORA, rbl)
            for m in range(KQ):
                act.wait_ge(s_nb, NB_Q + m + 1)
                nc.scalar.activation(XH[:, m, :], QL[:, m, :], ACT.Copy, scale=vcol("q_norm", m)).then_inc(s_lh, 1)
            for k in range(1, 4):
                ahead(T0["UKV"] + k)
            for k in range(6):
                ahead(T0["UQ"] + k)

            def head_hi(h):
                act.wait_ge(s_pv, 4 * h + 4)
                nc.scalar.activation(OH[:, h, :], ps[h % 2][:, :], ACT.Copy).then_inc(s_oh, 1)

            for a in range(BLOCKS_A + 1):
                if a < BLOCKS_A:
                    L = (a % 4 + 1) * P
                    if a >= 4:
                        act.wait_ge(s_pt, a - 3)
                    act.wait_ge(s_mx, a + 1)
                    nc.scalar.activation(PB[a % 4][:, 0:L], ps[SB[a % 4]][:, 0:L], ACT.Exp,
                                         bias=stat[:, 1, a:a + 1], scale=MLA_SCALE,
                                         accum_out=stat[:, 2, a:a + 1]).then_inc(s_p, 1)
                b = a - 1
                if b >= 0:
                    L = (b % 4 + 1) * P
                    act.wait_ge(s_rs, b + 1)
                    nc.scalar.activation(PB[b % 4][:, 0:L], PB[b % 4][:, 0:L], ACT.Copy,
                                         scale=stat[:, 3, b:b + 1]).then_inc(s_pn, 1)
                if a % 4 == 0 and a >= 8:
                    head_hi(a // 4 - 2)
            head_hi(HEADS - 1)
            residual("WO", 1, "ffn_norm1", N_F1)

            root(N_F1, D, rb)
            up(1, "UP1", False)
            residual("DN1", 3, None, N_FIN, second=True)
            act.dma_start(MK1[:, :, :], mask1_in).then_inc(s_in["mask"], 16)
            act.dma_start(MK2[:, :], mask2_in).then_inc(s_in["mask"], 16)
            act.dma_start(WS[:, :, :], wsp_in).then_inc(s_in["wsp"], 16)
            act.dma_start(posi[:, :], pos_in).then_inc(s_in["pos"], 16)
            act.wait_ge(s_ms, 1)
            nc.scalar.activation(rb[:, :], rb[:, :], ACT.Sqrt).then_inc(s_root, 1)
            nc.scalar.activation(acc[:, :], acc[:, :], ACT.Sqrt, bias=epsc[:, :], scale=1.0 / D).then_inc(s_root, 1)

            def modulated(nb0, shift):
                for m in range(KD):
                    act.wait_ge(s_nb, nb0 + m + 1)
                    nc.scalar.activation(XH[:, m, :], AT[:, m % 2, :], ACT.Identity,
                                         bias=mod[:, shift * KD + m:shift * KD + m + 1]).then_inc(s_xh, 1)
            modulated(NB_M2, 0)
            act.wait_ge(s_arg, 1)
            nc.scalar.activation(sin_t[:, :], RA[:, :], ACT.Sin, scale=vcol("sin_sign", 0)).then_inc(s_trig, 1)
            act.wait_ge(s_arg, 2)
            nc.scalar.activation(cos_t[:, :], RB[:, :], ACT.Sin).then_inc(s_trig, 1)
            for k in range(22):
                ahead(T0["IN2"] + k)
                if k == 6:
                    act.wait_ge(s_auxev, AUX_2 + 4)
                    nc.scalar.activation(VV[:, :, :], VV[:, :, :], ACT.Gelu_apprx_tanh).then_inc(s_gelu, 1)
                    nc.scalar.activation(U[:, :, :], U[:, :, :], ACT.Gelu_apprx_tanh).then_inc(s_gelu, 1)
            act.wait_ge(s_vs, 1)
            nc.scalar.activation(vst[:, 1, :], vst[:, 0, :], ACT.Sqrt, bias=epsc[:, :], scale=1.0 / HD)\
                .then_inc(s_vr, 1)
            for c in range(A_W // P):
                act.wait_ge(s_aux, AUX_YA + c + 1)
                nc.scalar.activation(XH[:, c, :], ps[5 + (AUX_YA + c) % 2][:, :], ACT.Copy).then_inc(s_y2h, 1)
            nc.scalar.preload_act_table_set("natural_log_exp_and_others")

            def weight(b):
                N = (b % 4 + 1) * P
                if b >= 2:
                    act.wait_ge(s_bo, b - 1)
                act.wait_ge(s_wa, b + 1)
                nc.scalar.activation(WT[b % 2][:, 0:N], ZB[b % 2][:, 0:N], ACT.Exp).then_inc(s_w, 1)

            def pair_hi(c):
                act.wait_ge(s_bo, 8 * c + 8)
                nc.scalar.activation(XH[:, 2 + c, :], ps[6 + c % 2][:, :], ACT.Copy).then_inc(s_y2h, 1)

            for b in range(BLOCKS_B):
                N = (b % 4 + 1) * P
                act.wait_ge(s_zb, b + 1)
                E = EB[b % 2][:, 0:N]
                ch.link(nc.scalar.activation(E, ZB[b % 2][:, 0:N], ACT.Abs))
                ch.link(nc.scalar.activation(E, E, ACT.Exp, scale=-1.0))
                nc.scalar.activation(E, E, ACT.Ln, bias=1.0).then_inc(s_ln, 1)
                if b >= 1:
                    weight(b - 1)
                if b % 8 == 2 and b > 8:
                    pair_hi(b // 8 - 1)
            weight(BLOCKS_B - 1)
            pair_hi(B_HEADS // 2 - 1)
            def class_hi(r):
                act.wait_ge(s_co, 2 * r + 2)
                nc.scalar.activation(XH[:, 5:8, r::4], ps[6 + r % 2][:, 0:3 * P].rearrange("p (c q) -> p c q", c=3),
                                     ACT.Copy).then_inc(s_y2h, 1)

            for u in range(8):
                if u >= 2:
                    act.wait_ge(s_ct, u - 1)
                act.wait_ge(s_cm, u + 1)
                nc.scalar.activation(PC[u % 2][:, :], ZC[u % 2][:, :], ACT.Exp, bias=cstat[:, 1, u:u + 1],
                                     accum_out=cstat[:, 2, u:u + 1]).then_inc(s_cp, 1)
                if u % 2 == 1 and u > 1:
                    class_hi(u // 2 - 1)
            class_hi(3)
            residual("OUT2", 1, None, N_F2)
            root(N_F2, D, rb)
            modulated(NB_F2, 3)
            up(2, "UP2", True)
            residual("DN2", 3, None, N_END)
            root(N_END, D, rb)

        @block.vector
        def _(dve):
            ch = Chain(dve, s_dve)
            v = nc.vector
            v.memset(epsc[:, :], EPS).then_inc(s_set, 1)

            def zero_pads():
                ch.step(v.memset(TG[:, 0:2], 0.0))
                ch.link(v.memset(TU[:, 0:2], 0.0))

            def add_square(n, m, k):
                dve.wait_ge(s_sq, m + (SQ0[n] + 1))
                if not (n == 0 and isinstance(m, int) and m == 0):
                    dve.wait_ge(s_acc, m + SQ0[n])
                v.tensor_tensor(acc[:, :], acc[:, :], SQ[:, k % 2, :], ALU.add).then_inc(s_acc, 1)

            def inverse(n, dst):
                dve.wait_ge(s_root, n + 1 + (n > N_FIN))
                v.reciprocal(dst[:, :], dst[:, :]).then_inc(s_rb, 1)
                dve.wait_ge(s_rb, n + 1)
                ch.link(v.memset(acc[:, :], 0.0))

            def lo_half(dst_h, dst_l, src, g, done_h, sem_l):
                dve.wait_ge(*done_h)
                v.scalar_tensor_tensor(dst_l, src, g, f32(dst_h), ALU.mult, ALU.subtract).then_inc(sem_l, 1)

            def product(M, i=0, per=0):
                dve.wait_ge(s_pe, i * per + DONE_M[M])

            def residual(phase, tiles_per_m, e, gname, n, gate=None, beside=None, second=False):
                per = 4 * tiles_per_m

                def body(i):
                    for k in range(4):
                        m, M = i * 4 + k, M0[phase] + k
                        product(M, i, per)
                        bank = ps[M % 4][:, :]
                        if gate is None:
                            ins = v.tensor_tensor(at(X, m), bank, at(X, m), ALU.add)
                        else:
                            g = gm[:, gate, m:m + 1] if isinstance(m, int) else \
                                gm[:, gate, :][:, bass.ds(m, 1)]
                            ins = v.scalar_tensor_tensor(at(X, m), bank, g, at(X, m), ALU.mult, ALU.add)
                        ins.then_inc(s_ev, 1)
                        if gname:
                            lo_half(at(XH, m), at(XL, m), at(X, m), vcol(gname, m), (s_xh, m + (KD * e + 1)), s_xl)
                        add_square(n, m, k)
                        if second:
                            dve.wait_ge(s_sq2, m + 1)
                            dve.wait_ge(s_acc2, m + 2)
                            v.tensor_tensor(rbl[:, :], rbl[:, :], AT[:, k % 2, :], ALU.add).then_inc(s_acc2, 1)
                        if beside:
                            beside(i, k)
                repeat(dve, KD // 4, body)

            def conv(dst, src, w, j, chunks, last):
                ch.link(v.tensor_scalar(dst, src[:, 2:S + 2], vcol(w, j + 2 * chunks), None, ALU.mult))
                ch.link(v.scalar_tensor_tensor(dst, src[:, 1:S + 1], vcol(w, j + chunks), dst, ALU.mult, ALU.add))
                last(v.scalar_tensor_tensor(dst, src[:, 0:S], vcol(w, j), dst, ALU.mult, ALU.add))

            def up(f, phase, deferred):
                w = f"ffn_conv{f}"
                zero_pads()

                def body(i):
                    for j in range(2):
                        jj = i * 2 + j
                        for half, (pad, dst) in enumerate(((TG, CG), (TU, CU))):
                            M = M0[phase] + 2 * j + half
                            product(M, i, 4)
                            if deferred:
                                ins = v.tensor_tensor(pad[:, 2:S + 2], ps[M % 4][:, :], rb[:, :], ALU.mult)
                            else:
                                ins = v.tensor_copy(pad[:, 2:S + 2], ps[M % 4][:, :])
                            ins.then_inc(s_ev, 1)
                            dve.wait_ge(s_ev, i * 4 + (M + 1))
                            if half == 0:
                                conv(dst[:, :], pad, w, jj, 2 * FF, lambda ins: ins.then_inc(s_gc, 1))
                            else:
                                conv(dst[:, :], pad, w, jj + FF, 2 * FF, ch.link)
                        dve.wait_ge(s_sg, jj + (FF * f + 1))
                        if deferred:
                            ins = v.tensor_tensor(CU[:, :], CU[:, :], CG[:, :], ALU.mult)
                        else:
                            ins = v.scalar_tensor_tensor(CU[:, :], CU[:, :], vcol("conv_b", jj + FF), CG[:, :],
                                                         ALU.add, ALU.mult)
                        ins.then_inc(s_h, 1)
                        dve.wait_ge(s_hh, jj + (FF * f + 1))
                        v.tensor_tensor(at(HL, jj), CU[:, :], f32(at(HH, jj)), ALU.subtract).then_inc(s_hl, 1)
                repeat(dve, FF // 2, body, ch, 10)

            ch.link(v.memset(acc[:, :], 0.0))
            zero_pads()
            for m in range(KD):
                lo_half(XH[:, m, :], XL[:, m, :], X[:, m, :], vcol("a_mix", m), (s_xh, m + 1), s_xl)
            for m in range(KD):
                add_square(N_A, m, m)
            inverse(N_A, rb)

            def adaln(i, q):
                a = i * 6 + q
                dve.wait_ge(s_ada_in[q % 2], i * 48 + 16 * (q // 2 + 1))
                dst = mod[:, a:a + 1] if isinstance(a, int) else mod[:, bass.ds(a, 1)]
                w = ada[:, q % 2, :]
                v.scalar_tensor_tensor(w, w, 1.0, crow[:, :], ALU.mult, ALU.mult, accum_out=dst).then_inc(s_ada, 1)

            dve.wait_ge(s_cact, 1)

            def a_ch(i):
                for k in range(2):
                    for half, dst in enumerate((CG, CU)):
                        M = M0["A_CH"] + 2 * k + half
                        product(M, i, 4)
                        v.tensor_tensor(dst[:, :], ps[M % 4][:, :], rb[:, :], ALU.mult).then_inc(s_ev, 1)
                    dve.wait_ge(s_ev, i * 4 + (M + 1))
                    ch.link(v.tensor_tensor(TG[:, 2:S + 2], CG[:, :], CU[:, :], ALU.mult))
                    conv(at(CV, i * 2 + k), TG, "a_conv", i * 2 + k, KD, ch.link)
                    for q in range(3 * k, 3 * k + 3):
                        adaln(i, q)
            repeat(dve, 4, a_ch, ch, 8)

            def a_b(i):
                for k in range(4):
                    j, M = i * 4 + k, M0["A_B"] + k
                    product(M, i, 4)
                    v.tensor_tensor(CG[:, :], ps[M % 4][:, :], rb[:, :], ALU.mult).then_inc(s_ev, 1)
                    dve.wait_ge(s_ev, i * 4 + (M + 1))
                    v.tensor_tensor(CU[:, :], CG[:, :], at(CV, j), ALU.mult).then_inc(s_y, 1)
                    dve.wait_ge(s_yh, j + 1)
                    v.tensor_tensor(at(ML, j), CU[:, :], f32(at(MH, j)), ALU.subtract).then_inc(s_yl, 1)
                    for q in ADA_AT[k]:
                        adaln(i + 4, q)
            repeat(dve, 2, a_b)

            def ada_beside(i, k):
                for q in ADA_AT[k]:
                    adaln(i + 6, q)
            residual("A_OUT", 1, E_F0, "ffn_norm0", N_F0, beside=ada_beside)
            dve.wait_ge(s_ada, 6 * KD)
            b0 = V["b_ada"][0]
            ch.link(v.tensor_tensor(mod[:, :], mod[:, :], vec[:, b0:b0 + 6 * KD], ALU.add))
            for row, (part, g) in enumerate(((1, "g_mix"), (4, "g_ffn"))):
                ch.step(v.scalar_tensor_tensor(gm[:, row, :], mod[:, part * KD:(part + 1) * KD], 1.0,
                                               vec[:, V[g][0]:V[g][0] + KD], ALU.add, ALU.mult))
            for row, part in ((2, 2), (3, 5)):
                ch.link(v.tensor_scalar(gm[:, row, :], mod[:, part * KD:(part + 1) * KD], 1.0, None, ALU.add))
            ch.link(v.tensor_tensor(gm[:, 0, :], gm[:, 0, :], vec[:, V["final"][0]:V["final"][0] + KD], ALU.mult))

            inverse(N_F0, rb)
            up(0, "UP0", True)
            residual("DN0", 3, E_KV, "kv_in", N_KV)

            inverse(N_KV, rb)

            def to_aux(aux, M, scale=None, by=None):
                product(M)
                if aux >= 2:
                    dve.wait_ge(s_aux, aux - 1)
                if by is not None:
                    ins = v.tensor_tensor(AT[:, aux % 2, :], ps[M % 4][:, :], by[:, :], ALU.mult)
                elif scale is not None:
                    ins = v.tensor_scalar(AT[:, aux % 2, :], ps[M % 4][:, :], scale, None, ALU.mult)
                else:
                    ins = v.tensor_copy(AT[:, aux % 2, :], ps[M % 4][:, :])
                ins.then_inc(s_ev, 1)

            ropes = [0]

            def rope(aux, dst):
                if ropes[0]:
                    dve.wait_ge(s_qk, ropes[0])
                ropes[0] += 1
                dve.wait_ge(s_aux, aux + 1)
                v.tensor_tensor(RB[:, :], ps[5 + aux % 2][:, :], sin_t[:, :], ALU.mult).then_inc(s_auxev, 1)
                ch.link(v.tensor_tensor(RA[:, :], AT[:, aux % 2, :], cos_t[:, :], ALU.mult))
                dve.wait_ge(s_auxev, aux + 1)
                v.tensor_tensor(dst, RA[:, :], RB[:, :], ALU.add).then_inc(s_qk, 1)

            def take(aux, dst, src=None):
                dve.wait_ge(s_aux, aux + 1)
                v.tensor_copy(dst, ps[5 + aux % 2][:, :] if src is None else src(ps[5 + aux % 2]))\
                    .then_inc(s_auxev, 1)

            for m in range(KD):
                lo_half(QXH[:, m, :], QXL[:, m, :], X[:, m, :], vcol("b_mix", m), (s_xh, KD * E_Q + m + 1), s_xl)
            for k in range(KKV):
                product(M0["DKV"] + k)
                v.tensor_tensor(CL[:, k, :], ps[(M0["DKV"] + k) % 4][:, :], rb[:, :], ALU.mult).then_inc(s_ev, 1)
                add_square(N_LK, k, k)
            to_aux(AUX_KR, M0["DKV"] + KKV, by=rb)
            inverse(N_LK, rbl)
            for m in range(KKV):
                v.tensor_tensor(CL[:, m, :], CL[:, m, :], rbl[:, :], ALU.mult).then_inc(s_nb, 1)
            for m in range(KKV):
                lo_half(CLH[:, m, :], CLL[:, m, :], CL[:, m, :], vcol("kv_norm", m), (s_lh, m + 1), s_ll)
            dve.wait_ge(s_in["rope"], 32)
            rope(AUX_KR, KR[:, :])
            for k in range(KQ):
                product(M0["DQ"] + k)
                v.tensor_tensor(QL[:, k, :], ps[(M0["DQ"] + k) % 4][:, :], rb[:, :], ALU.mult).then_inc(s_ev, 1)
                add_square(N_LQ, k, k)
            inverse(N_LQ, rbl)
            for m in range(KQ):
                v.tensor_tensor(QL[:, m, :], QL[:, m, :], rbl[:, :], ALU.mult).then_inc(s_nb, 1)
            for m in range(KQ):
                lo_half(XH[:, m, :], XL[:, m, :], QL[:, m, :], vcol("q_norm", m), (s_lh, KKV + m + 1), s_ll)
            for t in range(HEADS // 2):
                for g in range(2):
                    h, M = 2 * t + g, M0["UKV"] + 4 * t + 2 * g
                    product(M)
                    v.tensor_copy(KN[:, h, :], ps[M % 4][:, :]).then_inc(s_ev, 1)
                    if t > 0:
                        take(AUX_V + h - 2, VT[:, h - 2, :])
                    to_aux(AUX_V + h, M + 1)
            for h in range(HEADS):
                M = M0["UQ"] + h
                product(M)
                v.tensor_copy(QN[:, h, :], ps[M % 4][:, :]).then_inc(s_ev, 1)
                if h < 2:
                    take(AUX_V + HEADS - 2 + h, VT[:, HEADS - 2 + h, :])
            for p in range(HEADS // 2):
                to_aux(AUX_QR + p, M0["UQ"] + HEADS + p)
                if p >= 1:
                    rope(AUX_QR + p - 1, QR[:, p - 1, :])
            rope(AUX_QR + HEADS // 2 - 1, QR[:, HEADS // 2 - 1, :])

            dve.wait_ge(s_in["const"], 16)
            v.tensor_copy(mask16[:, 0, :], cc("ident")).then_inc(s_m16, 1)
            v.tensor_copy(mask16[:, 1, :], cc("causal_neg")).then_inc(s_m16, 1)

            def head_lo(h):
                dve.wait_ge(s_oh, h + 1)
                v.tensor_tensor(OL[:, h, :], ps[h % 2][:, :], f32(OH[:, h, :]), ALU.subtract).then_inc(s_ol, 1)

            for a in range(BLOCKS_A + 3):
                if a < BLOCKS_A:
                    L = (a % 4 + 1) * P
                    dve.wait_ge(s_s, a + 1)
                    ch.link(v.reduce_max(stat[:, 0, a:a + 1], ps[SB[a % 4]][:, 0:L], AX_X))
                    v.tensor_scalar(stat[:, 1, a:a + 1], stat[:, 0, a:a + 1], -MLA_SCALE, None, ALU.mult)\
                        .then_inc(s_mx, 1)
                b = a - 3
                if 0 <= b:
                    L = (b % 4 + 1) * P
                    dve.wait_ge(s_pt, b + 1)
                    if b >= 2:
                        dve.wait_ge(s_pv, b - 1)
                    v.tensor_copy(AT[:, b % 2, 0:L], ps[6 + b % 2][:, 0:L]).then_inc(s_ptc, 1)
                b = a - 1
                if 0 <= b < BLOCKS_A:
                    dve.wait_ge(s_p, b + 1)
                    v.reciprocal(stat[:, 3, b:b + 1], stat[:, 2, b:b + 1]).then_inc(s_rs, 1)
                if a % 4 == 1 and a >= 9:
                    head_lo(a // 4 - 2)
            head_lo(HEADS - 1)
            residual("WO", 1, E_F1, "ffn_norm1", N_F1)

            inverse(N_F1, rb)
            up(1, "UP1", True)
            for half in range(2):
                v.memset(rbl[:, half * (S // 2):(half + 1) * (S // 2)], 0.0).then_inc(s_acc2, 1)
            residual("DN1", 3, None, None, N_FIN, second=True)

            dve.wait_ge(s_ssum, N_FIN + 1)
            ch.link(v.tensor_scalar(rb[:, :], ps[4][:, :], 1.0 / D, EPS, ALU.mult, ALU.add))
            ch.link(v.reciprocal(rb[:, :], rb[:, :]))
            dve.wait_ge(s_ssum, N_FIN + 2)
            v.tensor_tensor(acc[:, :], ps[5][:, :], rb[:, :], ALU.mult).then_inc(s_ms, 1)
            dve.wait_ge(s_root, N_FIN + 2)
            ch.link(v.reciprocal(rbl[:, :], acc[:, :]))
            v.tensor_tensor(rbl[:, :], rbl[:, :], rb[:, :], ALU.mult).then_inc(s_rb, 1)
            dve.wait_ge(s_rb, N_FIN + 1)

            def modulated(e, nb0, row, shift, r):
                for m in range(KD + 1):
                    if m < KD:
                        if m >= 2:
                            dve.wait_ge(s_xl, KD * e + m - 1)
                        v.scalar_tensor_tensor(AT[:, m % 2, :], X[:, m, :], gm[:, row, m:m + 1], r[:, :],
                                               ALU.mult, ALU.mult).then_inc(s_nb, 1)
                    if m >= 1:
                        k = m - 1
                        dve.wait_ge(s_xh, KD * e + k + 1)
                        v.scalar_tensor_tensor(XL[:, k, :], AT[:, k % 2, :],
                                               mod[:, shift * KD + k:shift * KD + k + 1], f32(XH[:, k, :]),
                                               ALU.add, ALU.subtract).then_inc(s_xl, 1)
            modulated(E_M2, NB_M2, 0, 0, rbl)
            for m in range(KD):
                v.scalar_tensor_tensor(X[:, m, :], X[:, m, :], vcol("final", m), rb[:, :], ALU.mult, ALU.mult)\
                    .then_inc(s_x, 1)
            dve.wait_ge(s_x, KD)

            dve.wait_ge(s_in["pos"], 16)
            ch.link(v.tensor_copy(rbl[:, :], posi[:, :]))
            ch.link(v.tensor_scalar(rbl[:, :], rbl[:, :], vcol("inv_freq", 0), None, ALU.mult))
            two_pi = 2.0 * np.pi
            part1 = 6.28125
            part2 = 507.0 / 2 ** 18
            part3 = two_pi - part1 - part2
            magic = 1.5 * 2 ** 23
            limit = 3.1415925
            for dst, quarter in ((RA, 0.0), (RB, 0.25)):
                ch.link(v.tensor_scalar(acc[:, :], rbl[:, :], 1.0 / two_pi, quarter, ALU.mult, ALU.add))
                ch.link(v.tensor_scalar(acc[:, :], acc[:, :], magic, None, ALU.add))
                ch.link(v.tensor_scalar(acc[:, :], acc[:, :], -magic, None, ALU.add))
                ch.link(v.scalar_tensor_tensor(dst[:, :], acc[:, :], -part1, rbl[:, :], ALU.mult, ALU.add))
                ch.link(v.scalar_tensor_tensor(dst[:, :], acc[:, :], -part2, dst[:, :], ALU.mult, ALU.add))
                ch.link(v.scalar_tensor_tensor(dst[:, :], acc[:, :], -part3, dst[:, :], ALU.mult, ALU.add))
                ch.link(v.tensor_scalar(dst[:, :], dst[:, :], quarter * two_pi, limit, ALU.add, ALU.min))
                v.tensor_scalar(dst[:, :], dst[:, :], -limit, None, ALU.max).then_inc(s_arg, 1)
            ch.link(v.memset(acc[:, :], 0.0))

            def in_tile(k):
                M, aux = M0["IN2"] + k, AUX_2 + k
                if k < N_TOK:
                    to_aux(aux, M)
                elif k < N_TOK + 3:
                    to_aux(aux, M, scale=QK_SCALE)
                elif k < N_TOK + 6:
                    to_aux(aux, M)
                else:
                    product(M)
                    v.tensor_scalar(FT[:, k - N_TOK, :], ps[M % 4][:, :], QK_SCALE if k < N_TOK + 9 else 1.0, None,
                                    ALU.mult).then_inc(s_ev, 1)

            def blocks(bank):
                return bank[:, :].rearrange("p (n f) -> p n f", n=4)

            def in_take(k):
                aux = AUX_2 + k
                if k < 2:
                    take(aux, VV[:, :, k * P:(k + 1) * P], blocks)
                elif k < 4:
                    take(aux, U[:, :, (k - 2) * P:(k - 1) * P], blocks)
                elif k == 4:
                    take(aux, CV0[:, :, :], blocks)
                elif k < 7:
                    take(aux, CV12[:, :, (k - 5) * P:(k - 4) * P], blocks)
                elif k < 10:
                    take(aux, BV[:, :, (k - 7) * P:(k - 6) * P], blocks)
                elif k < 16:
                    if k == 10:
                        dve.wait_ge(s_trig, 2)
                    rope(aux, FT[:, k - N_TOK, :])

            for k in range(22):
                in_tile(k)
                if k >= 1:
                    in_take(k - 1)

            def by_group(t):
                return t.rearrange("p n (g c) -> p (n g) c", g=GROUPS)
            dve.wait_ge(s_gelu, 1)
            ch.link(v.tensor_tensor(VN[:, :, :], VV[:, :, :], VV[:, :, :], ALU.mult))
            v.reduce_sum(vst[:, 0, :], by_group(VN[:, :, :]), AX_X).then_inc(s_vs, 1)
            dve.wait_ge(s_vr, 1)
            ch.link(v.reciprocal(vst[:, 2, :], vst[:, 1, :]))
            ch.link(v.tensor_tensor(by_group(VN[:, :, :]), by_group(VV[:, :, :]),
                                    vst[:, 2, :].unsqueeze(2).to_broadcast([P, 4 * GROUPS, HD]), ALU.mult))
            dve.wait_ge(s_in["gsgu"], 16)
            v.tensor_tensor(VN[:, :, :], VN[:, :, :], gsgu[:, :].unsqueeze(1).to_broadcast([P, 4, A_W]), ALU.mult)\
                .then_inc(s_vn, 1)
            dve.wait_ge(s_mixed, 1)
            dve.wait_ge(s_gelu, 2)
            for g in range(GROUPS):
                last = v.scalar_tensor_tensor(
                    YA[:, :, g * HD:(g + 1) * HD],
                    ps[g // 2][:, (g % 2) * 256:(g % 2) * 256 + 256].rearrange("p (n c) -> p n c", n=4),
                    vcol("b_sp", g), U[:, :, g * HD:(g + 1) * HD], ALU.add, ALU.mult)
            last.then_inc(s_ya, 1)
            for c in range(A_W // P):
                dve.wait_ge(s_y2h, c + 1)
                v.tensor_tensor(XL[:, c, :], ps[5 + (AUX_YA + c) % 2][:, :], f32(XH[:, c, :]), ALU.subtract)\
                    .then_inc(s_y2l, 1)

            def exponent(b):
                N = (b % 4 + 1) * P
                Z = ZB[b % 2]
                dve.wait_ge(s_r, b + 1)
                ch.link(v.tensor_tensor(Z[:, 0:N], Z[:, 0:N], ps[2 + b % 2][:, 0:N], ALU.subtract))
                v.tensor_tensor(Z[:, 0:P], Z[:, 0:P], cc("strict_neg"), ALU.add).then_inc(s_wa, 1)

            for b in range(BLOCKS_B):
                kb, N = 3 - b % 4, (b % 4 + 1) * P
                dve.wait_ge(s_z, b + 1)
                if b >= 2:
                    dve.wait_ge(s_w, b - 1)
                v.tensor_copy(ZB[b % 2][:, 0:N], ps[b % 2][:, 0:N]).then_inc(s_zb, 1)
                if b >= 1:
                    exponent(b - 1)
                dve.wait_ge(s_ln, b + 1)
                ch.link(v.scalar_tensor_tensor(SP[:, kb, kb * P:S], ZB[b % 2][:, 0:N], 0.0, EB[b % 2][:, 0:N],
                                               ALU.max, ALU.add))
                v.tensor_tensor(SP[:, kb, kb * P:kb * P + P], SP[:, kb, kb * P:kb * P + P], cc("strict"), ALU.mult)\
                    .then_inc(s_sp, 1)
                if b % 8 == 3 and b > 8:
                    pair_lo = b // 8 - 1
                    dve.wait_ge(s_y2h, 2 + pair_lo + 1)
                    v.tensor_tensor(XL[:, 2 + pair_lo, :], ps[6 + pair_lo % 2][:, :], f32(XH[:, 2 + pair_lo, :]),
                                    ALU.subtract).then_inc(s_y2l, 1)
            exponent(BLOCKS_B - 1)
            c = B_HEADS // 2 - 1
            dve.wait_ge(s_y2h, 2 + c + 1)
            v.tensor_tensor(XL[:, 2 + c, :], ps[6 + c % 2][:, :], f32(XH[:, 2 + c, :]), ALU.subtract)\
                .then_inc(s_y2l, 1)

            dve.wait_ge(s_in["mask"], 32)

            def class_lo(r):
                dve.wait_ge(s_y2h, 5 + r + 1)
                v.tensor_tensor(XL[:, 5:8, r::4], ps[6 + r % 2][:, 0:3 * P].rearrange("p (c q) -> p c q", c=3),
                                f32(XH[:, 5:8, r::4]), ALU.subtract).then_inc(s_y2l, 1)

            for u in range(8 + 2):
                if u < 8:
                    r = u // 2
                    dve.wait_ge(s_cz, u + 1)
                    ch.step(v.tensor_tensor(ZC[u % 2][:, 0:S], ps[u % 2][:, :], MK1[:, r, :], ALU.add))
                    ch.link(v.tensor_tensor(ZC[u % 2][:, S:S + 2 * P], ps[2 + u % 2][:, 0:2 * P], MK2[:, :], ALU.add))
                    ch.link(v.reduce_max(cstat[:, 0, u:u + 1], ZC[u % 2][:, :], AX_X))
                    v.tensor_scalar(cstat[:, 1, u:u + 1], cstat[:, 0, u:u + 1], -1.0, None, ALU.mult)\
                        .then_inc(s_cm, 1)
                b = u - 1
                if 0 <= b < 8:
                    dve.wait_ge(s_cp, b + 1)
                    ch.link(v.reciprocal(cstat[:, 3, b:b + 1], cstat[:, 2, b:b + 1]))
                    v.tensor_scalar(PC[b % 2][:, :], PC[b % 2][:, :], cstat[:, 3, b:b + 1], None, ALU.mult)\
                        .then_inc(s_cn, 1)
                    dve.wait_ge(s_ct, b + 1)
                    if b >= 2:
                        dve.wait_ge(s_co, b - 1)
                    ch.step(v.tensor_copy(PCT[b % 2][:, 0:S], ps[4][:, :]))
                    v.tensor_copy(PCT[b % 2][:, S:S + 2 * P], ps[5][:, 0:2 * P]).then_inc(s_cc, 1)
                if u % 2 == 0 and u >= 4:
                    class_lo(u // 2 - 2)
            class_lo(3)
            residual("OUT2", 1, None, None, N_F2, gate=2)

            inverse(N_F2, rb)
            modulated(E_F2, NB_F2, 1, 3, rb)
            up(2, "UP2", False)
            residual("DN2", 3, None, None, N_END, gate=3)
            inverse(N_END, rb)
            for m in range(KD):
                v.scalar_tensor_tensor(X[:, m, :], X[:, m, :], vcol("g_final", m), rb[:, :], ALU.mult, ALU.mult)\
                    .then_inc(s_fin, 1)

        @block.tensor
        def _(pe):
            mm = nc.tensor.matmul

            def tile_ready(t, i=0, per=0):
                pe.wait_ge(s_lo, i * per + (t + 1))

            def bank_free(M, i=0, per=0):
                if M >= 4:
                    pe.wait_ge(s_ev, i * per + (M - 3))
                elif not isinstance(i, int) or i > 0:
                    pe.wait_ge(s_ev, i * per + (M - 3))

            def dot(bank, t, blk, xh, xl, first, last):
                h = WH[t % SPL][:, blk * P:(blk + 1) * P]
                lo = WL[t % SPL][:, blk * P:(blk + 1) * P]
                mm(bank, h, xh, start=first, stop=False)
                mm(bank, h, xl, start=False, stop=False)
                return mm(bank, lo, xh, start=False, stop=last)

            def wide(t, M, i=0, per=0, before=None, src=(XH, XL)):
                tile_ready(t, i, per)
                bank_free(M, i, per)
                for k in range(KD):
                    if before:
                        before(k)
                    last = dot(ps[M % 4][:, :], t, k, src[0][:, k, :], src[1][:, k, :], k == 0, k == KD - 1)
                last.then_inc(s_pe, 1)

            def inputs(e):
                return lambda k: pe.wait_ge(s_xl, KD * e + k + 1)

            def sum_squares(n):
                pe.wait_ge(s_acc, SQ0[n + 1])
                mm(ps[4][:, :], cc("ones"), acc[:, :], start=True, stop=True).then_inc(s_ssum, 1)

            def a_ch(i):
                start = isinstance(i, int)
                for k in range(4):
                    wide(T0["A_CH"] + k, M0["A_CH"] + k, i, 4, inputs(E_A) if start and k == 0 else None)
                    if start and k == 0:
                        pe.wait_ge(s_in["const"], 16)
                        sum_squares(N_A)
            repeat(pe, 4, a_ch, peel=1)

            def a_b(i):
                for k in range(4):
                    wide(T0["A_B"] + k, M0["A_B"] + k, i, 4)
            repeat(pe, 2, a_b)

            def out_product(phase, src, ready):
                def body(i):
                    for k in range(4):
                        wide(T0[phase] + k, M0[phase] + k, i, 4, ready if k == 0 else None, src)
                repeat(pe, KD // 4, body)

            out_product("A_OUT", (MH, ML), lambda k: pe.wait_ge(s_yl, k + 1))

            def up(f, phase, e, n):
                def body(i):
                    start = isinstance(i, int)
                    for k in range(4):
                        wide(T0[phase] + k, M0[phase] + k, i, 4, inputs(e) if start and k == 0 else None)
                        if start and k == 0 and n is not None:
                            sum_squares(n)
                repeat(pe, FF // 2, body, peel=1)

            def down(f, phase):
                def body(i):
                    for k in range(4):
                        M = M0[phase] + k
                        bank_free(M, i, 4)
                        for j in range(3):
                            t = T0[phase] + 3 * k + j
                            tile_ready(t, i, 12)
                            n = min(BLK, FF - BLK * j)
                            pe.wait_ge(s_hl, FF * f + BLK * j + n)
                            for b in range(n):
                                c = BLK * j + b
                                last = dot(ps[M % 4][:, :], t, b, HH[:, c, :], HL[:, c, :], c == 0, c == FF - 1)
                            last.then_inc(s_pe, 1)
                repeat(pe, KD // 4, body)

            up(0, "UP0", E_F0, N_F0)
            down(0, "DN0")

            def swap(aux, M):
                pe.wait_ge(s_ev, M + 1)
                if aux >= 2:
                    pe.wait_ge(s_auxev, aux - 1)
                mm(ps[5 + aux % 2][:, :], cc("swap"), AT[:, aux % 2, :], start=True, stop=True).then_inc(s_aux, 1)

            def turn(aux, M, strided=False):
                pe.wait_ge(s_ev, M + 1)
                if aux >= 2:
                    pe.wait_ge(s_auxev, aux - 1)
                for n in range(4):
                    src = AT[:, aux % 2, n::4] if strided else AT[:, aux % 2, n * P:(n + 1) * P]
                    last = nc.tensor.transpose(ps[5 + aux % 2][:, n * P:(n + 1) * P], src, cc("ident"))
                last.then_inc(s_aux, 1)

            for k in range(3):
                wide(T0["DKV"] + k, M0["DKV"] + k, before=inputs(E_KV) if k == 0 else None)
                if k == 0:
                    sum_squares(N_KV)
            for k in range(KQ):
                wide(T0["DQ"] + k, M0["DQ"] + k, before=inputs(E_Q) if k == 0 else None, src=(QXH, QXL))
                if k == 0:
                    sum_squares(N_LK)
                    swap(AUX_KR, M0["DKV"] + 2)
            for t in range(HEADS // 2):
                tile_ready(T0["UKV"] + t)
                for j in range(4):
                    M = M0["UKV"] + 4 * t + j
                    bank_free(M)
                    for k in range(KKV):
                        if t == 0 and j == 0:
                            pe.wait_ge(s_ll, k + 1)
                        last = dot(ps[M % 4][:, :], T0["UKV"] + t, 2 * j + k, CLH[:, k, :], CLL[:, k, :],
                                   k == 0, k == KKV - 1)
                    last.then_inc(s_pe, 1)
                    if t == 0 and j == 1:
                        sum_squares(N_LQ)
                    if t > 0 and j % 2 == 0:
                        h = 2 * (t - 1) + j // 2
                        turn(AUX_V + h, M0["UKV"] + 2 * h + 1)
            for t in range(6):
                tile_ready(T0["UQ"] + t)
                for j in range(2):
                    M = M0["UQ"] + 2 * t + j
                    bank_free(M)
                    for k in range(KQ):
                        if t == 0 and j == 0:
                            pe.wait_ge(s_ll, KKV + k + 1)
                        last = dot(ps[M % 4][:, :], T0["UQ"] + t, KQ * j + k, XH[:, k, :], XL[:, k, :],
                                   k == 0, k == KQ - 1)
                    last.then_inc(s_pe, 1)
                    if t == 0:
                        h = HEADS - 2 + j
                        turn(AUX_V + h, M0["UKV"] + 2 * h + 1)
                    p = 2 * t + j - HEADS - 1
                    if p >= 0:
                        swap(AUX_QR + p, M0["UQ"] + HEADS + p)
            swap(AUX_QR + HEADS // 2 - 1, M0["UQ"] + HEADS + HEADS // 2 - 1)

            pe.wait_ge(s_qk, 1 + HEADS // 2)
            pe.wait_ge(s_m16, 2)
            for a in range(BLOCKS_A + 4):
                if a < BLOCKS_A:
                    h, qb = a // 4, a % 4
                    L, half = (qb + 1) * P, h % 2 * HD
                    bank = ps[SB[a % 4]]
                    if a >= 4:
                        pe.wait_ge(s_p, a - 3)
                    mm(bank[:, 0:L], QN[:, h, qb * P:L], KN[:, h, 0:L], start=True, stop=False)
                    mm(bank[:, L - P:L], mask16[:, 0, :], mask16[:, 1, :], start=False, stop=False,
                       skip_group_check=True)
                    mm(bank[:, 0:L], QR[half:half + HD, h // 2, qb * P:L], KR[half:half + HD, 0:L],
                       start=False, stop=True).then_inc(s_s, 1)
                b = a - 2
                if 0 <= b < BLOCKS_A:
                    pe.wait_ge(s_pn, b + 1)
                    if b >= 2:
                        pe.wait_ge(s_ptc, b - 1)
                    for kb in range(b % 4 + 1):
                        last = nc.tensor.transpose(ps[6 + b % 2][:, kb * P:(kb + 1) * P],
                                                   PB[b % 4][:, kb * P:(kb + 1) * P], cc("ident"))
                    last.then_inc(s_pt, 1)
                b = a - 4
                if 0 <= b:
                    h, qb = b // 4, b % 4
                    pe.wait_ge(s_ptc, b + 1)
                    if qb == 0 and h >= 2:
                        pe.wait_ge(s_ol, h - 1)
                    for kb in range(qb + 1):
                        last = mm(ps[h % 2][:, qb * P:(qb + 1) * P], VT[:, h, kb * P:(kb + 1) * P],
                                  AT[:, b % 2, kb * P:(kb + 1) * P], start=kb == 0, stop=kb == qb)
                    last.then_inc(s_pv, 1)
            pe.wait_ge(s_ol, HEADS)
            out_product("WO", (OH, OL), lambda k: None)
            up(1, "UP1", E_F1, N_F1)
            down(1, "DN1")

            sum_squares(N_FIN)
            pe.wait_ge(s_acc2, KD + 2)
            mm(ps[5][:, :], cc("ones"), rbl[:, :], start=True, stop=True).then_inc(s_ssum, 1)
            n_in = 22

            def second_trip(k):
                aux, M = AUX_2 + k, M0["IN2"] + k
                if k < N_TOK:
                    turn(aux, M, strided=k in (5, 6))
                elif k < N_TOK + 6:
                    swap(aux, M)
            for k in range(n_in):
                wide(T0["IN2"] + k, M0["IN2"] + k, before=inputs(E_M2) if k == 0 else None)
                if k >= 1:
                    second_trip(k - 1)
            pe.wait_ge(s_ws, 1)
            pe.wait_ge(s_vn, 1)
            for g in range(GROUPS):
                last = mm(ps[g // 2][:, (g % 2) * 256:(g % 2) * 256 + 256].rearrange("p (n c) -> p n c", n=4),
                          WS[:, g, :], VN[:, :, g * HD:(g + 1) * HD], start=True, stop=True)
            last.then_inc(s_mixed, 1)
            pe.wait_ge(s_ya, 1)
            for c in range(A_W // P):
                aux = AUX_YA + c
                for n in range(4):
                    last = nc.tensor.transpose(ps[5 + aux % 2][:, n * P:(n + 1) * P], YA[:, n, c * P:(c + 1) * P],
                                               cc("ident"))
                last.then_inc(s_aux, 1)
            pe.wait_ge(s_y2l, A_W // P)

            for b in range(BLOCKS_B + 2):
                if b < BLOCKS_B:
                    h, kb = b // 4, 3 - b % 4
                    N, half = S - kb * P, h % 2 * HD
                    if b >= 2:
                        pe.wait_ge(s_zb, b - 1)
                    mm(ps[b % 2][:, 0:N], FT[half:half + HD, 9 + h // 2, kb * P:(kb + 1) * P],
                       FT[half:half + HD, 6 + h // 2, kb * P:S], start=True, stop=True).then_inc(s_z, 1)
                c = b - 1
                if 0 <= c < BLOCKS_B:
                    kb = 3 - c % 4
                    N = S - kb * P
                    pe.wait_ge(s_sp, c + 1)
                    if c >= 2:
                        pe.wait_ge(s_wa, c - 1)
                    last = mm(ps[2 + c % 2][:, 0:N], cc("tri"), SP[:, kb, kb * P:S], start=True, stop=True)
                    for later in range(kb + 1, 4):
                        last = mm(ps[2 + c % 2][:, (later - kb) * P:N], cc("ones"), SP[:, later, later * P:S],
                                  start=False, stop=True, skip_group_check=True)
                    last.then_inc(s_r, 1)
                c = b - 2
                if 0 <= c:
                    h, kb = c // 4, 3 - c % 4
                    half = h % 2 * HD
                    pe.wait_ge(s_w, c + 1)
                    if h == 4 and kb == 3:
                        pe.wait_ge(s_y2l, 3)
                    mm(ps[6 + h // 2 % 2][half:half + HD, kb * P:S], BV[:, kb, h * HD:(h + 1) * HD],
                       WT[c % 2][:, 0:S - kb * P], start=kb == 3, stop=True, skip_group_check=True)\
                        .then_inc(s_bo, 1)

            pe.wait_ge(s_y2l, 5)
            for u in range(8 + 2):
                if u < 8:
                    r, half = u // 2, u % 2 * HD
                    if u >= 2:
                        pe.wait_ge(s_cm, u - 1)
                    mm(ps[u % 2][:, :], FT[half:half + HD, 0, r::4], FT[half:half + HD, 3, :], start=True, stop=True)
                    for g in (1, 2):
                        last = mm(ps[2 + u % 2][:, (g - 1) * P:g * P], FT[half:half + HD, g, r::4],
                                  FT[half:half + HD, 3 + g, r::4], start=True, stop=True)
                    last.then_inc(s_cz, 1)
                b = u - 1
                if 0 <= b < 8:
                    pe.wait_ge(s_cn, b + 1)
                    if b >= 1:
                        pe.wait_ge(s_cc, b)
                    for n in range(6):
                        last = nc.tensor.transpose(ps[4 + n // 4][:, n % 4 * P:(n % 4 + 1) * P],
                                                   PC[b % 2][:, n * P:(n + 1) * P], cc("ident"))
                    last.then_inc(s_ct, 1)
                b = u - 2
                if 0 <= b:
                    r, half = b // 2, b % 2 * HD
                    pe.wait_ge(s_cc, b + 1)
                    if r >= 2 and b % 2 == 0:
                        pe.wait_ge(s_y2l, 5 + r - 1)
                    dst = ps[6 + r % 2]
                    for kb in range(4):
                        mm(dst[half:half + HD, 0:P], CV0[:, kb, half:half + HD], PCT[b % 2][:, kb * P:(kb + 1) * P],
                           start=kb == 0, stop=kb == 3)
                    for g in (1, 2):
                        last = mm(dst[half:half + HD, g * P:(g + 1) * P],
                                  CV12[:, r, (g - 1) * P + half:(g - 1) * P + half + HD],
                                  PCT[b % 2][:, (3 + g) * P:(4 + g) * P], start=True, stop=True)
                    last.then_inc(s_co, 1)
            pe.wait_ge(s_y2l, 9)
            out_product("OUT2", (XH, XL), lambda k: None)
            sum_squares(N_F2)
            up(2, "UP2", E_F2, None)
            down(2, "DN2")
            sum_squares(N_END)


def constants():
    C = const_layout()
    i = np.arange(P)
    c = np.zeros((P, C["width"]), np.float32)

    def put(name, a):
        c[:, C[name][0]:C[name][0] + C[name][1]] = a
    put("ident", i[:, None] == i[None, :])
    put("swap", (i[:, None] // 64 == i[None, :] // 64) & ((i[:, None] + 32) % 64 == i[None, :] % 64))
    put("ones", 1.0)
    put("tri", i[:, None] >= i[None, :])
    put("causal_neg", np.where(i[None, :] <= i[:, None], 0.0, NEG))
    put("strict", i[:, None] < i[None, :])
    put("strict_neg", np.where(i[:, None] < i[None, :], 0.0, NEG))
    inv = (1.0 / (np.float32(THETA) ** (np.arange(0, ROPE, 2, dtype=np.float32) / np.float32(ROPE)))).astype(np.float32)
    ang = np.arange(S, dtype=np.float32)[:, None] * inv[None, :]
    row = i % 32
    sign = np.where(i % 64 < 32, -1.0, 1.0).astype(np.float32)
    rope = np.stack([np.cos(ang).T[row], np.sin(ang).T[row] * sign[:, None]]).astype(np.float32)
    inv2 = (np.float32(THETA) ** (-np.arange(0, HD, 2, dtype=np.float32) / np.float32(HD))).astype(np.float32)
    mask1 = np.zeros((P, 4, S), np.float32)
    k = np.arange(S)
    for r in range(4):
        q = r + 4 * i
        d = q[:, None] - k[None, :]
        mask1[:, r, :] = np.where((d >= 0) & (d < N_OFFSETS), 0.0, NEG)
    d = i[:, None] - i[None, :]
    mask2 = np.concatenate([np.where(d >= 0, 0.0, NEG), np.where((d >= 0) & (d % 4 == 0), 0.0, NEG)], 1)
    return c, rope, mask1, mask2.astype(np.float32), inv2[row][:, None], sign[:, None]


def kernel(**inputs):
    import concourse.bacc as _bacc
    from concourse.bass_utils import run_bass_kernel_spmd as _run

    a = {k: np.asarray(v) for k, v in inputs.items()}
    const, rope, mask1, mask2, inv2, sign = constants()

    def chunks(v):
        v = v.reshape(-1, P)
        return v.T

    V = vec_layout()
    parts = {
        "a_mix": chunks(a["a_mix_norm"]), "a_conv": chunks(a["a_conv"]), "b_mix": chunks(a["b_mix_norm"]),
        "q_norm": chunks(a["b_q_norm"]), "kv_in": chunks(a["kv_in_norm"]), "kv_norm": chunks(a["kv_norm"]),
        "ffn_norm0": chunks(a["ffn_norm"][0]), "ffn_norm1": chunks(a["ffn_norm"][1]),
        "ffn_conv0": chunks(a["ffn_conv"][0]), "ffn_conv1": chunks(a["ffn_conv"][1]),
        "final": chunks(a["final_norm"]), "b_ada": chunks(a["b_ada_2"]),
        "g_mix": chunks(a["g_mix_2"]), "g_ffn": chunks(a["g_ffn_2"]), "ffn_conv2": chunks(a["conv_w_2"]),
        "conv_b": chunks(a["conv_b_2"]), "g_final": chunks(a["g_final_2"]), "b_sp": a["b_sp_2"][0].T,
        "inv_freq": inv2, "sin_sign": sign,
    }
    vec = np.ascontiguousarray(np.concatenate([parts[n] for n in V if n != "width"], axis=1))
    assert vec.shape == (P, V["width"])

    def tiles(w, cols=None):
        w = w if cols is None else w[:, cols]
        kc, n = w.shape[0] // P, w.shape[1] // P
        t = w.reshape(kc, P, n, P).transpose(2, 0, 1, 3)
        if kc > BLK:
            pad = -kc % BLK
            t = np.concatenate([t, np.zeros((n, pad, P, P), t.dtype)], axis=1)
        t = t.reshape(-1, BLK, P, P).transpose(0, 2, 1, 3)
        return t.reshape(-1, P, TILE)

    def interleave(*starts):
        firsts, n = starts[:-1], starts[-1]
        return np.concatenate([np.arange(f + j * P, f + (j + 1) * P) for j in range(n) for f in firsts])

    hw = np.arange(NOPE + ROPE)
    uq_cols = np.concatenate([h * (NOPE + ROPE) + hw[:NOPE] for h in range(HEADS)]
                             + [h * (NOPE + ROPE) + hw[NOPE:] for h in range(HEADS)])
    dkv_cols = np.concatenate([np.arange(KV_LORA + ROPE), KV_LORA + np.arange(ROPE)])
    offs = np.cumsum([0, A_W, A_W, B_W, B_W, B_W, C_W, C_W, C_W])
    a_u, a_v, b_q, b_k, b_v, c_q, c_k, c_v = [np.arange(offs[i], offs[i + 1]) for i in range(8)]
    in2_cols = np.concatenate([a_v, a_u, c_v, b_v, c_q, c_k, b_q, b_k])
    up_cols = interleave(0, D_FF, FF)
    w_all = np.ascontiguousarray(np.concatenate([
        tiles(a["a_w_in"][0], interleave(D, 2 * D, KD)), tiles(a["a_w_in"][0], np.arange(D)),
        tiles(a["a_w_out"][0]), tiles(a["ffn_w_up"][0], up_cols), tiles(a["ffn_w_down"][0]),
        tiles(a["w_dkv"], dkv_cols), tiles(a["b_w_dq"][0]), tiles(a["w_ukv"]), tiles(a["b_w_uq"][0], uq_cols),
        tiles(a["b_w_o"][0]), tiles(a["ffn_w_up"][1], up_cols), tiles(a["ffn_w_down"][1]),
        tiles(a["w_in_2"][0], in2_cols), tiles(a["w_out_2"][0]), tiles(a["w_up_2"][0], up_cols),
        tiles(a["w_down_2"][0]),
    ]))
    assert len(w_all) == len(schedule()[2])
    arrays = {
        "w_tiles": w_all, "ada_tiles": np.ascontiguousarray(a["w_ada_2"][0].T).reshape(6 * KD, P, D),
        "c_in": np.ascontiguousarray(np.broadcast_to(a["c_2"][0], (P, D))),
        "x_in": np.ascontiguousarray(a["x"][0].T.reshape(KD, P, S).transpose(1, 0, 2)),
        "vec_in": vec, "const_in": const, "rope_in": rope, "mask1_in": mask1, "mask2_in": mask2,
        "gsgu_in": np.ascontiguousarray(np.broadcast_to(a["g_sgu_2"][0], (P, A_W))),
        "wsp_in": np.ascontiguousarray(a["w_sp_2"][0].transpose(2, 0, 1)),
        "pos_in": np.ascontiguousarray(np.broadcast_to(a["positions_2"][0], (P, S))),
    }
    nc = _bacc.Bacc("TRN2", target_bir_lowering=False, num_devices=1)
    aps = {n: nc.dram_tensor(n, v.shape, mybir.dt.from_np(v.dtype), kind="ExternalInput").ap()
           for n, v in arrays.items()}
    out = nc.dram_tensor("out_x", (P, KD, S), F32, kind="ExternalOutput").ap()
    build(nc, out=out, **aps)
    r = _run(nc, [arrays], core_ids=[0])
    got = r.results[0]["out_x"]
    return np.ascontiguousarray(got.transpose(1, 0, 2).reshape(D, S).T)[None]
```

```python
from contextlib import ExitStack

import numpy as np
import concourse.bass as bass
from concourse import mybir

F32 = mybir.dt.float32
F32R = mybir.dt.float32r
I32 = mybir.dt.int32
BF16 = mybir.dt.bfloat16
ACT = mybir.ActivationFunctionType
ALU = mybir.AluOpType
AX_X = mybir.AxisListType.X

P = 128
D = 1024
KD = D // P
S = 512
D_FF = 2816
FF = D_FF // P
HEADS = 8
NOPE, ROPE, VD = 128, 64, 128
Q_LORA, KV_LORA = 512, 256
KQ, KKV = Q_LORA // P, KV_LORA // P
THETA = 10000.0
EPS = 1e-6
MLA_SCALE = float((NOPE + ROPE) ** -0.5)
HD = 64
A_W, B_W, C_W = 256, 384, 384
GROUPS = A_W // HD
B_HEADS = B_W // HD
QK_SCALE = HD ** -0.5
N_OFFSETS = 129
NEG = -1.0e30
BLK = 8
TILE = BLK * P
RAW = 4
SPL = 2
ADA = 6
CONV = 3


def vec_layout():
    at, out = 0, {}
    for name, n in (("a_mix", KD), ("a_conv", CONV * KD), ("b_mix", KD), ("q_norm", KQ), ("kv_in", KD),
                    ("kv_norm", KKV), ("ffn_norm0", KD), ("ffn_norm1", KD), ("ffn_conv0", CONV * 2 * FF),
                    ("ffn_conv1", CONV * 2 * FF), ("final", KD), ("b_ada", 6 * KD), ("g_mix", KD),
                    ("g_ffn", KD), ("ffn_conv2", CONV * 2 * FF), ("conv_b", 2 * FF), ("g_final", KD),
                    ("b_sp", GROUPS), ("inv_freq", 1), ("sin_sign", 1)):
        out[name] = (at, n)
        at += n
    out["width"] = at
    return out


def const_layout():
    at, out = 0, {}
    for name, n in (("ident", P), ("swap", P), ("ones", P), ("tri", P), ("causal_neg", P), ("strict", P),
                    ("strict_neg", P)):
        out[name] = (at, n)
        at += n
    out["width"] = at
    return out


PHASES = (
    ("A_CH", 16, [1]), ("A_B", 8, [1]), ("A_OUT", 8, [1]),
    ("UP0", 2 * FF, [1]), ("DN0", 24, [0, 0, 1]),
    ("DKV", 3, [1]), ("DQ", 4, [1]), ("UKV", 4, [4]), ("UQ", 6, [2]), ("WO", 8, [1]),
    ("UP1", 2 * FF, [1]), ("DN1", 24, [0, 0, 1]),
    ("IN2", 22, [1]), ("OUT2", 8, [1]), ("UP2", 2 * FF, [1]), ("DN2", 24, [0, 0, 1]),
)


def schedule():
    t0, m0, done_t, done_m, steps = {}, {}, [], [], 0
    for name, tiles, ends in PHASES:
        t0[name], m0[name] = len(done_t), len(done_m)
        for i in range(tiles):
            n = ends[i % len(ends)]
            for _ in range(n):
                steps += 1
                done_m.append(steps)
            steps += n == 0
            done_t.append(steps)
    return t0, m0, done_t, done_m


def build(nc, w_tiles, ada_tiles, c_in, x_in, vec_in, const_in, rope_in, mask1_in, mask2_in, gsgu_in, wsp_in, pos_in, out):
    T0, M0, DONE_T, DONE_M = schedule()
    NT = len(DONE_T)
    V = vec_layout()
    C = const_layout()
    ctx = ExitStack()
    with ctx:
        def sb(name, shape, dt=F32, stack=ctx):
            return stack.enter_context(nc.sbuf_tensor(name, shape, dt))

        def sem(name):
            return ctx.enter_context(nc.semaphore(name))

        X = sb("X", [P, KD, S])
        XH = sb("XH", [P, KD, S], F32R)
        XL = sb("XL", [P, KD, S], F32R)
        raw = sb("raw", [P, RAW, TILE])
        WH = [sb(f"WH{i}", [P, TILE], F32R) for i in range(SPL)]
        WL = [sb(f"WL{i}", [P, TILE], F32R) for i in range(SPL)]
        vec = sb("vec", [P, V["width"]])
        cst = sb("cst", [P, C["width"]])
        cos_t = sb("cos_t", [P, S])
        sin_t = sb("sin_t", [P, S])
        rb = sb("rb", [P, S])
        rbl = sb("rbl", [P, S])
        acc = sb("acc", [P, S])
        SQ = sb("SQ", [P, 2, S])
        AT = sb("AT", [P, 2, S])
        RA = sb("RA", [P, S])
        RB = sb("RB", [P, S])
        mask16 = sb("mask16", [P, 2, P], BF16)
        mod = sb("mod", [P, 6 * KD])
        gm = sb("gm", [P, 4, KD])
        epsc = sb("epsc", [P, 1])
        gsgu = sb("gsgu", [P, A_W])
        nt = sb("nt", [P, 5, 4])

        st = ExitStack()
        CV = sb("CV", [P, KD, S], F32, st)
        MH = sb("MH", [P, KD, S], F32R, st)
        ML = sb("ML", [P, KD, S], F32R, st)
        ada = sb("ada", [P, ADA, D], F32, st)
        crow = sb("crow", [P, D], F32, st)
        st.close()
        st = ExitStack()
        HH = sb("HH", [P, FF, S], F32R, st)
        HL = sb("HL", [P, FF, S], F32R, st)
        TG = sb("TG", [P, S + 2], F32, st)
        TU = sb("TU", [P, S + 2], F32, st)
        CG = sb("CG", [P, S], F32, st)
        CU = sb("CU", [P, S], F32, st)
        st.close()
        st = ExitStack()
        QXH = sb("QXH", [P, KD, S], F32R, st)
        QXL = sb("QXL", [P, KD, S], F32R, st)
        st.close()
        st = ExitStack()
        KN = sb("KN", [P, HEADS, S], F32, st)
        VT = sb("VT", [P, HEADS, S], F32, st)
        KR = sb("KR", [P, S], F32, st)
        QN = sb("QN", [P, HEADS, S], F32, st)
        QR = sb("QR", [P, HEADS // 2, S], F32, st)
        stat = sb("stat", [P, 4, 4 * HEADS], F32, st)
        st2 = ExitStack()
        CL = sb("CL", [P, KKV, S], F32, st2)
        CLH = sb("CLH", [P, KKV, S], F32R, st2)
        CLL = sb("CLL", [P, KKV, S], F32R, st2)
        QL = sb("QL", [P, KQ, S], F32, st2)
        st2.close()
        OH = sb("OH", [P, HEADS, S], F32R, st)
        OL = sb("OL", [P, HEADS, S], F32R, st)
        st.close()
        st = ExitStack()
        FT = sb("FT", [P, 12, S], F32, st)
        BV = sb("BV", [P, 4, B_W], F32, st)
        CV0 = sb("CV0", [P, 4, P], F32, st)
        CV12 = sb("CV12", [P, 4, 2 * P], F32, st)
        WS = sb("WS", [P, GROUPS, P], F32, st)
        MK1 = sb("MK1", [P, 4, S], F32, st)
        MK2 = sb("MK2", [P, 2 * P], F32, st)
        posi = sb("posi", [P, S], I32, st)
        st2 = ExitStack()
        U = sb("U", [P, 4, A_W], F32, st2)
        VV = sb("VV", [P, 4, A_W], F32, st2)
        VN = sb("VN", [P, 4, A_W], F32, st2)
        YA = sb("YA", [P, 4, A_W], F32, st2)
        vst = sb("vst", [P, 3, 4 * GROUPS], F32, st2)
        st2.close()
        st2 = ExitStack()
        ZB = [sb(f"ZB{i}", [P, S], F32, st2) for i in range(4)]
        EB = [sb(f"EB{i}", [P, S], F32, st2) for i in range(2)]
        SP = sb("SP", [P, 8, S], F32, st2)
        WT = [sb(f"WT{i}", [P, S], F32, st2) for i in range(2)]
        st2.close()
        st2 = ExitStack()
        ZC = [sb(f"ZC{i}", [P, S + 2 * P], F32, st2) for i in range(2)]
        PC = [sb(f"PC{i}", [P, S + 2 * P], F32, st2) for i in range(3)]
        PCT = [sb(f"PCT{i}", [P, S + 2 * P], F32, st2) for i in range(2)]
        cstat = sb("cstat", [P, 4, 8], F32, st2)
        st2.close()
        st.close()

        PB = [SQ[:, 0, :], SQ[:, 1, :], RA[:, :], RB[:, :]]
        SB = (4, 5, 2, 3)

        ps = [ctx.enter_context(nc.psum_tensor(f"ps{i}", [P, S], F32)) for i in range(8)]

        MIXED = (ps[7], ps[4])

        s_in = {n: sem(f"s_in_{n}") for n in ("x0", "x1", "x2", "x3", "c", "vec", "const", "rope", "gsgu", "wsp", "mask", "pos")}
        s_raw = [sem(f"s_raw{i}") for i in range(RAW)]
        s_hi = sem("s_hi")
        s_lo = sem("s_lo")
        s_pe = sem("s_pe")
        s_ev = sem("s_ev")
        s_ada_in = [sem(f"s_ada_in{i}") for i in range(ADA)]
        s_ada = sem("s_ada")
        s_cact = sem("s_cact")
        s_set = sem("s_set")
        s_x = sem("s_x")
        s_sq = sem("s_sq")
        s_acc = sem("s_acc")
        s_sq2 = sem("s_sq2")
        s_acc2 = sem("s_acc2")
        s_ms = sem("s_ms")
        s_ssum = sem("s_ssum")
        s_root = sem("s_root")
        s_rb = sem("s_rb")
        s_dg = sem("s_dg")
        s_bc = sem("s_bc")
        s_xh = sem("s_xh")
        s_xl = sem("s_xl")
        s_nb = sem("s_nb")
        s_dve = sem("s_dve")
        s_act = sem("s_act")
        s_gc = sem("s_gc")
        s_sg = sem("s_sg")
        s_h = sem("s_h")
        s_hh = sem("s_hh")
        s_hl = sem("s_hl")
        s_y = sem("s_y")
        s_yh = sem("s_yh")
        s_yl = sem("s_yl")
        s_aux = sem("s_aux")
        s_auxev = sem("s_auxev")
        s_lh = sem("s_lh")
        s_ll = sem("s_ll")
        s_qk = sem("s_qk")
        s_m16 = sem("s_m16")
        s_s = sem("s_s")
        s_mx = sem("s_mx")
        s_p = sem("s_p")
        s_rs = sem("s_rs")
        s_pn = sem("s_pn")
        s_pt = sem("s_pt")
        s_ptc = sem("s_ptc")
        s_pv = sem("s_pv")
        s_oh = sem("s_oh")
        s_ol = sem("s_ol")
        s_ws = sem("s_ws")
        s_arg = sem("s_arg")
        s_trig = sem("s_trig")
        s_gelu = sem("s_gelu")
        s_vs = sem("s_vs")
        s_vr = sem("s_vr")
        s_vn = sem("s_vn")
        s_mixed = sem("s_mixed")
        s_ya = sem("s_ya")
        s_y2h = sem("s_y2h")
        s_y2l = sem("s_y2l")
        s_z = sem("s_z")
        s_zb = sem("s_zb")
        s_ln = sem("s_ln")
        s_sp = sem("s_sp")
        s_r = sem("s_r")
        s_wa = sem("s_wa")
        s_w = sem("s_w")
        s_bo = sem("s_bo")
        s_cz = sem("s_cz")
        s_cm = sem("s_cm")
        s_cp = sem("s_cp")
        s_crs = sem("s_crs")
        s_cn = sem("s_cn")
        s_ct = sem("s_ct")
        s_cc = sem("s_cc")
        s_co = sem("s_co")
        s_fin = sem("s_fin")
        s_out = sem("s_out")

        block = ctx.enter_context(nc.Block())

        def vcol(name, i):
            first = V[name][0]
            return vec[:, first + i:first + i + 1] if isinstance(i, int) else vec[:, bass.ds(i + first, 1)]

        def cc(name):
            return cst[:, C[name][0]:C[name][0] + C[name][1]]

        def at(t, i):
            return t[:, i, :] if isinstance(i, int) else t[:, bass.ds(i, 1), :].rearrange("p a b -> p (a b)")

        def f32(ap):
            return ap.bitcast(F32)

        ADA_AT = ((0, 1), (2,), (3, 4), (5,))
        NORM_CHUNKS = [KD, KD, KD, KKV, KQ, KD, KD, KD, KD]
        N_A, N_F0, N_KV, N_LK, N_LQ, N_F1, N_FIN, N_F2, N_END = range(9)
        SQ0 = [sum(NORM_CHUNKS[:i]) for i in range(10)]
        E_A, E_F0, E_KV, E_Q, E_F1, E_M2, E_F2 = range(7)
        NB_KV, NB_Q, NB_M2, NB_F2 = 0, KKV, KKV + KQ, KKV + KQ + KD
        AUX_KR, AUX_V, AUX_QR = 0, 1, 1 + HEADS
        AUX_2 = AUX_QR + HEADS // 2
        N_TOK = 2 * (A_W // P) + C_W // P + B_W // P
        AUX_YA = AUX_2 + N_TOK + 2 * (C_W // P)
        BLOCKS_A = 4 * HEADS
        BLOCKS_B = 4 * B_HEADS

        class Chain:

            def __init__(self, eng, s):
                self.eng, self.s, self.n, self.i, self.per = eng, s, 0, None, 0

            def enter(self, i, per):
                self.i, self.per, self.base = i, per, self.n

            def leave(self):
                assert self.n - self.base == self.per, (self.n - self.base, self.per)
                self.n, self.i = self.base, None

            def step(self, ins):
                ins.then_inc(self.s, 1)
                self.n += 1

            def wait(self):
                self.eng.wait_ge(self.s, self.n if self.i is None else self.i * self.per + self.n)

            def link(self, ins):
                self.step(ins)
                self.wait()

        def repeat(eng, times, body, chain=None, per=0, peel=0):
            def one(i):
                if chain:
                    chain.enter(i, per)
                body(i)
                if chain:
                    chain.leave()
            for i in range(peel):
                one(i)
            if times > peel:
                with eng.Fori(peel, times) as i:
                    one(i)
            if chain:
                chain.n += times * per

        @block.sync
        def _(sp):
            def load(t, slot, first=False):
                if not first:
                    sp.wait_ge(s_lo, t - (RAW - 1))
                src = w_tiles[t] if isinstance(t, int) else \
                    w_tiles[bass.ds(t, 1), :, :].rearrange("a p n -> p (a n)")
                sp.dma_start(raw[:, slot, :], src).then_inc(s_raw[slot], 16)

            def load_ada(a, slot, first=False):
                if not first:
                    sp.wait_ge(s_ada, a - (ADA - 1))
                src = ada_tiles[a] if isinstance(a, int) else \
                    ada_tiles[bass.ds(a, 1), :, :].rearrange("a p n -> p (a n)")
                sp.dma_start(ada[:, slot, :], src).then_inc(s_ada_in[slot], 16)

            for k in range(RAW):
                load(k, k, True)

            def with_ada(i):
                for k in range(RAW):
                    load(i * RAW + (RAW + k), k)
                    for q in ADA_AT[k]:
                        load_ada(i * ADA + q, q, isinstance(i, int))
            n_ada = 6 * KD // 6
            repeat(sp, n_ada, with_ada, peel=1)

            def four(i):
                for k in range(RAW):
                    load(i * RAW + ((n_ada + 1) * RAW + k), k)
            repeat(sp, NT // RAW - n_ada - 1, four)
            for t in range(NT // RAW * RAW, NT):
                load(t, t % RAW)
            for m in range(KD):
                sp.wait_ge(s_fin, m + 1)
                sp.dma_start(out[:, m, :], X[:, m, :]).then_inc(s_out, 16)
            sp.wait_ge(s_out, 16 * KD)

        @block.gpsimd
        def _(pool):
            def lo(t, k):
                pool.wait_ge(s_hi, t + 1)
                nc.gpsimd.tensor_tensor(WL[k % SPL][:, :], raw[:, k, :], f32(WH[k % SPL][:, :]),
                                        ALU.subtract).then_inc(s_lo, 1)

            cut = (T0["IN2"] + RAW) // RAW

            def before(i):
                for k in range(RAW):
                    lo(i * RAW + k, k)
            repeat(pool, cut, before)
            pool.wait_ge(s_in["wsp"], 16)
            nc.gpsimd.affine_select(out=WS[:, :, :], in_=WS[:, :, :], compare_op=ALU.is_ge, fill=0.0, base=0,
                                    pattern=[[0, GROUPS], [1, P]], channel_multiplier=-1).then_inc(s_ws, 1)

            def after(i):
                for k in range(RAW):
                    lo(i * RAW + (cut * RAW + k), k)
            repeat(pool, NT // RAW - cut, after)
            for t in range(NT // RAW * RAW, NT):
                lo(t, t % RAW)

        @block.scalar
        def _(act):
            ch = Chain(act, s_act)
            act.dma_start(vec[:, :], vec_in).then_inc(s_in["vec"], 16)
            for m in range(4):
                act.dma_start(X[:, 2 * m:2 * m + 2, :], x_in[:, 2 * m:2 * m + 2, :]).then_inc(s_in[f"x{m}"], 16)
            act.dma_start(crow[:, :], c_in).then_inc(s_in["c"], 16)
            act.dma_start(cst[:, :], const_in).then_inc(s_in["const"], 16)
            act.dma_start(cos_t[:, :], rope_in[0]).then_inc(s_in["rope"], 16)
            act.dma_start(sin_t[:, :], rope_in[1]).then_inc(s_in["rope"], 16)
            act.dma_start(gsgu[:, :], gsgu_in).then_inc(s_in["gsgu"], 16)

            def hi(t, i=0, per=0):
                slot = t % RAW
                act.wait_ge(s_raw[slot], i * (16 * per // RAW) + 16 * (t // RAW + 1))
                nc.scalar.activation(WH[t % SPL][:, :], raw[:, slot, :], ACT.Copy).then_inc(s_hi, 1)

            def ahead(t, i=0, per=0):
                if not isinstance(i, int) or t + i * per + SPL < NT:
                    act.wait_ge(s_pe, i * per + DONE_T[t])
                    hi(t + SPL, i, per)

            def apart():
                act.wait_ge(s_set, 1)

            def square(n, m, k, src):
                act.wait_ge(s_acc, m + (SQ0[n] - 1))
                nc.scalar.activation(SQ[:, k % 2, :], src, ACT.Square).then_inc(s_sq, 1)

            def token_root(n):
                act.wait_ge(s_ssum, n + 2)
                nc.scalar.activation(nt[:, 2, :], ps[4][:, 0:4], ACT.Sqrt, bias=epsc[:, :], scale=1.0 / D)\
                    .then_inc(s_root, 1)

            def root(n, dim, dst):
                act.wait_ge(s_ssum, n + 1)
                nc.scalar.activation(dst[:, :], ps[4][:, :], ACT.Sqrt, bias=epsc[:, :], scale=1.0 / dim)\
                    .then_inc(s_root, 1)

            def residual(phase, tiles_per_m, gname, n, second=False):
                per = 4 * tiles_per_m

                def body(i):
                    for k in range(4):
                        for j in range(tiles_per_m):
                            ahead(T0[phase] + k * tiles_per_m + j, i, per)
                        m = i * 4 + k
                        act.wait_ge(s_acc, m + (SQ0[n] - 1))
                        act.wait_ge(s_ev, m + (M0[phase] + 1))
                        apart()
                        if gname:
                            nc.scalar.activation(at(XH, m), at(X, m), ACT.Copy, scale=vcol(gname, m))\
                                .then_inc(s_xh, 1)
                        nc.scalar.activation(SQ[:, k % 2, :], at(X, m), ACT.Square).then_inc(s_sq, 1)
                        if second:
                            act.wait_ge(s_acc2, m + 1)
                            apart()
                            nc.scalar.activation(AT[:, k % 2, :], at(X, m), ACT.Square, scale=vcol("final", m))\
                                .then_inc(s_sq2, 1)
                repeat(act, KD // 4, body, peel=KD // 4 if phase == PHASES[-1][0] else 0)

            def up(f, phase, bias):
                def body(i):
                    for j in range(2):
                        t, jj = T0[phase] + 2 * j, i * 2 + j
                        ahead(t, i, 4)
                        act.wait_ge(s_gc, jj + (FF * f + 1))
                        apart()
                        nc.scalar.activation(CG[:, :], CG[:, :], ACT.Silu, bias=vcol("conv_b", jj) if bias else 0.0)\
                            .then_inc(s_sg, 1)
                        ahead(t + 1, i, 4)
                        act.wait_ge(s_h, jj + (FF * f + 1))
                        apart()
                        nc.scalar.activation(at(HH, jj), CU[:, :], ACT.Copy).then_inc(s_hh, 1)
                repeat(act, FF // 2, body)

            act.wait_ge(s_in["vec"], 16)
            for m in range(KD):
                if m % 2 == 0:
                    act.wait_ge(s_in[f"x{m // 2}"], 16)
                nc.scalar.activation(XH[:, m, :], X[:, m, :], ACT.Copy, scale=vcol("a_mix", m)).then_inc(s_xh, 1)
                if m % 2 == 1 and m < 4:
                    hi(m // 2)
            for m in range(KD):
                if m >= 2:
                    act.wait_ge(s_acc, m - 1)
                nc.scalar.activation(SQ[:, m % 2, :], X[:, m, :], ACT.Square).then_inc(s_sq, 1)
            act.wait_ge(s_in["c"], 16)
            nc.scalar.activation(crow[:, :], crow[:, :], ACT.Silu).then_inc(s_cact, 1)
            act.wait_ge(s_set, 1)

            def a_ch(i):
                for k in range(4):
                    if isinstance(i, int) and k == 2:
                        root(N_A, D, rb)
                    ahead(T0["A_CH"] + k, i, 4)
            repeat(act, 4, a_ch, peel=1)

            def a_b(i):
                for k in range(4):
                    ahead(T0["A_B"] + k, i, 4)
                    act.wait_ge(s_y, i * 4 + (k + 1))
                    apart()
                    nc.scalar.activation(at(MH, i * 4 + k), CU[:, :], ACT.Copy).then_inc(s_yh, 1)
            repeat(act, 2, a_b)
            residual("A_OUT", 1, "ffn_norm0", N_F0)

            root(N_F0, D, rb)
            up(0, "UP0", False)
            residual("DN0", 3, "kv_in", N_KV)

            ahead(T0["DKV"])
            root(N_KV, D, rb)
            for m in range(KD):
                nc.scalar.activation(QXH[:, m, :], X[:, m, :], ACT.Copy, scale=vcol("b_mix", m)).then_inc(s_xh, 1)
                if m % 4 == 3:
                    ahead(T0["DKV"] + 1 + m // 4)
            for k in range(KKV):
                act.wait_ge(s_ev, M0["DKV"] + k + 1)
                square(N_LK, k, k, CL[:, k, :])
            ahead(T0["DQ"])
            root(N_LK, KV_LORA, rbl)
            ahead(T0["DQ"] + 1)
            for m in range(KKV):
                act.wait_ge(s_nb, NB_KV + m + 1)
                nc.scalar.activation(CLH[:, m, :], CL[:, m, :], ACT.Copy, scale=vcol("kv_norm", m)).then_inc(s_lh, 1)
            for k in range(KQ):
                if k > 1:
                    ahead(T0["DQ"] + k)
                act.wait_ge(s_ev, M0["DQ"] + k + 1)
                square(N_LQ, k, k, QL[:, k, :])
            ahead(T0["UKV"])
            root(N_LQ, Q_LORA, rbl)
            ahead(T0["UKV"] + 1)
            for m in range(KQ):
                act.wait_ge(s_nb, NB_Q + m + 1)
                nc.scalar.activation(XH[:, m, :], QL[:, m, :], ACT.Copy, scale=vcol("q_norm", m)).then_inc(s_lh, 1)
            for k in range(2, 4):
                ahead(T0["UKV"] + k)
            for k in range(6):
                ahead(T0["UQ"] + k)

            def head_hi(h):
                act.wait_ge(s_pv, 4 * h + 4)
                nc.scalar.activation(OH[:, h, :], ps[h % 2][:, :], ACT.Copy).then_inc(s_oh, 1)

            for a in range(BLOCKS_A + 1):
                if a < BLOCKS_A:
                    L = (a % 4 + 1) * P
                    if a >= 4:
                        act.wait_ge(s_pt, a - 3)
                    act.wait_ge(s_mx, a + 1)
                    nc.scalar.activation(PB[a % 4][:, 0:L], ps[SB[a % 4]][:, 0:L], ACT.Exp,
                                         bias=stat[:, 1, a:a + 1], scale=MLA_SCALE,
                                         accum_out=stat[:, 2, a:a + 1]).then_inc(s_p, 1)
                b = a - 1
                if b >= 0:
                    L = (b % 4 + 1) * P
                    act.wait_ge(s_rs, b + 1)
                    nc.scalar.activation(PB[b % 4][:, 0:L], PB[b % 4][:, 0:L], ACT.Copy,
                                         scale=stat[:, 3, b:b + 1]).then_inc(s_pn, 1)
                if a % 4 == 0 and a >= 8:
                    head_hi(a // 4 - 2)
            head_hi(HEADS - 1)
            residual("WO", 1, "ffn_norm1", N_F1)

            root(N_F1, D, rb)
            up(1, "UP1", False)
            residual("DN1", 3, None, N_FIN, second=True)
            act.dma_start(MK1[:, :, :], mask1_in).then_inc(s_in["mask"], 16)
            act.dma_start(MK2[:, :], mask2_in).then_inc(s_in["mask"], 16)
            act.dma_start(WS[:, :, :], wsp_in).then_inc(s_in["wsp"], 16)
            act.dma_start(posi[:, :], pos_in).then_inc(s_in["pos"], 16)
            act.wait_ge(s_ms, 1)
            nc.scalar.activation(nt[:, 2:4, :], nt[:, 0:2, :], ACT.Sqrt).then_inc(s_root, 1)

            def modulated(nb0, shift):
                for m in range(KD):
                    act.wait_ge(s_nb, nb0 + m + 1)
                    nc.scalar.activation(XH[:, m, :], AT[:, m % 2, :], ACT.Identity,
                                         bias=mod[:, shift * KD + m:shift * KD + m + 1]).then_inc(s_xh, 1)
            modulated(NB_M2, 0)
            for k in range(22):
                ahead(T0["IN2"] + k)
                if k == 6:
                    act.wait_ge(s_arg, 1)
                    nc.scalar.activation(sin_t[:, :], RA[:, :], ACT.Sin, scale=vcol("sin_sign", 0)).then_inc(s_trig, 1)
                    act.wait_ge(s_arg, 2)
                    nc.scalar.activation(cos_t[:, :], RB[:, :], ACT.Sin).then_inc(s_trig, 1)
                if k == 7:
                    act.wait_ge(s_auxev, AUX_2 + 4)
                    nc.scalar.activation(VV[:, :, :], VV[:, :, :], ACT.Gelu_apprx_tanh).then_inc(s_gelu, 1)
                    nc.scalar.activation(U[:, :, :], U[:, :, :], ACT.Gelu_apprx_tanh).then_inc(s_gelu, 1)
                if k == 9:
                    act.wait_ge(s_vs, 1)
                    nc.scalar.activation(vst[:, 1, :], vst[:, 0, :], ACT.Sqrt, bias=epsc[:, :], scale=1.0 / HD)\
                        .then_inc(s_vr, 1)
            for c in range(A_W // P):
                act.wait_ge(s_aux, AUX_YA + c + 1)
                nc.scalar.activation(XH[:, c, :], ps[5 + (AUX_YA + c) % 2][:, :], ACT.Copy).then_inc(s_y2h, 1)
            nc.scalar.preload_act_table_set("natural_log_exp_and_others")

            def weight(b):
                N = (b % 4 + 1) * P
                if b >= 2:
                    act.wait_ge(s_bo, b - 1)
                act.wait_ge(s_wa, b + 1)
                nc.scalar.activation(WT[b % 2][:, 0:N], ZB[b % 4][:, 0:N], ACT.Exp).then_inc(s_w, 1)

            def pair_hi(c):
                act.wait_ge(s_bo, 8 * c + 8)
                nc.scalar.activation(XH[:, 2 + c, :], ps[7 - c % 2][:, :], ACT.Copy).then_inc(s_y2h, 1)

            for b in range(BLOCKS_B + 3):
                if b < BLOCKS_B:
                    N = (b % 4 + 1) * P
                    if b >= 2:
                        act.wait_ge(s_sp, b - 1)
                    act.wait_ge(s_zb, b + 1)
                    E = EB[b % 2][:, 0:N]
                    ch.link(nc.scalar.activation(E, ZB[b % 4][:, 0:N], ACT.Abs))
                    ch.link(nc.scalar.activation(E, E, ACT.Exp, scale=-1.0))
                    nc.scalar.activation(E, E, ACT.Ln, bias=1.0).then_inc(s_ln, 1)
                if b >= 3:
                    weight(b - 3)
                if b % 8 == 4 and b > 8:
                    pair_hi(b // 8 - 1)
            pair_hi(B_HEADS // 2 - 1)

            def class_hi(r):
                act.wait_ge(s_co, 2 * r + 2)
                nc.scalar.activation(XH[:, 5:8, r::4], ps[6 + r % 2][:, 0:3 * P].rearrange("p (c q) -> p c q", c=3),
                                     ACT.Copy).then_inc(s_y2h, 1)

            for u in range(9):
                if u < 8:
                    if u >= 3:
                        act.wait_ge(s_ct, u - 2)
                    act.wait_ge(s_cm, u + 1)
                    nc.scalar.activation(PC[u % 3][:, :], ZC[u % 2][:, :], ACT.Exp, bias=cstat[:, 1, u:u + 1],
                                         accum_out=cstat[:, 2, u:u + 1]).then_inc(s_cp, 1)
                b = u - 1
                if b >= 0:
                    act.wait_ge(s_crs, b + 1)
                    nc.scalar.activation(PC[b % 3][:, :], PC[b % 3][:, :], ACT.Copy, scale=cstat[:, 3, b:b + 1])\
                        .then_inc(s_cn, 1)
                if u % 2 == 1 and u >= 5:
                    class_hi((u - 5) // 2)
            class_hi(2)
            class_hi(3)
            residual("OUT2", 1, None, N_F2)
            token_root(N_F2)
            modulated(NB_F2, 3)
            up(2, "UP2", True)
            residual("DN2", 3, None, N_END)
            token_root(N_END)

        @block.vector
        def _(dve):
            ch = Chain(dve, s_dve)
            v = nc.vector
            v.memset(epsc[:, :], EPS).then_inc(s_set, 1)

            def zero_pads():
                ch.step(v.memset(TG[:, 0:2], 0.0))
                ch.link(v.memset(TU[:, 0:2], 0.0))

            def add_square(n, m, k):
                dve.wait_ge(s_sq, m + (SQ0[n] + 1))
                if not (n == 0 and isinstance(m, int) and m == 0):
                    dve.wait_ge(s_acc, m + SQ0[n])
                v.tensor_tensor(acc[:, :], acc[:, :], SQ[:, k % 2, :], ALU.add).then_inc(s_acc, 1)

            def inverse(n, dst):
                dve.wait_ge(s_root, n + 1)
                v.reciprocal(dst[:, :], dst[:, :]).then_inc(s_rb, 1)
                dve.wait_ge(s_rb, n + 1)
                ch.link(v.memset(acc[:, :], 0.0))

            def lo_half(dst_h, dst_l, src, g, done_h, sem_l):
                dve.wait_ge(*done_h)
                v.scalar_tensor_tensor(dst_l, src, g, f32(dst_h), ALU.mult, ALU.subtract).then_inc(sem_l, 1)

            def product(M, i=0, per=0):
                dve.wait_ge(s_pe, i * per + DONE_M[M])

            def residual(phase, tiles_per_m, e, gname, n, gate=None, beside=None, second=False):
                per = 4 * tiles_per_m

                def body(i):
                    for k in range(4):
                        m, M = i * 4 + k, M0[phase] + k
                        product(M, i, per)
                        bank = ps[M % 4][:, :]
                        if gate is None:
                            ins = v.tensor_tensor(at(X, m), bank, at(X, m), ALU.add)
                        else:
                            g = gm[:, gate, m:m + 1] if isinstance(m, int) else \
                                gm[:, gate, :][:, bass.ds(m, 1)]
                            ins = v.scalar_tensor_tensor(at(X, m), bank, g, at(X, m), ALU.mult, ALU.add)
                        ins.then_inc(s_ev, 1)
                        if gname:
                            lo_half(at(XH, m), at(XL, m), at(X, m), vcol(gname, m), (s_xh, m + (KD * e + 1)), s_xl)
                        add_square(n, m, k)
                        if second:
                            dve.wait_ge(s_sq2, m + 1)
                            dve.wait_ge(s_acc2, m + 2)
                            v.tensor_tensor(rbl[:, :], rbl[:, :], AT[:, k % 2, :], ALU.add).then_inc(s_acc2, 1)
                        if beside:
                            beside(i, k)
                repeat(dve, KD // 4, body)

            def conv(dst, src, w, j, chunks, last):
                ch.link(v.tensor_scalar(dst, src[:, 2:S + 2], vcol(w, j + 2 * chunks), None, ALU.mult))
                ch.link(v.scalar_tensor_tensor(dst, src[:, 1:S + 1], vcol(w, j + chunks), dst, ALU.mult, ALU.add))
                last(v.scalar_tensor_tensor(dst, src[:, 0:S], vcol(w, j), dst, ALU.mult, ALU.add))

            def up(f, phase, deferred):
                w = f"ffn_conv{f}"
                zero_pads()

                def body(i):
                    for j in range(2):
                        jj = i * 2 + j
                        for half, (pad, dst) in enumerate(((TG, CG), (TU, CU))):
                            M = M0[phase] + 2 * j + half
                            product(M, i, 4)
                            if deferred:
                                ins = v.tensor_tensor(pad[:, 2:S + 2], ps[M % 4][:, :], rb[:, :], ALU.mult)
                            else:
                                ins = v.tensor_copy(pad[:, 2:S + 2], ps[M % 4][:, :])
                            ins.then_inc(s_ev, 1)
                            dve.wait_ge(s_ev, i * 4 + (M + 1))
                            if half == 0:
                                conv(dst[:, :], pad, w, jj, 2 * FF, lambda ins: ins.then_inc(s_gc, 1))
                            else:
                                conv(dst[:, :], pad, w, jj + FF, 2 * FF, ch.link)
                        dve.wait_ge(s_sg, jj + (FF * f + 1))
                        if deferred:
                            ins = v.tensor_tensor(CU[:, :], CU[:, :], CG[:, :], ALU.mult)
                        else:
                            ins = v.scalar_tensor_tensor(CU[:, :], CU[:, :], vcol("conv_b", jj + FF), CG[:, :],
                                                         ALU.add, ALU.mult)
                        ins.then_inc(s_h, 1)
                        dve.wait_ge(s_hh, jj + (FF * f + 1))
                        v.tensor_tensor(at(HL, jj), CU[:, :], f32(at(HH, jj)), ALU.subtract).then_inc(s_hl, 1)
                repeat(dve, FF // 2, body, ch, 10)

            ch.link(v.memset(acc[:, :], 0.0))
            zero_pads()
            for m in range(KD):
                lo_half(XH[:, m, :], XL[:, m, :], X[:, m, :], vcol("a_mix", m), (s_xh, m + 1), s_xl)
            for m in range(KD):
                add_square(N_A, m, m)
            inverse(N_A, rb)

            def adaln(i, q):
                a = i * 6 + q
                dve.wait_ge(s_ada_in[q], i * 16 + 16)
                dst = mod[:, a:a + 1] if isinstance(a, int) else mod[:, bass.ds(a, 1)]
                w = ada[:, q, :]
                v.scalar_tensor_tensor(w, w, 1.0, crow[:, :], ALU.mult, ALU.mult, accum_out=dst).then_inc(s_ada, 1)

            dve.wait_ge(s_cact, 1)

            def a_ch(i):
                for k in range(2):
                    for half, dst in enumerate((CG, CU)):
                        M = M0["A_CH"] + 2 * k + half
                        product(M, i, 4)
                        v.tensor_tensor(dst[:, :], ps[M % 4][:, :], rb[:, :], ALU.mult).then_inc(s_ev, 1)
                    dve.wait_ge(s_ev, i * 4 + (M + 1))
                    ch.link(v.tensor_tensor(TG[:, 2:S + 2], CG[:, :], CU[:, :], ALU.mult))
                    conv(at(CV, i * 2 + k), TG, "a_conv", i * 2 + k, KD, ch.link)
                    for q in range(3 * k, 3 * k + 3):
                        adaln(i, q)
            repeat(dve, 4, a_ch, ch, 8)

            def a_b(i):
                for k in range(4):
                    j, M = i * 4 + k, M0["A_B"] + k
                    product(M, i, 4)
                    v.tensor_tensor(CG[:, :], ps[M % 4][:, :], rb[:, :], ALU.mult).then_inc(s_ev, 1)
                    dve.wait_ge(s_ev, i * 4 + (M + 1))
                    v.tensor_tensor(CU[:, :], CG[:, :], at(CV, j), ALU.mult).then_inc(s_y, 1)
                    dve.wait_ge(s_yh, j + 1)
                    v.tensor_tensor(at(ML, j), CU[:, :], f32(at(MH, j)), ALU.subtract).then_inc(s_yl, 1)
                    for q in ADA_AT[k]:
                        adaln(i + 4, q)
            repeat(dve, 2, a_b)

            def ada_beside(i, k):
                for q in ADA_AT[k]:
                    adaln(i + 6, q)
            residual("A_OUT", 1, E_F0, "ffn_norm0", N_F0, beside=ada_beside)
            dve.wait_ge(s_ada, 6 * KD)
            b0 = V["b_ada"][0]
            ch.link(v.tensor_tensor(mod[:, :], mod[:, :], vec[:, b0:b0 + 6 * KD], ALU.add))
            for row, (part, g) in enumerate(((1, "g_mix"), (4, "g_ffn"))):
                ch.step(v.scalar_tensor_tensor(gm[:, row, :], mod[:, part * KD:(part + 1) * KD], 1.0,
                                               vec[:, V[g][0]:V[g][0] + KD], ALU.add, ALU.mult))
            for row, part in ((2, 2), (3, 5)):
                ch.link(v.tensor_scalar(gm[:, row, :], mod[:, part * KD:(part + 1) * KD], 1.0, None, ALU.add))
            ch.link(v.tensor_tensor(gm[:, 0, :], gm[:, 0, :], vec[:, V["final"][0]:V["final"][0] + KD], ALU.mult))

            inverse(N_F0, rb)
            up(0, "UP0", True)
            residual("DN0", 3, E_KV, "kv_in", N_KV)

            inverse(N_KV, rb)

            def to_aux(aux, M, scale=None, by=None):
                product(M)
                if aux >= 2:
                    dve.wait_ge(s_aux, aux - 1)
                if by is not None:
                    ins = v.tensor_tensor(AT[:, aux % 2, :], ps[M % 4][:, :], by[:, :], ALU.mult)
                elif scale is not None:
                    ins = v.tensor_scalar(AT[:, aux % 2, :], ps[M % 4][:, :], scale, None, ALU.mult)
                else:
                    ins = v.tensor_copy(AT[:, aux % 2, :], ps[M % 4][:, :])
                ins.then_inc(s_ev, 1)

            ropes = [0]

            def rope(aux, dst):
                if ropes[0]:
                    dve.wait_ge(s_qk, ropes[0])
                ropes[0] += 1
                dve.wait_ge(s_aux, aux + 1)
                v.tensor_tensor(RB[:, :], ps[5 + aux % 2][:, :], sin_t[:, :], ALU.mult).then_inc(s_auxev, 1)
                ch.link(v.tensor_tensor(RA[:, :], AT[:, aux % 2, :], cos_t[:, :], ALU.mult))
                dve.wait_ge(s_auxev, aux + 1)
                v.tensor_tensor(dst, RA[:, :], RB[:, :], ALU.add).then_inc(s_qk, 1)

            def take(aux, dst, src=None):
                dve.wait_ge(s_aux, aux + 1)
                v.tensor_copy(dst, ps[5 + aux % 2][:, :] if src is None else src(ps[5 + aux % 2]))\
                    .then_inc(s_auxev, 1)

            for m in range(KD):
                lo_half(QXH[:, m, :], QXL[:, m, :], X[:, m, :], vcol("b_mix", m), (s_xh, KD * E_Q + m + 1), s_xl)
            for k in range(KKV):
                product(M0["DKV"] + k)
                v.tensor_tensor(CL[:, k, :], ps[(M0["DKV"] + k) % 4][:, :], rb[:, :], ALU.mult).then_inc(s_ev, 1)
                add_square(N_LK, k, k)
            to_aux(AUX_KR, M0["DKV"] + KKV, by=rb)
            inverse(N_LK, rbl)
            for m in range(KKV):
                v.tensor_tensor(CL[:, m, :], CL[:, m, :], rbl[:, :], ALU.mult).then_inc(s_nb, 1)
            for m in range(KKV):
                lo_half(CLH[:, m, :], CLL[:, m, :], CL[:, m, :], vcol("kv_norm", m), (s_lh, m + 1), s_ll)
            dve.wait_ge(s_in["rope"], 32)
            rope(AUX_KR, KR[:, :])
            for k in range(KQ):
                product(M0["DQ"] + k)
                v.tensor_tensor(QL[:, k, :], ps[(M0["DQ"] + k) % 4][:, :], rb[:, :], ALU.mult).then_inc(s_ev, 1)
                add_square(N_LQ, k, k)
            for t in range(HEADS // 2):
                for g in range(2):
                    h, M = 2 * t + g, M0["UKV"] + 4 * t + 2 * g
                    product(M)
                    v.tensor_copy(KN[:, h, :], ps[M % 4][:, :]).then_inc(s_ev, 1)
                    if t > 0:
                        take(AUX_V + h - 2, VT[:, h - 2, :])
                    to_aux(AUX_V + h, M + 1)
                if t == 0:
                    inverse(N_LQ, rbl)
                    for m in range(KQ):
                        v.tensor_tensor(QL[:, m, :], QL[:, m, :], rbl[:, :], ALU.mult).then_inc(s_nb, 1)
                if t == 1:
                    for m in range(KQ):
                        lo_half(XH[:, m, :], XL[:, m, :], QL[:, m, :], vcol("q_norm", m), (s_lh, KKV + m + 1), s_ll)
            for p in range(HEADS // 2):
                to_aux(AUX_QR + p, M0["UQ"] + p)
                if p < 2:
                    take(AUX_V + HEADS - 2 + p, VT[:, HEADS - 2 + p, :])
                if p >= 1:
                    rope(AUX_QR + p - 1, QR[:, p - 1, :])
            for h in range(HEADS):
                M = M0["UQ"] + HEADS // 2 + h
                product(M)
                v.tensor_copy(QN[:, h, :], ps[M % 4][:, :]).then_inc(s_ev, 1)
                if h == 0:
                    rope(AUX_QR + HEADS // 2 - 1, QR[:, HEADS // 2 - 1, :])

            dve.wait_ge(s_in["const"], 16)
            v.tensor_copy(mask16[:, 0, :], cc("ident")).then_inc(s_m16, 1)
            v.tensor_copy(mask16[:, 1, :], cc("causal_neg")).then_inc(s_m16, 1)

            def head_lo(h):
                dve.wait_ge(s_oh, h + 1)
                v.tensor_tensor(OL[:, h, :], ps[h % 2][:, :], f32(OH[:, h, :]), ALU.subtract).then_inc(s_ol, 1)

            for a in range(BLOCKS_A + 3):
                if a < BLOCKS_A:
                    L = (a % 4 + 1) * P
                    dve.wait_ge(s_s, a + 1)
                    ch.link(v.reduce_max(stat[:, 0, a:a + 1], ps[SB[a % 4]][:, 0:L], AX_X))
                    v.tensor_scalar(stat[:, 1, a:a + 1], stat[:, 0, a:a + 1], -MLA_SCALE, None, ALU.mult)\
                        .then_inc(s_mx, 1)
                b = a - 3
                if 0 <= b:
                    L = (b % 4 + 1) * P
                    dve.wait_ge(s_pt, b + 1)
                    if b >= 2:
                        dve.wait_ge(s_pv, b - 1)
                    v.tensor_copy(AT[:, b % 2, 0:L], ps[6 + b % 2][:, 0:L]).then_inc(s_ptc, 1)
                b = a - 1
                if 0 <= b < BLOCKS_A:
                    dve.wait_ge(s_p, b + 1)
                    v.reciprocal(stat[:, 3, b:b + 1], stat[:, 2, b:b + 1]).then_inc(s_rs, 1)
                if a % 4 == 1 and a >= 9:
                    head_lo(a // 4 - 2)
            head_lo(HEADS - 1)
            residual("WO", 1, E_F1, "ffn_norm1", N_F1)

            inverse(N_F1, rb)
            up(1, "UP1", True)
            for half in range(2):
                v.memset(rbl[:, half * (S // 2):(half + 1) * (S // 2)], 0.0).then_inc(s_acc2, 1)
            residual("DN1", 3, None, None, N_FIN, second=True)

            def spread(dst, src):
                v.tensor_tensor(dst[:, :].rearrange("p (n q) -> p n q", n=4),
                                cc("ident").unsqueeze(1).to_broadcast([P, 4, P]),
                                src.unsqueeze(2).to_broadcast([P, 4, P]), ALU.mult).then_inc(s_dg, 1)

            def token_inverse(n):
                dve.wait_ge(s_root, n + 1)
                ch.link(v.reciprocal(nt[:, 4, :], nt[:, 2, :]))
                spread(RA, nt[:, 4, :])

            dve.wait_ge(s_ssum, N_FIN + 2)
            ch.link(v.tensor_scalar(nt[:, 0, :], ps[4][:, 0:4], 1.0 / D, EPS, ALU.mult, ALU.add))
            ch.link(v.reciprocal(nt[:, 0, :], nt[:, 0, :]))
            ch.link(v.tensor_tensor(nt[:, 1, :], ps[4][:, 4:8], nt[:, 0, :], ALU.mult))
            v.tensor_scalar(nt[:, 1, :], nt[:, 1, :], 1.0 / D, EPS, ALU.mult, ALU.add).then_inc(s_ms, 1)
            dve.wait_ge(s_root, N_FIN + 1)
            ch.link(v.reciprocal(nt[:, 4, :], nt[:, 3, :]))
            ch.link(v.tensor_tensor(nt[:, 4, :], nt[:, 4, :], nt[:, 2, :], ALU.mult))
            spread(RA, nt[:, 4, :])
            spread(RB, nt[:, 2, :])
            dve.wait_ge(s_bc, 1)

            def modulated(e, nb0, row, shift, r):
                for m in range(KD + 1):
                    if m < KD:
                        if m >= 2:
                            dve.wait_ge(s_xl, KD * e + m - 1)
                        v.scalar_tensor_tensor(AT[:, m % 2, :], X[:, m, :], gm[:, row, m:m + 1], r[:, :],
                                               ALU.mult, ALU.mult).then_inc(s_nb, 1)
                    if m >= 1:
                        k = m - 1
                        dve.wait_ge(s_xh, KD * e + k + 1)
                        v.scalar_tensor_tensor(XL[:, k, :], AT[:, k % 2, :],
                                               mod[:, shift * KD + k:shift * KD + k + 1], f32(XH[:, k, :]),
                                               ALU.add, ALU.subtract).then_inc(s_xl, 1)
            modulated(E_M2, NB_M2, 0, 0, ps[4])
            dve.wait_ge(s_bc, 2)

            def first_result(m):
                v.scalar_tensor_tensor(X[:, m, :], X[:, m, :], vcol("final", m), ps[7][:, :], ALU.mult, ALU.mult)\
                    .then_inc(s_x, 1)

            two_pi = 2.0 * np.pi
            part1 = 6.28125
            part2 = 507.0 / 2 ** 18
            part3 = two_pi - part1 - part2
            magic = 1.5 * 2 ** 23
            limit = 3.1415925

            def positions():
                dve.wait_ge(s_in["pos"], 16)
                ch.link(v.tensor_copy(rbl[:, :], posi[:, :]))
                ch.link(v.tensor_scalar(rbl[:, :], rbl[:, :], vcol("inv_freq", 0), None, ALU.mult))

            def angle(dst, quarter):
                ch.link(v.tensor_scalar(acc[:, :], rbl[:, :], 1.0 / two_pi, quarter, ALU.mult, ALU.add))
                ch.link(v.tensor_scalar(acc[:, :], acc[:, :], magic, None, ALU.add))
                ch.link(v.tensor_scalar(acc[:, :], acc[:, :], -magic, None, ALU.add))
                ch.link(v.scalar_tensor_tensor(dst[:, :], acc[:, :], -part1, rbl[:, :], ALU.mult, ALU.add))
                ch.link(v.scalar_tensor_tensor(dst[:, :], acc[:, :], -part2, dst[:, :], ALU.mult, ALU.add))
                ch.link(v.scalar_tensor_tensor(dst[:, :], acc[:, :], -part3, dst[:, :], ALU.mult, ALU.add))
                ch.link(v.tensor_scalar(dst[:, :], dst[:, :], quarter * two_pi, limit, ALU.add, ALU.min))
                v.tensor_scalar(dst[:, :], dst[:, :], -limit, None, ALU.max).then_inc(s_arg, 1)

            def in_tile(k):
                M, aux = M0["IN2"] + k, AUX_2 + k
                if k < N_TOK:
                    to_aux(aux, M)
                elif k < N_TOK + 3:
                    to_aux(aux, M, scale=QK_SCALE)
                elif k < N_TOK + 6:
                    to_aux(aux, M)
                else:
                    product(M)
                    v.tensor_scalar(FT[:, k - N_TOK, :], ps[M % 4][:, :], QK_SCALE if k < N_TOK + 9 else 1.0, None,
                                    ALU.mult).then_inc(s_ev, 1)

            def blocks(bank):
                return bank[:, :].rearrange("p (n f) -> p n f", n=4)

            def in_take(k):
                aux = AUX_2 + k
                if k < 2:
                    take(aux, VV[:, :, k * P:(k + 1) * P], blocks)
                elif k < 4:
                    take(aux, U[:, :, (k - 2) * P:(k - 1) * P], blocks)
                elif k == 4:
                    take(aux, CV0[:, :, :], blocks)
                elif k < 7:
                    take(aux, CV12[:, :, (k - 5) * P:(k - 4) * P], blocks)
                elif k < 10:
                    take(aux, BV[:, :, (k - 7) * P:(k - 6) * P], blocks)
                elif k < 16:
                    if k == 10:
                        dve.wait_ge(s_trig, 2)
                    rope(aux, FT[:, k - N_TOK, :])

            def by_group(t):
                return t.rearrange("p n (g c) -> p (n g) c", g=GROUPS)

            def v_squares():
                dve.wait_ge(s_gelu, 1)
                ch.link(v.tensor_tensor(VN[:, :, :], VV[:, :, :], VV[:, :, :], ALU.mult))
                v.reduce_sum(vst[:, 0, :], by_group(VN[:, :, :]), AX_X).then_inc(s_vs, 1)

            def v_norm():
                dve.wait_ge(s_vr, 1)
                ch.link(v.reciprocal(vst[:, 2, :], vst[:, 1, :]))
                ch.link(v.tensor_tensor(by_group(VN[:, :, :]), by_group(VV[:, :, :]),
                                        vst[:, 2, :].unsqueeze(2).to_broadcast([P, 4 * GROUPS, HD]), ALU.mult))
                dve.wait_ge(s_in["gsgu"], 16)
                v.tensor_tensor(VN[:, :, :], VN[:, :, :], gsgu[:, :].unsqueeze(1).to_broadcast([P, 4, A_W]),
                                ALU.mult).then_inc(s_vn, 1)

            def gating():
                dve.wait_ge(s_mixed, 1)
                dve.wait_ge(s_gelu, 2)
                for g in range(GROUPS):
                    last = v.scalar_tensor_tensor(
                        YA[:, :, g * HD:(g + 1) * HD],
                        MIXED[g // 2][:, (g % 2) * 256:(g % 2) * 256 + 256].rearrange("p (n c) -> p n c", n=4),
                        vcol("b_sp", g), U[:, :, g * HD:(g + 1) * HD], ALU.add, ALU.mult)
                last.then_inc(s_ya, 1)

            for k in range(22):
                in_tile(k)
                if k >= 1:
                    in_take(k - 1)
                if k < KD:
                    first_result(k)
                if k == 3:
                    positions()
                    angle(RA, 0.0)
                if k == 5:
                    angle(RB, 0.25)
                    ch.link(v.memset(acc[:, :], 0.0))
                if k == 8:
                    v_squares()
                if k == 10:
                    v_norm()
                if k == 14:
                    gating()
            for c in range(A_W // P):
                dve.wait_ge(s_y2h, c + 1)
                v.tensor_tensor(XL[:, c, :], ps[5 + (AUX_YA + c) % 2][:, :], f32(XH[:, c, :]), ALU.subtract)\
                    .then_inc(s_y2l, 1)

            def logits(b):
                N = (b % 4 + 1) * P
                dve.wait_ge(s_z, b + 1)
                if b >= 4:
                    dve.wait_ge(s_w, b - 3)
                v.tensor_copy(ZB[b % 4][:, 0:N], ps[b % 2][:, 0:N]).then_inc(s_zb, 1)

            def softplus(b):
                h, kb, N = b // 4, 3 - b % 4, (b % 4 + 1) * P
                sp = SP[:, h % 2 * 4 + kb, :]
                dve.wait_ge(s_ln, b + 1)
                if h >= 2:
                    dve.wait_ge(s_r, 4 * (h - 1))
                ch.link(v.scalar_tensor_tensor(sp[:, kb * P:S], ZB[b % 4][:, 0:N], 0.0, EB[b % 2][:, 0:N],
                                               ALU.max, ALU.add))
                v.tensor_tensor(sp[:, kb * P:kb * P + P], sp[:, kb * P:kb * P + P], cc("strict"), ALU.mult)\
                    .then_inc(s_sp, 1)

            def exponent(b):
                N = (b % 4 + 1) * P
                Z = ZB[b % 4]
                dve.wait_ge(s_r, b + 1)
                ch.link(v.tensor_tensor(Z[:, 0:N], Z[:, 0:N], ps[2 + b % 2][:, 0:N], ALU.subtract))
                v.tensor_tensor(Z[:, 0:P], Z[:, 0:P], cc("strict_neg"), ALU.add).then_inc(s_wa, 1)

            def pair_lo(c):
                dve.wait_ge(s_y2h, 2 + c + 1)
                v.tensor_tensor(XL[:, 2 + c, :], ps[7 - c % 2][:, :], f32(XH[:, 2 + c, :]), ALU.subtract)\
                    .then_inc(s_y2l, 1)

            for b in range(BLOCKS_B + 3):
                if b < BLOCKS_B:
                    logits(b)
                if 0 <= b - 1 < BLOCKS_B:
                    softplus(b - 1)
                if b >= 3:
                    exponent(b - 3)
                if b % 8 == 5 and b > 8:
                    pair_lo(b // 8 - 1)
            pair_lo(B_HEADS // 2 - 1)

            dve.wait_ge(s_in["mask"], 32)

            def class_lo(r):
                dve.wait_ge(s_y2h, 5 + r + 1)
                v.tensor_tensor(XL[:, 5:8, r::4], ps[6 + r % 2][:, 0:3 * P].rearrange("p (c q) -> p c q", c=3),
                                f32(XH[:, 5:8, r::4]), ALU.subtract).then_inc(s_y2l, 1)

            for u in range(8 + 2):
                if u < 8:
                    r = u // 2
                    dve.wait_ge(s_cz, u + 1)
                    if u >= 2:
                        dve.wait_ge(s_cp, u - 1)
                    ch.step(v.tensor_tensor(ZC[u % 2][:, 0:S], ps[u % 2][:, :], MK1[:, r, :], ALU.add))
                    ch.link(v.tensor_tensor(ZC[u % 2][:, S:S + 2 * P], ps[2 + u % 2][:, 0:2 * P], MK2[:, :], ALU.add))
                    ch.link(v.reduce_max(cstat[:, 0, u:u + 1], ZC[u % 2][:, :], AX_X))
                    v.tensor_scalar(cstat[:, 1, u:u + 1], cstat[:, 0, u:u + 1], -1.0, None, ALU.mult)\
                        .then_inc(s_cm, 1)
                b = u - 1
                if 0 <= b < 8:
                    dve.wait_ge(s_cp, b + 1)
                    v.reciprocal(cstat[:, 3, b:b + 1], cstat[:, 2, b:b + 1]).then_inc(s_crs, 1)
                b = u - 2
                if 0 <= b:
                    dve.wait_ge(s_ct, b + 1)
                    if b >= 2:
                        dve.wait_ge(s_co, b - 1)
                    ch.step(v.tensor_copy(PCT[b % 2][:, 0:S], ps[4][:, :]))
                    v.tensor_copy(PCT[b % 2][:, S:S + 2 * P], ps[5][:, 0:2 * P]).then_inc(s_cc, 1)
                if u % 2 == 0 and u >= 6:
                    class_lo((u - 6) // 2)
            class_lo(2)
            class_lo(3)
            residual("OUT2", 1, None, None, N_F2, gate=2)

            token_inverse(N_F2)
            ch.link(v.memset(acc[:, :], 0.0))
            dve.wait_ge(s_bc, 3)
            modulated(E_F2, NB_F2, 1, 3, ps[4])
            up(2, "UP2", False)
            residual("DN2", 3, None, None, N_END, gate=3)
            token_inverse(N_END)
            dve.wait_ge(s_bc, 4)
            for m in range(KD):
                v.scalar_tensor_tensor(X[:, m, :], X[:, m, :], vcol("g_final", m), ps[4][:, :], ALU.mult, ALU.mult)\
                    .then_inc(s_fin, 1)

        @block.tensor
        def _(pe):
            mm = nc.tensor.matmul

            def tile_ready(t, i=0, per=0):
                pe.wait_ge(s_lo, i * per + (t + 1))

            def bank_free(M, i=0, per=0):
                if M >= 4:
                    pe.wait_ge(s_ev, i * per + (M - 3))
                elif not isinstance(i, int) or i > 0:
                    pe.wait_ge(s_ev, i * per + (M - 3))

            def dot(bank, t, blk, xh, xl, first, last):
                h = WH[t % SPL][:, blk * P:(blk + 1) * P]
                lo = WL[t % SPL][:, blk * P:(blk + 1) * P]
                mm(bank, h, xh, start=first, stop=False)
                mm(bank, h, xl, start=False, stop=False)
                return mm(bank, lo, xh, start=False, stop=last)

            def wide(t, M, i=0, per=0, before=None, src=(XH, XL)):
                tile_ready(t, i, per)
                bank_free(M, i, per)
                for k in range(KD):
                    if before:
                        before(k)
                    last = dot(ps[M % 4][:, :], t, k, src[0][:, k, :], src[1][:, k, :], k == 0, k == KD - 1)
                last.then_inc(s_pe, 1)

            def inputs(e):
                return lambda k: pe.wait_ge(s_xl, KD * e + k + 1)

            def sum_squares(n):
                pe.wait_ge(s_acc, SQ0[n + 1])
                mm(ps[4][:, :], cc("ones"), acc[:, :], start=True, stop=True).then_inc(s_ssum, 1)

            def token_squares(src, col):
                for n in range(4):
                    last = mm(ps[4][:, col + n:col + n + 1], src[:, n * P:(n + 1) * P], cc("ones")[:, 0:1],
                              start=True, stop=True)
                last.then_inc(s_ssum, 1)

            def spread(count, bank, src):
                pe.wait_ge(s_dg, count)
                mm(bank[:, :], cc("ones"), src[:, :], start=True, stop=True).then_inc(s_bc, 1)

            def a_ch(i):
                start = isinstance(i, int)
                for k in range(4):
                    wide(T0["A_CH"] + k, M0["A_CH"] + k, i, 4, inputs(E_A) if start and k == 0 else None)
                    if start and k == 2:
                        pe.wait_ge(s_in["const"], 16)
                        sum_squares(N_A)
            repeat(pe, 4, a_ch, peel=1)

            def a_b(i):
                for k in range(4):
                    wide(T0["A_B"] + k, M0["A_B"] + k, i, 4)
            repeat(pe, 2, a_b)

            def out_product(phase, src, ready):
                def body(i):
                    for k in range(4):
                        wide(T0[phase] + k, M0[phase] + k, i, 4, ready if k == 0 else None, src)
                repeat(pe, KD // 4, body)

            out_product("A_OUT", (MH, ML), lambda k: pe.wait_ge(s_yl, k + 1))

            def up(f, phase, e, n):
                def body(i):
                    start = isinstance(i, int)
                    for k in range(4):
                        wide(T0[phase] + k, M0[phase] + k, i, 4, inputs(e) if start and k == 0 else None)
                        if start and k == 0 and n is not None:
                            sum_squares(n)
                repeat(pe, FF // 2, body, peel=1)

            def down(f, phase):
                def body(i):
                    for k in range(4):
                        M = M0[phase] + k
                        bank_free(M, i, 4)
                        for j in range(3):
                            t = T0[phase] + 3 * k + j
                            tile_ready(t, i, 12)
                            n = min(BLK, FF - BLK * j)
                            pe.wait_ge(s_hl, FF * f + BLK * j + n)
                            for b in range(n):
                                c = BLK * j + b
                                last = dot(ps[M % 4][:, :], t, b, HH[:, c, :], HL[:, c, :], c == 0, c == FF - 1)
                            last.then_inc(s_pe, 1)
                repeat(pe, KD // 4, body)

            up(0, "UP0", E_F0, N_F0)
            down(0, "DN0")

            def swap(aux, M):
                pe.wait_ge(s_ev, M + 1)
                if aux >= 2:
                    pe.wait_ge(s_auxev, aux - 1)
                mm(ps[5 + aux % 2][:, :], cc("swap"), AT[:, aux % 2, :], start=True, stop=True).then_inc(s_aux, 1)

            def turn(aux, M, strided=False):
                pe.wait_ge(s_ev, M + 1)
                if aux >= 2:
                    pe.wait_ge(s_auxev, aux - 1)
                for n in range(4):
                    src = AT[:, aux % 2, n::4] if strided else AT[:, aux % 2, n * P:(n + 1) * P]
                    last = nc.tensor.transpose(ps[5 + aux % 2][:, n * P:(n + 1) * P], src, cc("ident"))
                last.then_inc(s_aux, 1)

            for k in range(3):
                wide(T0["DKV"] + k, M0["DKV"] + k, before=inputs(E_KV) if k == 0 else None)
                if k == 0:
                    sum_squares(N_KV)
            for k in range(KQ):
                wide(T0["DQ"] + k, M0["DQ"] + k, before=inputs(E_Q) if k == 0 else None, src=(QXH, QXL))
                if k == 0:
                    sum_squares(N_LK)
                    swap(AUX_KR, M0["DKV"] + 2)
            for t in range(HEADS // 2):
                tile_ready(T0["UKV"] + t)
                for j in range(4):
                    M = M0["UKV"] + 4 * t + j
                    bank_free(M)
                    for k in range(KKV):
                        if t == 0 and j == 0:
                            pe.wait_ge(s_ll, k + 1)
                        last = dot(ps[M % 4][:, :], T0["UKV"] + t, 2 * j + k, CLH[:, k, :], CLL[:, k, :],
                                   k == 0, k == KKV - 1)
                    last.then_inc(s_pe, 1)
                    if t == 0 and j == 1:
                        sum_squares(N_LQ)
                    if t > 0 and j % 2 == 0:
                        h = 2 * (t - 1) + j // 2
                        turn(AUX_V + h, M0["UKV"] + 2 * h + 1)
            for t in range(6):
                tile_ready(T0["UQ"] + t)
                for j in range(2):
                    M = M0["UQ"] + 2 * t + j
                    bank_free(M)
                    for k in range(KQ):
                        if t == 0 and j == 0:
                            pe.wait_ge(s_ll, KKV + k + 1)
                        last = dot(ps[M % 4][:, :], T0["UQ"] + t, KQ * j + k, XH[:, k, :], XL[:, k, :],
                                   k == 0, k == KQ - 1)
                    last.then_inc(s_pe, 1)
                    if t == 0:
                        h = HEADS - 2 + j
                        turn(AUX_V + h, M0["UKV"] + 2 * h + 1)
                    p = 2 * t + j - 1
                    if 0 <= p < HEADS // 2:
                        swap(AUX_QR + p, M0["UQ"] + p)

            pe.wait_ge(s_qk, 1 + HEADS // 2)
            pe.wait_ge(s_ev, M0["WO"])
            pe.wait_ge(s_m16, 2)
            for a in range(BLOCKS_A + 4):
                if a < BLOCKS_A:
                    h, qb = a // 4, a % 4
                    L, half = (qb + 1) * P, h % 2 * HD
                    bank = ps[SB[a % 4]]
                    if a >= 4:
                        pe.wait_ge(s_p, a - 3)
                    mm(bank[:, 0:L], QN[:, h, qb * P:L], KN[:, h, 0:L], start=True, stop=False)
                    mm(bank[:, L - P:L], mask16[:, 0, :], mask16[:, 1, :], start=False, stop=False,
                       skip_group_check=True)
                    mm(bank[:, 0:L], QR[half:half + HD, h // 2, qb * P:L], KR[half:half + HD, 0:L],
                       start=False, stop=True).then_inc(s_s, 1)
                b = a - 2
                if 0 <= b < BLOCKS_A:
                    pe.wait_ge(s_pn, b + 1)
                    if b >= 2:
                        pe.wait_ge(s_ptc, b - 1)
                    for kb in range(b % 4 + 1):
                        last = nc.tensor.transpose(ps[6 + b % 2][:, kb * P:(kb + 1) * P],
                                                   PB[b % 4][:, kb * P:(kb + 1) * P], cc("ident"))
                    last.then_inc(s_pt, 1)
                b = a - 4
                if 0 <= b:
                    h, qb = b // 4, b % 4
                    pe.wait_ge(s_ptc, b + 1)
                    if qb == 0 and h >= 2:
                        pe.wait_ge(s_ol, h - 1)
                    for kb in range(qb + 1):
                        last = mm(ps[h % 2][:, qb * P:(qb + 1) * P], VT[:, h, kb * P:(kb + 1) * P],
                                  AT[:, b % 2, kb * P:(kb + 1) * P], start=kb == 0, stop=kb == qb)
                    last.then_inc(s_pv, 1)
            pe.wait_ge(s_ol, HEADS)
            out_product("WO", (OH, OL), lambda k: None)
            up(1, "UP1", E_F1, N_F1)
            down(1, "DN1")

            pe.wait_ge(s_acc, SQ0[N_FIN + 1])
            token_squares(acc, 0)
            pe.wait_ge(s_acc2, KD + 2)
            token_squares(rbl, 4)
            spread(1, ps[4], RA)
            spread(2, ps[7], RB)
            n_in = 22

            def second_trip(k):
                aux, M = AUX_2 + k, M0["IN2"] + k
                if k < N_TOK:
                    turn(aux, M, strided=k in (5, 6))
                elif k < N_TOK + 6:
                    swap(aux, M)
            for k in range(n_in):
                wide(T0["IN2"] + k, M0["IN2"] + k, before=inputs(E_M2) if k == 0 else None)
                if k >= 1:
                    second_trip(k - 1)
                if k == 12:
                    pe.wait_ge(s_ws, 1)
                    pe.wait_ge(s_vn, 1)
                    for g in range(GROUPS):
                        last = mm(MIXED[g // 2][:, (g % 2) * 256:(g % 2) * 256 + 256]
                                  .rearrange("p (n c) -> p n c", n=4),
                                  WS[:, g, :], VN[:, :, g * HD:(g + 1) * HD], start=True, stop=True)
                    last.then_inc(s_mixed, 1)
            pe.wait_ge(s_ya, 1)
            for c in range(A_W // P):
                aux = AUX_YA + c
                pe.wait_ge(s_auxev, aux - 1 if c == 0 else AUX_YA)
                for n in range(4):
                    last = nc.tensor.transpose(ps[5 + aux % 2][:, n * P:(n + 1) * P], YA[:, n, c * P:(c + 1) * P],
                                               cc("ident"))
                last.then_inc(s_aux, 1)

            pe.wait_ge(s_ev, M0["IN2"] + n_in)
            for b in range(BLOCKS_B + 4):
                if b < BLOCKS_B:
                    h, kb = b // 4, 3 - b % 4
                    N, half = S - kb * P, h % 2 * HD
                    if b >= 2:
                        pe.wait_ge(s_zb, b - 1)
                    mm(ps[b % 2][:, 0:N], FT[half:half + HD, 9 + h // 2, kb * P:(kb + 1) * P],
                       FT[half:half + HD, 6 + h // 2, kb * P:S], start=True, stop=True).then_inc(s_z, 1)
                c = b - 2
                if 0 <= c < BLOCKS_B:
                    h, kb = c // 4, 3 - c % 4
                    N = S - kb * P
                    pe.wait_ge(s_sp, c + 1)
                    if c >= 2:
                        pe.wait_ge(s_wa, c - 1)
                    last = mm(ps[2 + c % 2][:, 0:N], cc("tri"), SP[:, h % 2 * 4 + kb, kb * P:S], start=True, stop=True)
                    for later in range(kb + 1, 4):
                        last = mm(ps[2 + c % 2][:, (later - kb) * P:N], cc("ones"),
                                  SP[:, h % 2 * 4 + later, later * P:S], start=False, stop=True,
                                  skip_group_check=True)
                    last.then_inc(s_r, 1)
                c = b - 4
                if 0 <= c:
                    h, kb = c // 4, 3 - c % 4
                    half = h % 2 * HD
                    pe.wait_ge(s_w, c + 1)
                    if kb == 3 and h in (2, 4):
                        pe.wait_ge(s_y2l, 2 if h == 2 else 3)
                    mm(ps[7 - h // 2 % 2][half:half + HD, kb * P:S], BV[:, kb, h * HD:(h + 1) * HD],
                       WT[c % 2][:, 0:S - kb * P], start=kb == 3, stop=True, skip_group_check=True)\
                        .then_inc(s_bo, 1)

            pe.wait_ge(s_qk, 1 + HEADS // 2 + 2 * (C_W // P))
            pe.wait_ge(s_wa, BLOCKS_B)
            for u in range(8 + 3):
                if u < 8:
                    r, half = u // 2, u % 2 * HD
                    if u >= 2:
                        pe.wait_ge(s_cm, u - 1)
                    mm(ps[u % 2][:, :], FT[half:half + HD, 0, r::4], FT[half:half + HD, 3, :], start=True, stop=True)
                    for g in (1, 2):
                        last = mm(ps[2 + u % 2][:, (g - 1) * P:g * P], FT[half:half + HD, g, r::4],
                                  FT[half:half + HD, 3 + g, r::4], start=True, stop=True)
                    last.then_inc(s_cz, 1)
                b = u - 2
                if 0 <= b < 8:
                    pe.wait_ge(s_cn, b + 1)
                    if b >= 1:
                        pe.wait_ge(s_cc, b)
                    for n in range(6):
                        last = nc.tensor.transpose(ps[4 + n // 4][:, n % 4 * P:(n % 4 + 1) * P],
                                                   PC[b % 3][:, n * P:(n + 1) * P], cc("ident"))
                    last.then_inc(s_ct, 1)
                b = u - 3
                if 0 <= b:
                    r, half = b // 2, b % 2 * HD
                    pe.wait_ge(s_cc, b + 1)
                    if b % 2 == 0:
                        pe.wait_ge(s_y2l, 4 + r)
                    dst = ps[6 + r % 2]
                    for kb in range(4):
                        mm(dst[half:half + HD, 0:P], CV0[:, kb, half:half + HD], PCT[b % 2][:, kb * P:(kb + 1) * P],
                           start=kb == 0, stop=kb == 3)
                    for g in (1, 2):
                        last = mm(dst[half:half + HD, g * P:(g + 1) * P],
                                  CV12[:, r, (g - 1) * P + half:(g - 1) * P + half + HD],
                                  PCT[b % 2][:, (3 + g) * P:(4 + g) * P], start=True, stop=True)
                    last.then_inc(s_co, 1)
            pe.wait_ge(s_y2l, 9)
            out_product("OUT2", (XH, XL), lambda k: None)
            pe.wait_ge(s_acc, SQ0[N_F2 + 1])
            token_squares(acc, 0)
            spread(3, ps[4], RA)
            up(2, "UP2", E_F2, None)
            down(2, "DN2")
            pe.wait_ge(s_acc, SQ0[N_END + 1])
            token_squares(acc, 0)
            spread(4, ps[4], RA)


def constants():
    C = const_layout()
    i = np.arange(P)
    c = np.zeros((P, C["width"]), np.float32)

    def put(name, a):
        c[:, C[name][0]:C[name][0] + C[name][1]] = a
    put("ident", i[:, None] == i[None, :])
    put("swap", (i[:, None] // 64 == i[None, :] // 64) & ((i[:, None] + 32) % 64 == i[None, :] % 64))
    put("ones", 1.0)
    put("tri", i[:, None] >= i[None, :])
    put("causal_neg", np.where(i[None, :] <= i[:, None], 0.0, NEG))
    put("strict", i[:, None] < i[None, :])
    put("strict_neg", np.where(i[:, None] < i[None, :], 0.0, NEG))
    inv = (1.0 / (np.float32(THETA) ** (np.arange(0, ROPE, 2, dtype=np.float32) / np.float32(ROPE)))).astype(np.float32)
    ang = np.arange(S, dtype=np.float32)[:, None] * inv[None, :]
    row = i % 32
    sign = np.where(i % 64 < 32, -1.0, 1.0).astype(np.float32)
    rope = np.stack([np.cos(ang).T[row], np.sin(ang).T[row] * sign[:, None]]).astype(np.float32)
    inv2 = (np.float32(THETA) ** (-np.arange(0, HD, 2, dtype=np.float32) / np.float32(HD))).astype(np.float32)
    mask1 = np.zeros((P, 4, S), np.float32)
    k = np.arange(S)
    for r in range(4):
        q = r + 4 * i
        d = q[:, None] - k[None, :]
        mask1[:, r, :] = np.where((d >= 0) & (d < N_OFFSETS), 0.0, NEG)
    d = i[:, None] - i[None, :]
    mask2 = np.concatenate([np.where(d >= 0, 0.0, NEG), np.where((d >= 0) & (d % 4 == 0), 0.0, NEG)], 1)
    return c, rope, mask1, mask2.astype(np.float32), inv2[row][:, None], sign[:, None]


def kernel(**inputs):
    import concourse.bacc as _bacc
    from concourse.bass_utils import run_bass_kernel_spmd as _run

    a = {k: np.asarray(v) for k, v in inputs.items()}
    const, rope, mask1, mask2, inv2, sign = constants()

    def chunks(v):
        v = v.reshape(-1, P)
        return v.T

    V = vec_layout()
    parts = {
        "a_mix": chunks(a["a_mix_norm"]), "a_conv": chunks(a["a_conv"]), "b_mix": chunks(a["b_mix_norm"]),
        "q_norm": chunks(a["b_q_norm"]), "kv_in": chunks(a["kv_in_norm"]), "kv_norm": chunks(a["kv_norm"]),
        "ffn_norm0": chunks(a["ffn_norm"][0]), "ffn_norm1": chunks(a["ffn_norm"][1]),
        "ffn_conv0": chunks(a["ffn_conv"][0]), "ffn_conv1": chunks(a["ffn_conv"][1]),
        "final": chunks(a["final_norm"]), "b_ada": chunks(a["b_ada_2"]),
        "g_mix": chunks(a["g_mix_2"]), "g_ffn": chunks(a["g_ffn_2"]), "ffn_conv2": chunks(a["conv_w_2"]),
        "conv_b": chunks(a["conv_b_2"]), "g_final": chunks(a["g_final_2"]), "b_sp": a["b_sp_2"][0].T,
        "inv_freq": inv2, "sin_sign": sign,
    }
    vec = np.ascontiguousarray(np.concatenate([parts[n] for n in V if n != "width"], axis=1))
    assert vec.shape == (P, V["width"])

    def tiles(w, cols=None):
        w = w if cols is None else w[:, cols]
        kc, n = w.shape[0] // P, w.shape[1] // P
        t = w.reshape(kc, P, n, P).transpose(2, 0, 1, 3)
        if kc > BLK:
            pad = -kc % BLK
            t = np.concatenate([t, np.zeros((n, pad, P, P), t.dtype)], axis=1)
        t = t.reshape(-1, BLK, P, P).transpose(0, 2, 1, 3)
        return t.reshape(-1, P, TILE)

    def interleave(*starts):
        firsts, n = starts[:-1], starts[-1]
        return np.concatenate([np.arange(f + j * P, f + (j + 1) * P) for j in range(n) for f in firsts])

    hw = np.arange(NOPE + ROPE)
    uq_cols = np.concatenate([h * (NOPE + ROPE) + hw[NOPE:] for h in range(HEADS)]
                             + [h * (NOPE + ROPE) + hw[:NOPE] for h in range(HEADS)])
    dkv_cols = np.concatenate([np.arange(KV_LORA + ROPE), KV_LORA + np.arange(ROPE)])
    offs = np.cumsum([0, A_W, A_W, B_W, B_W, B_W, C_W, C_W, C_W])
    a_u, a_v, b_q, b_k, b_v, c_q, c_k, c_v = [np.arange(offs[i], offs[i + 1]) for i in range(8)]
    in2_cols = np.concatenate([a_v, a_u, c_v, b_v, c_q, c_k, b_q, b_k])
    up_cols = interleave(0, D_FF, FF)
    w_all = np.ascontiguousarray(np.concatenate([
        tiles(a["a_w_in"][0], interleave(D, 2 * D, KD)), tiles(a["a_w_in"][0], np.arange(D)),
        tiles(a["a_w_out"][0]), tiles(a["ffn_w_up"][0], up_cols), tiles(a["ffn_w_down"][0]),
        tiles(a["w_dkv"], dkv_cols), tiles(a["b_w_dq"][0]), tiles(a["w_ukv"]), tiles(a["b_w_uq"][0], uq_cols),
        tiles(a["b_w_o"][0]), tiles(a["ffn_w_up"][1], up_cols), tiles(a["ffn_w_down"][1]),
        tiles(a["w_in_2"][0], in2_cols), tiles(a["w_out_2"][0]), tiles(a["w_up_2"][0], up_cols),
        tiles(a["w_down_2"][0]),
    ]))
    assert len(w_all) == len(schedule()[2])
    arrays = {
        "w_tiles": w_all, "ada_tiles": np.ascontiguousarray(a["w_ada_2"][0].T).reshape(6 * KD, P, D),
        "c_in": np.ascontiguousarray(np.broadcast_to(a["c_2"][0], (P, D))),
        "x_in": np.ascontiguousarray(a["x"][0].T.reshape(KD, P, S).transpose(1, 0, 2)),
        "vec_in": vec, "const_in": const, "rope_in": rope, "mask1_in": mask1, "mask2_in": mask2,
        "gsgu_in": np.ascontiguousarray(np.broadcast_to(a["g_sgu_2"][0], (P, A_W))),
        "wsp_in": np.ascontiguousarray(a["w_sp_2"][0].transpose(2, 0, 1)),
        "pos_in": np.ascontiguousarray(np.broadcast_to(a["positions_2"][0], (P, S))),
    }
    nc = _bacc.Bacc("TRN2", target_bir_lowering=False, num_devices=1)
    aps = {n: nc.dram_tensor(n, v.shape, mybir.dt.from_np(v.dtype), kind="ExternalInput").ap()
           for n, v in arrays.items()}
    out = nc.dram_tensor("out_x", (P, KD, S), F32, kind="ExternalOutput").ap()
    build(nc, out=out, **aps)
    r = _run(nc, [arrays], core_ids=[0])
    got = r.results[0]["out_x"]
    return np.ascontiguousarray(got.transpose(1, 0, 2).reshape(D, S).T)[None]
```

```python
from contextlib import ExitStack

import numpy as np
import concourse.bass as bass
from concourse import mybir

F32 = mybir.dt.float32
F32R = mybir.dt.float32r
I32 = mybir.dt.int32
BF16 = mybir.dt.bfloat16
ACT = mybir.ActivationFunctionType
ALU = mybir.AluOpType
AX_X = mybir.AxisListType.X

P = 128
D = 1024
KD = D // P
S = 512
D_FF = 2816
FF = D_FF // P
HEADS = 8
NOPE, ROPE, VD = 128, 64, 128
Q_LORA, KV_LORA = 512, 256
KQ, KKV = Q_LORA // P, KV_LORA // P
THETA = 10000.0
EPS = 1e-6
MLA_SCALE = float((NOPE + ROPE) ** -0.5)
HD = 64
A_W, B_W, C_W = 256, 384, 384
GROUPS = A_W // HD
B_HEADS = B_W // HD
QK_SCALE = HD ** -0.5
N_OFFSETS = 129
NEG = -1.0e30
BLK = 8
TILE = BLK * P
RAW = 4
SPL = 2
ADA = 6
CONV = 3


def vec_layout():
    at, out = 0, {}
    for name, n in (("a_mix", KD), ("a_conv", CONV * KD), ("b_mix", KD), ("q_norm", KQ), ("kv_in", KD),
                    ("kv_norm", KKV), ("ffn_norm0", KD), ("ffn_norm1", KD), ("ffn_conv0", CONV * 2 * FF),
                    ("ffn_conv1", CONV * 2 * FF), ("final", KD), ("b_ada", 6 * KD), ("g_mix", KD),
                    ("g_ffn", KD), ("ffn_conv2", CONV * 2 * FF), ("conv_b", 2 * FF), ("g_final", KD),
                    ("b_sp", GROUPS), ("inv_freq", 1), ("sin_sign", 1)):
        out[name] = (at, n)
        at += n
    out["width"] = at
    return out


def const_layout():
    at, out = 0, {}
    for name, n in (("ident", P), ("ones", P), ("tri", P), ("causal_neg", P), ("strict", P),
                    ("strict_neg", P)):
        out[name] = (at, n)
        at += n
    out["width"] = at
    return out


PHASES = (
    ("A_CH", 16, [1]), ("A_B", 8, [1]), ("A_OUT", 8, [1]),
    ("UP0", 2 * FF, [1]), ("DN0", 24, [0, 0, 1]),
    ("DKV", 3, [1]), ("DQ", 4, [1]), ("UKV", 4, [4]), ("UQ", 6, [2]), ("WO", 8, [1]),
    ("UP1", 2 * FF, [1]), ("DN1", 24, [0, 0, 1]),
    ("IN2", 22, [1]), ("OUT2", 8, [1]), ("UP2", 2 * FF, [1]), ("DN2", 24, [0, 0, 1]),
)


def schedule():
    t0, m0, done_t, done_m, steps = {}, {}, [], [], 0
    for name, tiles, ends in PHASES:
        t0[name], m0[name] = len(done_t), len(done_m)
        for i in range(tiles):
            n = ends[i % len(ends)]
            for _ in range(n):
                steps += 1
                done_m.append(steps)
            steps += n == 0
            done_t.append(steps)
    return t0, m0, done_t, done_m


def build(nc, w_tiles, ada_tiles, c_in, x_in, vec_in, const_in, rope_in, mask1_in, mask2_in, gsgu_in, wsp_in, pos_in, out):
    T0, M0, DONE_T, DONE_M = schedule()
    NT = len(DONE_T)
    V = vec_layout()
    C = const_layout()
    ctx = ExitStack()
    with ctx:
        def sb(name, shape, dt=F32, stack=ctx):
            return stack.enter_context(nc.sbuf_tensor(name, shape, dt))

        def sem(name):
            return ctx.enter_context(nc.semaphore(name))

        X = sb("X", [P, KD, S])
        XH = sb("XH", [P, KD, S], F32R)
        XL = sb("XL", [P, KD, S], F32R)
        raw = sb("raw", [P, RAW, TILE])
        WH = [sb(f"WH{i}", [P, TILE], F32R) for i in range(SPL)]
        WL = [sb(f"WL{i}", [P, TILE], F32R) for i in range(SPL)]
        vec = sb("vec", [P, V["width"]])
        cst = sb("cst", [P, C["width"]])
        cos_t = sb("cos_t", [P, S])
        sin_t = sb("sin_t", [P, S])
        rb = sb("rb", [P, S])
        rbl = sb("rbl", [P, S])
        acc = sb("acc", [P, S])
        SQ = sb("SQ", [P, 2, S])
        AT = sb("AT", [P, 2, S])
        RA = sb("RA", [P, S])
        RB = sb("RB", [P, S])
        mask16 = sb("mask16", [P, 3, P], BF16)
        mod = sb("mod", [P, 6 * KD])
        gm = sb("gm", [P, 4, KD])
        epsc = sb("epsc", [P, 1])
        gsgu = sb("gsgu", [P, A_W])
        nt = sb("nt", [P, 5, 4])

        st = ExitStack()
        CV = sb("CV", [P, KD, S], F32, st)
        MH = sb("MH", [P, KD, S], F32R, st)
        ML = sb("ML", [P, KD, S], F32R, st)
        ada = sb("ada", [P, ADA, D], F32, st)
        crow = sb("crow", [P, D], F32, st)
        st.close()
        st = ExitStack()
        HH = sb("HH", [P, FF, S], F32R, st)
        HL = sb("HL", [P, FF, S], F32R, st)
        TG = sb("TG", [P, S + 2], F32, st)
        TU = sb("TU", [P, S + 2], F32, st)
        CG = sb("CG", [P, S], F32, st)
        CU = sb("CU", [P, S], F32, st)
        st.close()
        st = ExitStack()
        QXH = sb("QXH", [P, KD, S], F32R, st)
        QXL = sb("QXL", [P, KD, S], F32R, st)
        st.close()
        st = ExitStack()
        KN = sb("KN", [P, HEADS, S], F32, st)
        VT = sb("VT", [P, HEADS, S], F32, st)
        KR = sb("KR", [P, S], F32, st)
        QN = sb("QN", [P, HEADS, S], F32, st)
        QR = sb("QR", [P, HEADS // 2, S], F32, st)
        stat = sb("stat", [P, 4, 4 * HEADS], F32, st)
        st2 = ExitStack()
        CL = sb("CL", [P, KKV, S], F32, st2)
        CLH = sb("CLH", [P, KKV, S], F32R, st2)
        CLL = sb("CLL", [P, KKV, S], F32R, st2)
        QL = sb("QL", [P, KQ, S], F32, st2)
        st2.close()
        OH = sb("OH", [P, HEADS, S], F32R, st)
        OL = sb("OL", [P, HEADS, S], F32R, st)
        st.close()
        st = ExitStack()
        FT = sb("FT", [P, 12, S], F32, st)
        BV = sb("BV", [P, 4, B_W], F32, st)
        CV0 = sb("CV0", [P, 4, P], F32, st)
        CV12 = sb("CV12", [P, 4, 2 * P], F32, st)
        WS = sb("WS", [P, GROUPS, P], F32, st)
        MK1 = sb("MK1", [P, 4, S], F32, st)
        MK2 = sb("MK2", [P, 2 * P], F32, st)
        posi = sb("posi", [P, S], I32, st)
        st2 = ExitStack()
        YA = sb("YA", [P, 4, A_W], F32, st2)
        st2.close()
        ZC = [sb(f"ZC{i}", [P, S + 2 * P], F32, st) for i in range(2)]
        PC = [sb("PC0", [P, S + 2 * P], F32, st)]
        cstat = sb("cstat", [P, 4, 8], F32, st)
        st2 = ExitStack()
        U = sb("U", [P, 4, A_W], F32, st2)
        VV = sb("VV", [P, 4, A_W], F32, st2)
        VN = sb("VN", [P, 4, A_W], F32, st2)
        vst = sb("vst", [P, 3, 4 * GROUPS], F32, st2)
        st2.close()
        st2 = ExitStack()
        ZB = [sb(f"ZB{i}", [P, S], F32, st2) for i in range(6)]
        EB = [sb(f"EB{i}", [P, S], F32, st2) for i in range(3)]
        SP = sb("SP", [P, 8, S], F32, st2)
        WT = [sb(f"WT{i}", [P, S], F32, st2) for i in range(3)]
        st2.close()
        st2 = ExitStack()
        PC += [sb(f"PC{i}", [P, S + 2 * P], F32, st2) for i in (1, 2)]
        PCT = [sb(f"PCT{i}", [P, S + 2 * P], F32, st2) for i in range(2)]
        st2.close()
        st.close()

        MB = (AT[:, 0, :], SQ[:, 0, :], AT[:, 1, :], SQ[:, 1, :])
        PB = [SQ[:, 0, :], SQ[:, 1, :], RA[:, :], RB[:, :]]
        SB = (4, 5, 2, 3)

        ps = [ctx.enter_context(nc.psum_tensor(f"ps{i}", [P, S], F32)) for i in range(8)]

        MIXED = (ps[7], ps[4])

        s_in = {n: sem(f"s_in_{n}") for n in ("x0", "x1", "x2", "x3", "c", "vec", "const", "rope", "gsgu", "wsp", "mask", "pos")}
        s_raw = [sem(f"s_raw{i}") for i in range(RAW)]
        s_hi = sem("s_hi")
        s_lo = sem("s_lo")
        s_pe = sem("s_pe")
        s_ev = sem("s_ev")
        s_ada_in = [sem(f"s_ada_in{i}") for i in range(ADA)]
        s_ada = sem("s_ada")
        s_cact = sem("s_cact")
        s_set = sem("s_set")
        s_sq = sem("s_sq")
        s_acc = sem("s_acc")
        s_sq2 = sem("s_sq2")
        s_acc2 = sem("s_acc2")
        s_ms = sem("s_ms")
        s_ssum = sem("s_ssum")
        s_root = sem("s_root")
        s_rb = sem("s_rb")
        s_dg = sem("s_dg")
        s_bc = sem("s_bc")
        s_xh = sem("s_xh")
        s_xl = sem("s_xl")
        s_xlp = sem("s_xlp")
        s_nb = sem("s_nb")
        s_dve = sem("s_dve")
        s_act = sem("s_act")
        s_gc = sem("s_gc")
        s_sg = sem("s_sg")
        s_h = sem("s_h")
        s_hh = sem("s_hh")
        s_hl = sem("s_hl")
        s_y = sem("s_y")
        s_yh = sem("s_yh")
        s_yl = sem("s_yl")
        s_aux = sem("s_aux")
        s_auxev = sem("s_auxev")
        s_lh = sem("s_lh")
        s_ll = sem("s_ll")
        s_qk = sem("s_qk")
        s_m16 = sem("s_m16")
        s_s = sem("s_s")
        s_mx = sem("s_mx")
        s_p = sem("s_p")
        s_rs = sem("s_rs")
        s_pn = sem("s_pn")
        s_pt = sem("s_pt")
        s_ptc = sem("s_ptc")
        s_pv = sem("s_pv")
        s_oh = sem("s_oh")
        s_ol = sem("s_ol")
        s_ws = sem("s_ws")
        s_arg = sem("s_arg")
        s_trig = sem("s_trig")
        s_gelu = sem("s_gelu")
        s_vs = sem("s_vs")
        s_vr = sem("s_vr")
        s_vn = sem("s_vn")
        s_mixed = sem("s_mixed")
        s_ya = sem("s_ya")
        s_y2h = sem("s_y2h")
        s_y2l = sem("s_y2l")
        s_z = sem("s_z")
        s_zb = sem("s_zb")
        s_ln = sem("s_ln")
        s_sp = sem("s_sp")
        s_r = sem("s_r")
        s_wa = sem("s_wa")
        s_w = sem("s_w")
        s_bo = sem("s_bo")
        s_cz = sem("s_cz")
        s_cm = sem("s_cm")
        s_cp = sem("s_cp")
        s_crs = sem("s_crs")
        s_cn = sem("s_cn")
        s_ct = sem("s_ct")
        s_cc = sem("s_cc")
        s_co = sem("s_co")
        s_fin = sem("s_fin")
        s_out = sem("s_out")

        block = ctx.enter_context(nc.Block())

        def vcol(name, i):
            first = V[name][0]
            return vec[:, first + i:first + i + 1] if isinstance(i, int) else vec[:, bass.ds(i + first, 1)]

        def cc(name):
            return cst[:, C[name][0]:C[name][0] + C[name][1]]

        def at(t, i):
            return t[:, i, :] if isinstance(i, int) else t[:, bass.ds(i, 1), :].rearrange("p a b -> p (a b)")

        def f32(ap):
            return ap.bitcast(F32)

        ADA_AT = ((0, 1), (2,), (3, 4), (5,))
        NORM_CHUNKS = [KD, KD, KD, KKV, KQ, KD, KD, KD, KD]
        N_A, N_F0, N_KV, N_LK, N_LQ, N_F1, N_FIN, N_F2, N_END = range(9)
        SQ0 = [sum(NORM_CHUNKS[:i]) for i in range(10)]
        E_A, E_F0, E_KV, E_Q, E_F1, E_M2, E_F2 = range(7)
        XL0 = [KD * e for e in range(E_M2 + 1)] + [KD * E_M2 + KD // 2]
        RB_AT = {n: i for i, n in enumerate((N_A, N_F0, N_KV, N_LK, N_F1))}
        XLP0 = {E_M2: 0, E_F2: KD // 2}
        NB_KV, NB_Q, NB_M2, NB_F2 = 0, KKV, KKV + KQ, KKV + KQ + KD
        AUX_V, AUX_2 = 0, HEADS
        N_TOK = 2 * (A_W // P) + C_W // P + B_W // P
        AUX_YA = AUX_2 + N_TOK
        BLOCKS_A = 4 * HEADS
        STEPS_B = []
        for i in range(2 * B_HEADS + 2):
            if i < 2 * B_HEADS:
                STEPS_B.append((i // 4 * 2, 3 - i % 4))
            if i >= 2:
                STEPS_B.append(((i - 2) // 4 * 2 + 1, 3 - (i - 2) % 4))
        BLOCKS_B = len(STEPS_B)
        BESIDE = 6
        KEYS_AT = N_TOK + 2 * (B_W // P)
        BANK_R = (5, 6)
        BANK_B = (7, 3, 2)

        def z_bank(b):
            return 4 if b < BESIDE + 2 else (4, 0, 1)[b % 3]
        BANKS_Z, BANKS_T, BANK_C = ((0, 1), (4, 3)), (5, 6), (7, 2)

        def before_b(b):
            return max((c for c in range(b) if (STEPS_B[c][0] - STEPS_B[b][0]) % 2 == 0), default=None)

        PAIR_END = [max(b for b, (h, kb) in enumerate(STEPS_B) if h // 2 == c) for c in range(B_HEADS // 2)]

        class Chain:

            def __init__(self, eng, s):
                self.eng, self.s, self.n, self.i, self.per = eng, s, 0, None, 0

            def enter(self, i, per):
                self.i, self.per, self.base = i, per, self.n

            def leave(self):
                assert self.n - self.base == self.per, (self.n - self.base, self.per)
                self.n, self.i = self.base, None

            def step(self, ins):
                ins.then_inc(self.s, 1)
                self.n += 1

            def wait(self):
                self.eng.wait_ge(self.s, self.n if self.i is None else self.i * self.per + self.n)

            def link(self, ins):
                self.step(ins)
                self.wait()

        def repeat(eng, times, body, chain=None, per=0, peel=0):
            def one(i):
                if chain:
                    chain.enter(i, per)
                body(i)
                if chain:
                    chain.leave()
            for i in range(peel):
                one(i)
            if times > peel:
                with eng.Fori(peel, times) as i:
                    one(i)
            if chain:
                chain.n += times * per

        @block.sync
        def _(sp):
            def load(t, slot, first=False):
                if not first:
                    sp.wait_ge(s_lo, t - (RAW - 1))
                src = w_tiles[t] if isinstance(t, int) else \
                    w_tiles[bass.ds(t, 1), :, :].rearrange("a p n -> p (a n)")
                sp.dma_start(raw[:, slot, :], src).then_inc(s_raw[slot], 16)

            def load_ada(a, slot, first=False):
                if not first:
                    sp.wait_ge(s_ada, a - (ADA - 1))
                src = ada_tiles[a] if isinstance(a, int) else \
                    ada_tiles[bass.ds(a, 1), :, :].rearrange("a p n -> p (a n)")
                sp.dma_start(ada[:, slot, :], src).then_inc(s_ada_in[slot], 16)

            for k in range(RAW):
                load(k, k, True)
                if k < 2:
                    sp.dma_start(X[:, 4 * k:4 * k + 2, :], x_in[:, 4 * k:4 * k + 2, :]).then_inc(s_in[f"x{2 * k}"], 16)

            def with_ada(i):
                for k in range(RAW):
                    load(i * RAW + (RAW + k), k)
                    for q in ADA_AT[k]:
                        load_ada(i * ADA + q, q, isinstance(i, int))
            n_ada = 6 * KD // 6
            repeat(sp, n_ada, with_ada, peel=1)

            def four(i):
                for k in range(RAW):
                    load(i * RAW + ((n_ada + 1) * RAW + k), k)
            repeat(sp, NT // RAW - n_ada - 1, four)
            for t in range(NT // RAW * RAW, NT):
                load(t, t % RAW)
            for m in range(KD):
                sp.wait_ge(s_fin, m + 1)
                sp.dma_start(out[:, m, :], X[:, m, :]).then_inc(s_out, 16)
            sp.wait_ge(s_out, 16 * KD)

        @block.gpsimd
        def _(pool):
            def lo(t, k):
                pool.wait_ge(s_hi, t + 1)
                nc.gpsimd.tensor_tensor(WL[k % SPL][:, :], raw[:, k, :], f32(WH[k % SPL][:, :]),
                                        ALU.subtract).then_inc(s_lo, 1)

            def modulated(e):
                for k in range(1, KD, 2):
                    pool.wait_ge(s_xh, KD * e + k + 1)
                    nc.gpsimd.tensor_tensor(XL[:, k, :], MB[k % 4], f32(XH[:, k, :]), ALU.subtract)\
                        .then_inc(s_xlp, 1)

            def lo_tiles(first, end):
                start = -(-first // RAW) * RAW
                for t in range(first, min(start, end)):
                    lo(t, t % RAW)

                def four(i):
                    for k in range(RAW):
                        lo(i * RAW + (start + k), k)
                rounds = max(0, (end - start) // RAW)
                repeat(pool, rounds, four)
                for t in range(start + rounds * RAW, end):
                    lo(t, t % RAW)

            lo_tiles(0, T0["IN2"] + SPL)
            modulated(E_M2)
            pool.wait_ge(s_in["wsp"], 16)
            nc.gpsimd.affine_select(out=WS[:, :, :], in_=WS[:, :, :], compare_op=ALU.is_ge, fill=0.0, base=0,
                                    pattern=[[0, GROUPS], [1, P]], channel_multiplier=-1).then_inc(s_ws, 1)
            lo_tiles(T0["IN2"] + SPL, T0["UP2"] + SPL)
            modulated(E_F2)
            lo_tiles(T0["UP2"] + SPL, NT)

        @block.scalar
        def _(act):
            ch = Chain(act, s_act)
            act.dma_start(vec[:, :], vec_in).then_inc(s_in["vec"], 16)
            for m in (1, 3):
                act.dma_start(X[:, 2 * m:2 * m + 2, :], x_in[:, 2 * m:2 * m + 2, :]).then_inc(s_in[f"x{m}"], 16)
            act.dma_start(crow[:, :], c_in).then_inc(s_in["c"], 16)
            act.dma_start(cst[:, :], const_in).then_inc(s_in["const"], 16)
            act.dma_start(cos_t[:, :], rope_in[0]).then_inc(s_in["rope"], 16)
            act.dma_start(sin_t[:, :], rope_in[1]).then_inc(s_in["rope"], 16)
            act.dma_start(gsgu[:, :], gsgu_in).then_inc(s_in["gsgu"], 16)

            def hi(t, i=0, per=0):
                slot = t % RAW
                act.wait_ge(s_raw[slot], i * (16 * per // RAW) + 16 * (t // RAW + 1))
                nc.scalar.activation(WH[t % SPL][:, :], raw[:, slot, :], ACT.Copy).then_inc(s_hi, 1)

            def ahead(t, i=0, per=0):
                if not isinstance(i, int) or t + i * per + SPL < NT:
                    act.wait_ge(s_pe, i * per + DONE_T[t])
                    hi(t + SPL, i, per)

            def apart():
                act.wait_ge(s_set, 1)

            def square(n, m, k, src):
                act.wait_ge(s_acc, m + (SQ0[n] - 1))
                nc.scalar.activation(SQ[:, k % 2, :], src, ACT.Square).then_inc(s_sq, 1)

            def token_root(n, dim=D):
                act.wait_ge(s_ssum, n + 1 + (n > N_FIN))
                nc.scalar.activation(nt[:, 2, :], ps[4][:, 0:4], ACT.Sqrt, bias=epsc[:, :], scale=1.0 / dim)\
                    .then_inc(s_root, 1)

            def root(n, dim, dst):
                act.wait_ge(s_ssum, n + 1)
                nc.scalar.activation(dst[:, :], ps[4][:, :], ACT.Sqrt, bias=epsc[:, :], scale=1.0 / dim)\
                    .then_inc(s_root, 1)

            def residual(phase, tiles_per_m, gname, n, second=False):
                per = 4 * tiles_per_m

                def body(i):
                    for k in range(4):
                        for j in range(tiles_per_m):
                            ahead(T0[phase] + k * tiles_per_m + j, i, per)
                        m = i * 4 + k
                        act.wait_ge(s_acc, m + (SQ0[n] - 1))
                        act.wait_ge(s_ev, m + (M0[phase] + 1))
                        apart()
                        if gname:
                            nc.scalar.activation(at(XH, m), at(X, m), ACT.Copy, scale=vcol(gname, m))\
                                .then_inc(s_xh, 1)
                        nc.scalar.activation(SQ[:, k % 2, :], at(X, m), ACT.Square).then_inc(s_sq, 1)
                        if second:
                            act.wait_ge(s_acc2, m + 1)
                            apart()
                            nc.scalar.activation(AT[:, k % 2, :], at(X, m), ACT.Square, scale=vcol("final", m))\
                                .then_inc(s_sq2, 1)
                repeat(act, KD // 4, body, peel=KD // 4 if phase == PHASES[-1][0] else 0)

            def up(f, phase, bias):
                def body(i):
                    for j in range(2):
                        t, jj = T0[phase] + 2 * j, i * 2 + j
                        ahead(t, i, 4)
                        act.wait_ge(s_gc, jj + (FF * f + 1))
                        apart()
                        nc.scalar.activation(CG[:, :], CG[:, :], ACT.Silu, bias=vcol("conv_b", jj) if bias else 0.0)\
                            .then_inc(s_sg, 1)
                        ahead(t + 1, i, 4)
                        act.wait_ge(s_h, jj + (FF * f + 1))
                        apart()
                        nc.scalar.activation(at(HH, jj), CU[:, :], ACT.Copy).then_inc(s_hh, 1)
                repeat(act, FF // 2, body)

            hi(0)
            act.wait_ge(s_in["vec"], 16)
            for m in range(KD):
                if m % 2 == 0:
                    act.wait_ge(s_in[f"x{m // 2}"], 16)
                nc.scalar.activation(XH[:, m, :], X[:, m, :], ACT.Copy, scale=vcol("a_mix", m)).then_inc(s_xh, 1)
                if m == 3:
                    hi(1)
            for m in range(KD):
                if m >= 2:
                    act.wait_ge(s_acc, m - 1)
                nc.scalar.activation(SQ[:, m % 2, :], X[:, m, :], ACT.Square).then_inc(s_sq, 1)
                if m == 4:
                    ahead(T0["A_CH"])
            act.wait_ge(s_set, 1)

            def a_ch(i):
                for k in range(4):
                    if isinstance(i, int) and k == 2:
                        act.wait_ge(s_in["c"], 16)
                        nc.scalar.activation(crow[:, :], crow[:, :], ACT.Silu).then_inc(s_cact, 1)
                        root(N_A, D, rb)
                    if not isinstance(i, int) or k > 0:
                        ahead(T0["A_CH"] + k, i, 4)
            repeat(act, 4, a_ch, peel=1)

            def a_b(i):
                for k in range(4):
                    ahead(T0["A_B"] + k, i, 4)
                    act.wait_ge(s_y, i * 4 + (k + 1))
                    apart()
                    nc.scalar.activation(at(MH, i * 4 + k), CU[:, :], ACT.Copy).then_inc(s_yh, 1)
            repeat(act, 2, a_b)
            residual("A_OUT", 1, "ffn_norm0", N_F0)

            root(N_F0, D, rb)
            up(0, "UP0", False)
            residual("DN0", 3, "kv_in", N_KV)

            ahead(T0["DKV"])
            root(N_KV, D, rb)
            for m in range(KD):
                nc.scalar.activation(QXH[:, m, :], X[:, m, :], ACT.Copy, scale=vcol("b_mix", m)).then_inc(s_xh, 1)
                if m % 4 == 3:
                    ahead(T0["DKV"] + 1 + m // 4)
            for k in range(KKV):
                act.wait_ge(s_ev, M0["DKV"] + k + 1)
                square(N_LK, k, k, CL[:, k, :])
            ahead(T0["DQ"])
            root(N_LK, KV_LORA, rbl)
            ahead(T0["DQ"] + 1)
            for m in range(KKV):
                act.wait_ge(s_nb, NB_KV + m + 1)
                nc.scalar.activation(CLH[:, m, :], CL[:, m, :], ACT.Copy, scale=vcol("kv_norm", m)).then_inc(s_lh, 1)
            for k in range(KQ):
                if k > 1:
                    ahead(T0["DQ"] + k)
                act.wait_ge(s_ev, M0["DQ"] + k + 1)
                square(N_LQ, k, k, QL[:, k, :])
            ahead(T0["UKV"])
            token_root(N_LQ, Q_LORA)

            def take_v(h):
                act.wait_ge(s_aux, AUX_V + h + 1)
                nc.scalar.activation(VT[:, h, :], ps[5 + (AUX_V + h) % 2][:, :], ACT.Copy).then_inc(s_auxev, 1)
            take_v(0)
            take_v(1)
            ahead(T0["UKV"] + 1)
            for k in range(2, 4):
                take_v(2 * k - 2)
                take_v(2 * k - 1)
                if k == 2:
                    for m in range(KQ):
                        act.wait_ge(s_nb, NB_Q + m + 1)
                        nc.scalar.activation(XH[:, m, :], QL[:, m, :], ACT.Copy, scale=vcol("q_norm", m))\
                            .then_inc(s_lh, 1)
                ahead(T0["UKV"] + k)
            take_v(6)
            take_v(7)
            for k in range(6):
                ahead(T0["UQ"] + k)

            def head_hi(h):
                act.wait_ge(s_pv, 4 * h + 4)
                nc.scalar.activation(OH[:, h, :], ps[h % 2][:, :], ACT.Copy).then_inc(s_oh, 1)

            for a in range(BLOCKS_A):
                L = (a % 4 + 1) * P
                if a >= 4:
                    act.wait_ge(s_pt, a - 3)
                act.wait_ge(s_mx, a + 1)
                nc.scalar.activation(PB[a % 4][:, 0:L], ps[SB[a % 4]][:, 0:L], ACT.Exp,
                                     bias=stat[:, 1, a:a + 1], scale=MLA_SCALE,
                                     accum_out=stat[:, 2, a:a + 1]).then_inc(s_p, 1)
                act.wait_ge(s_rs, a + 1)
                nc.scalar.activation(PB[a % 4][:, 0:L], PB[a % 4][:, 0:L], ACT.Copy,
                                     scale=stat[:, 3, a:a + 1]).then_inc(s_pn, 1)
                if a % 4 == 0 and a >= 8:
                    head_hi(a // 4 - 2)
            head_hi(HEADS - 2)
            head_hi(HEADS - 1)
            residual("WO", 1, "ffn_norm1", N_F1)

            root(N_F1, D, rb)
            up(1, "UP1", False)
            residual("DN1", 3, None, N_FIN, second=True)
            act.dma_start(MK1[:, :, :], mask1_in).then_inc(s_in["mask"], 16)
            act.dma_start(MK2[:, :], mask2_in).then_inc(s_in["mask"], 16)
            act.dma_start(WS[:, :, :], wsp_in).then_inc(s_in["wsp"], 16)
            act.dma_start(posi[:, :], pos_in).then_inc(s_in["pos"], 16)
            act.wait_ge(s_ms, 1)
            nc.scalar.activation(nt[:, 2:4, :], nt[:, 0:2, :], ACT.Sqrt).then_inc(s_root, 1)

            def modulated(nb0, shift):
                for m in range(KD):
                    act.wait_ge(s_nb, nb0 + m + 1)
                    b = mod[:, shift * KD + m:shift * KD + m + 1]
                    if m % 2 == 0:
                        nc.scalar.activation(XH[:, m, :], MB[m % 4], ACT.Identity, bias=b).then_inc(s_xh, 1)
                    else:
                        ch.link(nc.scalar.activation(MB[m % 4], MB[m % 4], ACT.Identity, bias=b))
                        nc.scalar.activation(XH[:, m, :], MB[m % 4], ACT.Copy).then_inc(s_xh, 1)
            modulated(NB_M2, 0)
            def weight(b):
                N = S - STEPS_B[b][1] * P
                if b >= 3:
                    act.wait_ge(s_bo, b - 2)
                act.wait_ge(s_wa, b + 1)
                nc.scalar.activation(WT[b % 3][:, 0:N], ZB[b % 6][:, 0:N], ACT.Exp).then_inc(s_w, 1)

            def pair_hi(c):
                act.wait_ge(s_bo, PAIR_END[c] + 1)
                nc.scalar.activation(XH[:, 2 + c, :], ps[BANK_B[c]][:, :], ACT.Copy).then_inc(s_y2h, 1)

            def stick(b):
                if b < BLOCKS_B:
                    N = S - STEPS_B[b][1] * P
                    if b >= 3:
                        act.wait_ge(s_sp, b - 2)
                    act.wait_ge(s_zb, b + 1)
                    E = EB[b % 3][:, 0:N]
                    ch.link(nc.scalar.activation(E, ZB[b % 6][:, 0:N], ACT.Abs))
                    ch.link(nc.scalar.activation(E, E, ACT.Exp, scale=-1.0))
                    nc.scalar.activation(E, E, ACT.Ln, bias=1.0).then_inc(s_ln, 1)
                if b >= 4:
                    weight(b - 4)
                if b - 6 in PAIR_END[:-1]:
                    pair_hi(PAIR_END.index(b - 6))

            for k in range(22):
                ahead(T0["IN2"] + k)
                if k == 6:
                    act.wait_ge(s_arg, 1)
                    nc.scalar.activation(sin_t[:, :], RA[:, :], ACT.Sin, scale=vcol("sin_sign", 0)).then_inc(s_trig, 1)
                    act.wait_ge(s_arg, 2)
                    nc.scalar.activation(cos_t[:, :], RB[:, :], ACT.Sin).then_inc(s_trig, 1)
                if k == 7:
                    act.wait_ge(s_auxev, AUX_2 + 4)
                    nc.scalar.activation(VV[:, :, :], VV[:, :, :], ACT.Gelu_apprx_tanh).then_inc(s_gelu, 1)
                    nc.scalar.activation(U[:, :, :], U[:, :, :], ACT.Gelu_apprx_tanh).then_inc(s_gelu, 1)
                if k == 9:
                    act.wait_ge(s_vs, 1)
                    nc.scalar.activation(vst[:, 1, :], vst[:, 0, :], ACT.Sqrt, bias=epsc[:, :], scale=1.0 / HD)\
                        .then_inc(s_vr, 1)
                if k == KEYS_AT:
                    nc.scalar.preload_act_table_set("natural_log_exp_and_others")
                if k >= KEYS_AT:
                    stick(k - KEYS_AT)

            def class_hi(r):
                act.wait_ge(s_co, 2 * r + 2)
                nc.scalar.activation(XH[:, 5:8, r::4],
                                     ps[BANK_C[r % 2]][:, 0:3 * P].rearrange("p (c q) -> p c q", c=3),
                                     ACT.Copy).then_inc(s_y2h, 1)

            def window_exp(u):
                if u >= 3:
                    act.wait_ge(s_ct, u - 2)
                act.wait_ge(s_cm, u + 1)
                nc.scalar.activation(PC[u % 3][:, :], ZC[u % 2][:, :], ACT.Exp, bias=cstat[:, 1, u:u + 1],
                                     accum_out=cstat[:, 2, u:u + 1]).then_inc(s_cp, 1)

            def window_norm(u):
                act.wait_ge(s_crs, u + 1)
                nc.scalar.activation(PC[u % 3][:, :], PC[u % 3][:, :], ACT.Copy, scale=cstat[:, 3, u:u + 1])\
                    .then_inc(s_cn, 1)

            for b in range(BESIDE, BLOCKS_B + 4):
                stick(b)
                if b == BESIDE + 1:
                    for c in range(A_W // P):
                        act.wait_ge(s_aux, AUX_YA + c + 1)
                        nc.scalar.activation(XH[:, c, :], ps[2 + c][:, :], ACT.Copy).then_inc(s_y2h, 1)
                if b == BLOCKS_B + 1:
                    window_exp(0)
                if b == BLOCKS_B + 2:
                    window_norm(0)
            pair_hi(B_HEADS // 2 - 1)
            for u in range(1, 8):
                window_exp(u)
                window_norm(u)
                if u % 2 == 1 and u >= 5:
                    class_hi((u - 5) // 2)
            class_hi(2)
            class_hi(3)
            residual("OUT2", 1, None, N_F2)
            token_root(N_F2)
            modulated(NB_F2, 3)
            up(2, "UP2", True)
            residual("DN2", 3, None, N_END)
            token_root(N_END)

        @block.vector
        def _(dve):
            ch = Chain(dve, s_dve)
            v = nc.vector
            v.memset(epsc[:, :], EPS).then_inc(s_set, 1)

            def zero_pads():
                ch.step(v.memset(TG[:, 0:2], 0.0))
                ch.link(v.memset(TU[:, 0:2], 0.0))

            def add_square(n, m, k):
                dve.wait_ge(s_sq, m + (SQ0[n] + 1))
                if not (n == 0 and isinstance(m, int) and m == 0):
                    dve.wait_ge(s_acc, m + SQ0[n])
                v.tensor_tensor(acc[:, :], acc[:, :], SQ[:, k % 2, :], ALU.add).then_inc(s_acc, 1)

            def inverse(n, dst):
                dve.wait_ge(s_root, n + 1)
                v.reciprocal(dst[:, :], dst[:, :]).then_inc(s_rb, 1)
                dve.wait_ge(s_rb, RB_AT[n] + 1)
                ch.link(v.memset(acc[:, :], 0.0))

            def lo_half(dst_h, dst_l, src, g, done_h, sem_l):
                dve.wait_ge(*done_h)
                v.scalar_tensor_tensor(dst_l, src, g, f32(dst_h), ALU.mult, ALU.subtract).then_inc(sem_l, 1)

            def product(M, i=0, per=0):
                dve.wait_ge(s_pe, i * per + DONE_M[M])

            def residual(phase, tiles_per_m, e, gname, n, gate=None, beside=None, second=False):
                per = 4 * tiles_per_m

                def body(i):
                    for k in range(4):
                        m, M = i * 4 + k, M0[phase] + k
                        product(M, i, per)
                        bank = ps[M % 4][:, :]
                        if gate is None:
                            ins = v.tensor_tensor(at(X, m), bank, at(X, m), ALU.add)
                        else:
                            g = gm[:, gate, m:m + 1] if isinstance(m, int) else \
                                gm[:, gate, :][:, bass.ds(m, 1)]
                            ins = v.scalar_tensor_tensor(at(X, m), bank, g, at(X, m), ALU.mult, ALU.add)
                        ins.then_inc(s_ev, 1)
                        if gname:
                            lo_half(at(XH, m), at(XL, m), at(X, m), vcol(gname, m), (s_xh, m + (KD * e + 1)), s_xl)
                        add_square(n, m, k)
                        if second:
                            dve.wait_ge(s_sq2, m + 1)
                            dve.wait_ge(s_acc2, m + 2)
                            v.tensor_tensor(rbl[:, :], rbl[:, :], AT[:, k % 2, :], ALU.add).then_inc(s_acc2, 1)
                        if beside:
                            beside(i, k)
                repeat(dve, KD // 4, body)

            def conv(dst, src, w, j, chunks, last):
                ch.link(v.tensor_scalar(dst, src[:, 2:S + 2], vcol(w, j + 2 * chunks), None, ALU.mult))
                ch.link(v.scalar_tensor_tensor(dst, src[:, 1:S + 1], vcol(w, j + chunks), dst, ALU.mult, ALU.add))
                last(v.scalar_tensor_tensor(dst, src[:, 0:S], vcol(w, j), dst, ALU.mult, ALU.add))

            def up(f, phase, deferred):
                w = f"ffn_conv{f}"
                zero_pads()

                def body(i):
                    for j in range(2):
                        jj = i * 2 + j
                        for half, (pad, dst) in enumerate(((TG, CG), (TU, CU))):
                            M = M0[phase] + 2 * j + half
                            product(M, i, 4)
                            if deferred:
                                ins = v.tensor_tensor(pad[:, 2:S + 2], ps[M % 4][:, :], rb[:, :], ALU.mult)
                            else:
                                ins = v.tensor_copy(pad[:, 2:S + 2], ps[M % 4][:, :])
                            ins.then_inc(s_ev, 1)
                            dve.wait_ge(s_ev, i * 4 + (M + 1))
                            if half == 0:
                                conv(dst[:, :], pad, w, jj, 2 * FF, lambda ins: ins.then_inc(s_gc, 1))
                            else:
                                conv(dst[:, :], pad, w, jj + FF, 2 * FF, ch.link)
                        dve.wait_ge(s_sg, jj + (FF * f + 1))
                        if deferred:
                            ins = v.tensor_tensor(CU[:, :], CU[:, :], CG[:, :], ALU.mult)
                        else:
                            ins = v.scalar_tensor_tensor(CU[:, :], CU[:, :], vcol("conv_b", jj + FF), CG[:, :],
                                                         ALU.add, ALU.mult)
                        ins.then_inc(s_h, 1)
                        dve.wait_ge(s_hh, jj + (FF * f + 1))
                        v.tensor_tensor(at(HL, jj), CU[:, :], f32(at(HH, jj)), ALU.subtract).then_inc(s_hl, 1)
                repeat(dve, FF // 2, body, ch, 10)

            ch.link(v.memset(acc[:, :], 0.0))
            zero_pads()
            for m in range(KD):
                lo_half(XH[:, m, :], XL[:, m, :], X[:, m, :], vcol("a_mix", m), (s_xh, m + 1), s_xl)
            for m in range(KD):
                add_square(N_A, m, m)
            inverse(N_A, rb)

            def adaln(i, q):
                a = i * 6 + q
                dve.wait_ge(s_ada_in[q], i * 16 + 16)
                dst = mod[:, a:a + 1] if isinstance(a, int) else mod[:, bass.ds(a, 1)]
                w = ada[:, q, :]
                v.scalar_tensor_tensor(w, w, 1.0, crow[:, :], ALU.mult, ALU.mult, accum_out=dst).then_inc(s_ada, 1)

            dve.wait_ge(s_cact, 1)

            def a_ch(i):
                for k in range(2):
                    for half, dst in enumerate((CG, CU)):
                        M = M0["A_CH"] + 2 * k + half
                        product(M, i, 4)
                        v.tensor_tensor(dst[:, :], ps[M % 4][:, :], rb[:, :], ALU.mult).then_inc(s_ev, 1)
                    dve.wait_ge(s_ev, i * 4 + (M + 1))
                    ch.link(v.tensor_tensor(TG[:, 2:S + 2], CG[:, :], CU[:, :], ALU.mult))
                    conv(at(CV, i * 2 + k), TG, "a_conv", i * 2 + k, KD, ch.link)
                    for q in range(3 * k, 3 * k + 3):
                        adaln(i, q)
            repeat(dve, 4, a_ch, ch, 8)

            def a_b(i):
                for k in range(4):
                    j, M = i * 4 + k, M0["A_B"] + k
                    product(M, i, 4)
                    v.tensor_tensor(CG[:, :], ps[M % 4][:, :], rb[:, :], ALU.mult).then_inc(s_ev, 1)
                    dve.wait_ge(s_ev, i * 4 + (M + 1))
                    v.tensor_tensor(CU[:, :], CG[:, :], at(CV, j), ALU.mult).then_inc(s_y, 1)
                    dve.wait_ge(s_yh, j + 1)
                    v.tensor_tensor(at(ML, j), CU[:, :], f32(at(MH, j)), ALU.subtract).then_inc(s_yl, 1)
                    for q in ADA_AT[k]:
                        adaln(i + 4, q)
            repeat(dve, 2, a_b)

            def ada_beside(i, k):
                for q in ADA_AT[k]:
                    adaln(i + 6, q)
            residual("A_OUT", 1, E_F0, "ffn_norm0", N_F0, beside=ada_beside)
            dve.wait_ge(s_ada, 6 * KD)
            b0 = V["b_ada"][0]
            ch.link(v.tensor_tensor(mod[:, :], mod[:, :], vec[:, b0:b0 + 6 * KD], ALU.add))
            for row, (part, g) in enumerate(((1, "g_mix"), (4, "g_ffn"))):
                ch.step(v.scalar_tensor_tensor(gm[:, row, :], mod[:, part * KD:(part + 1) * KD], 1.0,
                                               vec[:, V[g][0]:V[g][0] + KD], ALU.add, ALU.mult))
            for row, part in ((2, 2), (3, 5)):
                ch.link(v.tensor_scalar(gm[:, row, :], mod[:, part * KD:(part + 1) * KD], 1.0, None, ALU.add))
            ch.link(v.tensor_tensor(gm[:, 0, :], gm[:, 0, :], vec[:, V["final"][0]:V["final"][0] + KD], ALU.mult))

            inverse(N_F0, rb)
            up(0, "UP0", True)
            residual("DN0", 3, E_KV, "kv_in", N_KV)

            inverse(N_KV, rb)

            def spread(dst, src):
                v.tensor_tensor(dst[:, :].rearrange("p (n q) -> p n q", n=4),
                                cc("ident").unsqueeze(1).to_broadcast([P, 4, P]),
                                src.unsqueeze(2).to_broadcast([P, 4, P]), ALU.mult).then_inc(s_dg, 1)

            def token_inverse(n):
                dve.wait_ge(s_root, n + 1)
                ch.link(v.reciprocal(nt[:, 4, :], nt[:, 2, :]))
                spread(RA, nt[:, 4, :])

            def to_aux(aux, M):
                product(M)
                if aux >= 2:
                    dve.wait_ge(s_aux, aux - 1)
                v.tensor_copy(AT[:, aux % 2, :], ps[M % 4][:, :]).then_inc(s_ev, 1)

            ropes = [0]

            def rope(M, dst, scale=1.0, by=None):
                if ropes[0]:
                    dve.wait_ge(s_qk, ropes[0])
                ropes[0] += 1
                product(M)
                x = ps[M % 4]
                if by is not None:
                    v.tensor_tensor(RA[:, :], x[:, :], by[:, :], ALU.mult).then_inc(s_ev, 1)
                    dve.wait_ge(s_ev, M + 1)
                    x = RA
                for row in range(0, P, 32):
                    other = row ^ 32
                    ch.step(v.scalar_tensor_tensor(RB[row:row + 32, :], x[other:other + 32, :], scale,
                                                   sin_t[other:other + 32, :], ALU.mult, ALU.mult))
                if by is not None:
                    ch.wait()
                ins = v.scalar_tensor_tensor(RA[:, :], x[:, :], scale, cos_t[:, :], ALU.mult, ALU.mult)
                if by is None:
                    ins.then_inc(s_ev, 1)
                    dve.wait_ge(s_ev, M + 1)
                    ch.wait()
                else:
                    ch.link(ins)
                v.tensor_tensor(dst, RA[:, :], RB[:, :], ALU.add).then_inc(s_qk, 1)

            def take(aux, dst, src=None):
                dve.wait_ge(s_aux, aux + 1)
                v.tensor_copy(dst, ps[5 + aux % 2][:, :] if src is None else src(ps[5 + aux % 2]))\
                    .then_inc(s_auxev, 1)

            for m in range(KD):
                lo_half(QXH[:, m, :], QXL[:, m, :], X[:, m, :], vcol("b_mix", m), (s_xh, KD * E_Q + m + 1), s_xl)
            for k in range(KKV):
                product(M0["DKV"] + k)
                v.tensor_tensor(CL[:, k, :], ps[(M0["DKV"] + k) % 4][:, :], rb[:, :], ALU.mult).then_inc(s_ev, 1)
                add_square(N_LK, k, k)
            dve.wait_ge(s_in["rope"], 32)
            rope(M0["DKV"] + KKV, KR[:, :], by=rb)
            inverse(N_LK, rbl)
            for m in range(KKV):
                v.tensor_tensor(CL[:, m, :], CL[:, m, :], rbl[:, :], ALU.mult).then_inc(s_nb, 1)
            for m in range(KKV):
                lo_half(CLH[:, m, :], CLL[:, m, :], CL[:, m, :], vcol("kv_norm", m), (s_lh, m + 1), s_ll)
            for k in range(KQ):
                product(M0["DQ"] + k)
                v.tensor_tensor(QL[:, k, :], ps[(M0["DQ"] + k) % 4][:, :], rb[:, :], ALU.mult).then_inc(s_ev, 1)
                add_square(N_LQ, k, k)
            for t in range(HEADS // 2):
                for g in range(2):
                    h, M = 2 * t + g, M0["UKV"] + 4 * t + 2 * g
                    product(M)
                    v.tensor_copy(KN[:, h, :], ps[M % 4][:, :]).then_inc(s_ev, 1)
                    to_aux(AUX_V + h, M + 1)
                if t == 0:
                    dve.wait_ge(s_qk, 1)
                    token_inverse(N_LQ)
                    ch.link(v.memset(acc[:, :], 0.0))
                if t == 1:
                    dve.wait_ge(s_bc, 1)
                    for m in range(KQ):
                        v.tensor_tensor(QL[:, m, :], QL[:, m, :], ps[4][:, :], ALU.mult).then_inc(s_nb, 1)
                if t == 2:
                    for m in range(KQ):
                        lo_half(XH[:, m, :], XL[:, m, :], QL[:, m, :], vcol("q_norm", m), (s_lh, KKV + m + 1), s_ll)
            for p in range(HEADS // 2):
                rope(M0["UQ"] + p, QR[:, p, :])
            for h in range(HEADS):
                M = M0["UQ"] + HEADS // 2 + h
                product(M)
                v.tensor_copy(QN[:, h, :], ps[M % 4][:, :]).then_inc(s_ev, 1)

            dve.wait_ge(s_in["const"], 16)
            v.tensor_copy(mask16[:, 0, :], cc("ident")).then_inc(s_m16, 1)
            v.tensor_copy(mask16[:, 1, :], cc("causal_neg")).then_inc(s_m16, 1)
            v.tensor_copy(mask16[:, 2, :], cc("strict_neg")).then_inc(s_m16, 1)

            def head_lo(h):
                dve.wait_ge(s_oh, h + 1)
                v.tensor_tensor(OL[:, h, :], ps[h % 2][:, :], f32(OH[:, h, :]), ALU.subtract).then_inc(s_ol, 1)

            for a in range(BLOCKS_A + 3):
                if a < BLOCKS_A:
                    L = (a % 4 + 1) * P
                    dve.wait_ge(s_s, a + 1)
                    ch.link(v.reduce_max(stat[:, 0, a:a + 1], ps[SB[a % 4]][:, 0:L], AX_X))
                    v.tensor_scalar(stat[:, 1, a:a + 1], stat[:, 0, a:a + 1], -MLA_SCALE, None, ALU.mult)\
                        .then_inc(s_mx, 1)
                b = a - 3
                if 0 <= b:
                    L = (b % 4 + 1) * P
                    dve.wait_ge(s_pt, b + 1)
                    if b >= 2:
                        dve.wait_ge(s_pv, b - 1)
                    v.tensor_copy(AT[:, b % 2, 0:L], ps[6 + b % 2][:, 0:L]).then_inc(s_ptc, 1)
                if a < BLOCKS_A:
                    dve.wait_ge(s_p, a + 1)
                    v.reciprocal(stat[:, 3, a:a + 1], stat[:, 2, a:a + 1]).then_inc(s_rs, 1)
                if a % 4 == 1 and a >= 9:
                    head_lo(a // 4 - 2)
            head_lo(HEADS - 1)
            residual("WO", 1, E_F1, "ffn_norm1", N_F1)

            inverse(N_F1, rb)
            up(1, "UP1", True)
            for half in range(2):
                v.memset(rbl[:, half * (S // 2):(half + 1) * (S // 2)], 0.0).then_inc(s_acc2, 1)
            residual("DN1", 3, None, None, N_FIN, second=True)

            dve.wait_ge(s_ssum, N_FIN + 2)
            ch.link(v.tensor_scalar(nt[:, 0, :], ps[4][:, 0:4], 1.0 / D, EPS, ALU.mult, ALU.add))
            ch.link(v.reciprocal(nt[:, 0, :], nt[:, 0, :]))
            ch.link(v.tensor_tensor(nt[:, 1, :], ps[4][:, 4:8], nt[:, 0, :], ALU.mult))
            v.tensor_scalar(nt[:, 1, :], nt[:, 1, :], 1.0 / D, EPS, ALU.mult, ALU.add).then_inc(s_ms, 1)
            dve.wait_ge(s_root, N_FIN + 1)
            ch.link(v.reciprocal(nt[:, 4, :], nt[:, 3, :]))
            ch.link(v.tensor_tensor(nt[:, 4, :], nt[:, 4, :], nt[:, 2, :], ALU.mult))
            spread(RA, nt[:, 4, :])
            spread(RB, nt[:, 2, :])
            dve.wait_ge(s_bc, 2)

            def modulated(e, nb0, row, shift, r):
                for m in range(KD + 1):
                    if m < KD:
                        if m >= 4 and m % 2 == 0:
                            dve.wait_ge(s_xl, XL0[e] + m // 2 - 1)
                        elif m >= 4:
                            dve.wait_ge(s_xlp, XLP0[e] + m // 2 - 1)
                        v.scalar_tensor_tensor(MB[m % 4], X[:, m, :], gm[:, row, m:m + 1], r[:, :],
                                               ALU.mult, ALU.mult).then_inc(s_nb, 1)
                    k = m - 1
                    if k >= 0 and k % 2 == 0:
                        dve.wait_ge(s_xh, KD * e + k + 1)
                        v.scalar_tensor_tensor(XL[:, k, :], MB[k % 4],
                                               mod[:, shift * KD + k:shift * KD + k + 1], f32(XH[:, k, :]),
                                               ALU.add, ALU.subtract).then_inc(s_xl, 1)
            modulated(E_M2, NB_M2, 0, 0, ps[4])
            dve.wait_ge(s_bc, 3)

            def first_result(m):
                ch.step(v.scalar_tensor_tensor(X[:, m, :], X[:, m, :], vcol("final", m), ps[7][:, :],
                                               ALU.mult, ALU.mult))

            two_pi = 2.0 * np.pi
            part1 = 6.28125
            part2 = 507.0 / 2 ** 18
            part3 = two_pi - part1 - part2
            magic = 1.5 * 2 ** 23
            limit = 3.1415925

            def positions():
                dve.wait_ge(s_in["pos"], 16)
                ch.link(v.tensor_copy(rbl[:, :], posi[:, :]))
                ch.link(v.tensor_scalar(rbl[:, :], rbl[:, :], vcol("inv_freq", 0), None, ALU.mult))

            def angle(dst, quarter):
                ch.link(v.tensor_scalar(acc[:, :], rbl[:, :], 1.0 / two_pi, quarter, ALU.mult, ALU.add))
                ch.link(v.tensor_scalar(acc[:, :], acc[:, :], magic, None, ALU.add))
                ch.link(v.tensor_scalar(acc[:, :], acc[:, :], -magic, None, ALU.add))
                ch.link(v.scalar_tensor_tensor(dst[:, :], acc[:, :], -part1, rbl[:, :], ALU.mult, ALU.add))
                ch.link(v.scalar_tensor_tensor(dst[:, :], acc[:, :], -part2, dst[:, :], ALU.mult, ALU.add))
                ch.link(v.scalar_tensor_tensor(dst[:, :], acc[:, :], -part3, dst[:, :], ALU.mult, ALU.add))
                ch.link(v.tensor_scalar(dst[:, :], dst[:, :], quarter * two_pi, limit, ALU.add, ALU.min))
                v.tensor_scalar(dst[:, :], dst[:, :], -limit, None, ALU.max).then_inc(s_arg, 1)

            def in_tile(k):
                M, aux = M0["IN2"] + k, AUX_2 + k
                if k < N_TOK:
                    to_aux(aux, M)
                elif k < KEYS_AT:
                    product(M)
                    v.tensor_scalar(FT[:, k - N_TOK + 6, :], ps[M % 4][:, :], QK_SCALE if k < N_TOK + 3 else 1.0, None,
                                    ALU.mult).then_inc(s_ev, 1)
                else:
                    if k == KEYS_AT:
                        dve.wait_ge(s_trig, 2)
                    rope(M, FT[:, k - KEYS_AT, :], scale=QK_SCALE if k < KEYS_AT + 3 else 1.0)

            def blocks(bank):
                return bank[:, :].rearrange("p (n f) -> p n f", n=4)

            def in_take(k):
                aux = AUX_2 + k
                if k < 2:
                    take(aux, VV[:, :, k * P:(k + 1) * P], blocks)
                elif k < 4:
                    take(aux, U[:, :, (k - 2) * P:(k - 1) * P], blocks)
                elif k == 4:
                    take(aux, CV0[:, :, :], blocks)
                elif k < 7:
                    take(aux, CV12[:, :, (k - 5) * P:(k - 4) * P], blocks)
                elif k < 10:
                    take(aux, BV[:, :, (k - 7) * P:(k - 6) * P], blocks)

            def by_group(t):
                return t.rearrange("p n (g c) -> p (n g) c", g=GROUPS)

            def v_squares():
                dve.wait_ge(s_gelu, 1)
                ch.link(v.tensor_tensor(VN[:, :, :], VV[:, :, :], VV[:, :, :], ALU.mult))
                v.reduce_sum(vst[:, 0, :], by_group(VN[:, :, :]), AX_X).then_inc(s_vs, 1)

            def v_norm():
                dve.wait_ge(s_vr, 1)
                ch.link(v.reciprocal(vst[:, 2, :], vst[:, 1, :]))
                ch.link(v.tensor_tensor(by_group(VN[:, :, :]), by_group(VV[:, :, :]),
                                        vst[:, 2, :].unsqueeze(2).to_broadcast([P, 4 * GROUPS, HD]), ALU.mult))
                dve.wait_ge(s_in["gsgu"], 16)
                v.tensor_tensor(VN[:, :, :], VN[:, :, :], gsgu[:, :].unsqueeze(1).to_broadcast([P, 4, A_W]),
                                ALU.mult).then_inc(s_vn, 1)

            def gating():
                dve.wait_ge(s_mixed, 1)
                dve.wait_ge(s_gelu, 2)
                for g in range(GROUPS):
                    last = v.scalar_tensor_tensor(
                        YA[:, :, g * HD:(g + 1) * HD],
                        MIXED[g // 2][:, (g % 2) * 256:(g % 2) * 256 + 256].rearrange("p (n c) -> p n c", n=4),
                        vcol("b_sp", g), U[:, :, g * HD:(g + 1) * HD], ALU.add, ALU.mult)
                last.then_inc(s_ya, 1)

            def logits(b):
                N = S - STEPS_B[b][1] * P
                dve.wait_ge(s_z, b + 1)
                if b >= 6:
                    dve.wait_ge(s_w, b - 5)
                v.tensor_copy(ZB[b % 6][:, 0:N], ps[z_bank(b)][:, 0:N]).then_inc(s_zb, 1)

            def softplus(b):
                kb = STEPS_B[b][1]
                N = S - kb * P
                sp = SP[:, b % 8, :]
                dve.wait_ge(s_ln, b + 1)
                if b >= 8:
                    dve.wait_ge(s_r, b - 5)
                v.scalar_tensor_tensor(sp[:, kb * P:S], ZB[b % 6][:, 0:N], 0.0, EB[b % 3][:, 0:N],
                                       ALU.max, ALU.add).then_inc(s_sp, 1)

            def exponent(b):
                h, kb = STEPS_B[b]
                N = S - kb * P
                Z = ZB[b % 6]
                dve.wait_ge(s_r, b + 1)
                v.tensor_tensor(Z[:, 0:N], Z[:, 0:N], ps[BANK_R[h % 2]][:, kb * P:S], ALU.subtract).then_inc(s_wa, 1)

            def pair_lo(c):
                dve.wait_ge(s_y2h, 2 + c + 1)
                v.tensor_tensor(XL[:, 2 + c, :], ps[BANK_B[c]][:, :], f32(XH[:, 2 + c, :]), ALU.subtract)\
                    .then_inc(s_y2l, 1)

            def stick(b):
                if b < BLOCKS_B:
                    logits(b)
                if 0 <= b - 1 < BLOCKS_B:
                    softplus(b - 1)
                if b >= 4:
                    exponent(b - 4)
                if b - 7 in PAIR_END[:-1]:
                    pair_lo(PAIR_END.index(b - 7))

            for k in range(22):
                if k >= KEYS_AT:
                    stick(k - KEYS_AT)
                if k == 21:
                    stick(BESIDE)
                in_tile(k)
                if k >= 1:
                    in_take(k - 1)
                if k < KD:
                    first_result(k)
                if k == 3:
                    positions()
                    angle(RA, 0.0)
                if k == 5:
                    angle(RB, 0.25)
                    ch.link(v.memset(acc[:, :], 0.0))
                if k == 8:
                    v_squares()
                if k == 10:
                    v_norm()
                if k == 14:
                    gating()

            dve.wait_ge(s_in["mask"], 32)

            def class_lo(r):
                dve.wait_ge(s_y2h, 5 + r + 1)
                v.tensor_tensor(XL[:, 5:8, r::4], ps[BANK_C[r % 2]][:, 0:3 * P].rearrange("p (c q) -> p c q", c=3),
                                f32(XH[:, 5:8, r::4]), ALU.subtract).then_inc(s_y2l, 1)

            def window_max(u):
                dve.wait_ge(s_cz, u + 1)
                if u >= 2:
                    dve.wait_ge(s_cp, u - 1)
                ch.step(v.tensor_tensor(ZC[u % 2][:, 0:S], ps[BANKS_Z[u % 2][0]][:, :], MK1[:, u // 2, :], ALU.add))
                ch.link(v.tensor_tensor(ZC[u % 2][:, S:S + 2 * P], ps[BANKS_Z[u % 2][1]][:, 0:2 * P], MK2[:, :],
                                        ALU.add))
                ch.link(v.reduce_max(cstat[:, 0, u:u + 1], ZC[u % 2][:, :], AX_X))
                v.tensor_scalar(cstat[:, 1, u:u + 1], cstat[:, 0, u:u + 1], -1.0, None, ALU.mult)\
                    .then_inc(s_cm, 1)

            def window_sum(u):
                dve.wait_ge(s_cp, u + 1)
                v.reciprocal(cstat[:, 3, u:u + 1], cstat[:, 2, u:u + 1]).then_inc(s_crs, 1)

            def window_copy(u):
                dve.wait_ge(s_ct, u + 1)
                if u >= 2:
                    dve.wait_ge(s_co, u - 1)
                ch.step(v.tensor_copy(PCT[u % 2][:, 0:S], ps[BANKS_T[0]][:, :]))
                v.tensor_copy(PCT[u % 2][:, S:S + 2 * P], ps[BANKS_T[1]][:, 0:2 * P]).then_inc(s_cc, 1)

            for b in range(BESIDE + 1, BLOCKS_B + 4):
                stick(b)
                if b == BESIDE + 2:
                    for c in range(A_W // P):
                        dve.wait_ge(s_y2h, c + 1)
                        v.tensor_tensor(XL[:, c, :], ps[2 + c][:, :], f32(XH[:, c, :]), ALU.subtract)\
                            .then_inc(s_y2l, 1)
                if b == BLOCKS_B + 1:
                    window_max(0)
                if b == BLOCKS_B + 2:
                    window_sum(0)
            window_max(1)
            pair_lo(B_HEADS // 2 - 1)
            window_copy(0)
            window_sum(1)
            for u in range(2, 8 + 2):
                if u < 8:
                    window_max(u)
                if u > 2:
                    window_copy(u - 2)
                if u < 8:
                    window_sum(u)
                if u % 2 == 0 and u >= 6:
                    class_lo((u - 6) // 2)
            class_lo(2)
            class_lo(3)
            residual("OUT2", 1, None, None, N_F2, gate=2)

            token_inverse(N_F2)
            ch.link(v.memset(acc[:, :], 0.0))
            dve.wait_ge(s_bc, 4)
            modulated(E_F2, NB_F2, 1, 3, ps[4])
            up(2, "UP2", False)
            residual("DN2", 3, None, None, N_END, gate=3)
            token_inverse(N_END)
            dve.wait_ge(s_bc, 5)
            for m in range(KD):
                v.scalar_tensor_tensor(X[:, m, :], X[:, m, :], vcol("g_final", m), ps[4][:, :], ALU.mult, ALU.mult)\
                    .then_inc(s_fin, 1)

        @block.tensor
        def _(pe):
            mm = nc.tensor.matmul

            def tile_ready(t, i=0, per=0):
                pe.wait_ge(s_lo, i * per + (t + 1))

            def bank_free(M, i=0, per=0):
                if M >= 4:
                    pe.wait_ge(s_ev, i * per + (M - 3))
                elif not isinstance(i, int) or i > 0:
                    pe.wait_ge(s_ev, i * per + (M - 3))

            def dot(bank, t, blk, xh, xl, first, last):
                h = WH[t % SPL][:, blk * P:(blk + 1) * P]
                lo = WL[t % SPL][:, blk * P:(blk + 1) * P]
                mm(bank, h, xh, start=first, stop=False)
                mm(bank, h, xl, start=False, stop=False)
                return mm(bank, lo, xh, start=False, stop=last)

            def wide(t, M, i=0, per=0, before=None, src=(XH, XL)):
                tile_ready(t, i, per)
                bank_free(M, i, per)
                for k in range(KD):
                    if before:
                        before(k)
                    last = dot(ps[M % 4][:, :], t, k, src[0][:, k, :], src[1][:, k, :], k == 0, k == KD - 1)
                last.then_inc(s_pe, 1)

            def inputs(e):
                if e < E_M2:
                    return lambda k: pe.wait_ge(s_xl, KD * e + k + 1)
                return lambda k: pe.wait_ge(s_xlp, XLP0[e] + k // 2 + 1) if k % 2 else \
                    pe.wait_ge(s_xl, XL0[e] + k // 2 + 1)

            def sum_squares(n):
                pe.wait_ge(s_acc, SQ0[n + 1])
                mm(ps[4][:, :], cc("ones"), acc[:, :], start=True, stop=True).then_inc(s_ssum, 1)

            def token_squares(src, col):
                for n in range(4):
                    last = mm(ps[4][:, col + n:col + n + 1], src[:, n * P:(n + 1) * P], cc("ones")[:, 0:1],
                              start=True, stop=True)
                last.then_inc(s_ssum, 1)

            def spread(count, bank, src):
                pe.wait_ge(s_dg, count)
                mm(bank[:, :], cc("ones"), src[:, :], start=True, stop=True).then_inc(s_bc, 1)

            def a_ch(i):
                start = isinstance(i, int)
                for k in range(4):
                    wide(T0["A_CH"] + k, M0["A_CH"] + k, i, 4, inputs(E_A) if start and k == 0 else None)
                    if start and k == 2:
                        pe.wait_ge(s_in["const"], 16)
                        sum_squares(N_A)
            repeat(pe, 4, a_ch, peel=1)

            def a_b(i):
                for k in range(4):
                    wide(T0["A_B"] + k, M0["A_B"] + k, i, 4)
            repeat(pe, 2, a_b)

            def out_product(phase, src, ready):
                def body(i):
                    for k in range(4):
                        wide(T0[phase] + k, M0[phase] + k, i, 4, ready if k == 0 else None, src)
                repeat(pe, KD // 4, body)

            out_product("A_OUT", (MH, ML), lambda k: pe.wait_ge(s_yl, k + 1))

            def up(f, phase, e, n):
                def body(i):
                    start = isinstance(i, int)
                    for k in range(4):
                        wide(T0[phase] + k, M0[phase] + k, i, 4, inputs(e) if start and k == 0 else None)
                        if start and k == 0 and n is not None:
                            sum_squares(n)
                repeat(pe, FF // 2, body, peel=1)

            def down(f, phase):
                def body(i):
                    for k in range(4):
                        M = M0[phase] + k
                        bank_free(M, i, 4)
                        for j in range(3):
                            t = T0[phase] + 3 * k + j
                            tile_ready(t, i, 12)
                            n = min(BLK, FF - BLK * j)
                            pe.wait_ge(s_hl, FF * f + BLK * j + n)
                            for b in range(n):
                                c = BLK * j + b
                                last = dot(ps[M % 4][:, :], t, b, HH[:, c, :], HL[:, c, :], c == 0, c == FF - 1)
                            last.then_inc(s_pe, 1)
                repeat(pe, KD // 4, body)

            up(0, "UP0", E_F0, N_F0)
            down(0, "DN0")

            def turn(aux, M, strided=False):
                pe.wait_ge(s_ev, M + 1)
                if aux >= 2:
                    pe.wait_ge(s_auxev, aux - 1)
                for n in range(4):
                    src = AT[:, aux % 2, n::4] if strided else AT[:, aux % 2, n * P:(n + 1) * P]
                    last = nc.tensor.transpose(ps[5 + aux % 2][:, n * P:(n + 1) * P], src, cc("ident"))
                last.then_inc(s_aux, 1)

            for k in range(3):
                wide(T0["DKV"] + k, M0["DKV"] + k, before=inputs(E_KV) if k == 0 else None)
                if k == 0:
                    sum_squares(N_KV)
            for k in range(KQ):
                wide(T0["DQ"] + k, M0["DQ"] + k, before=inputs(E_Q) if k == 0 else None, src=(QXH, QXL))
                if k == 0:
                    sum_squares(N_LK)
            for t in range(HEADS // 2):
                tile_ready(T0["UKV"] + t)
                for j in range(4):
                    M = M0["UKV"] + 4 * t + j
                    bank_free(M)
                    for k in range(KKV):
                        if t == 0 and j == 0:
                            pe.wait_ge(s_ll, k + 1)
                        last = dot(ps[M % 4][:, :], T0["UKV"] + t, 2 * j + k, CLH[:, k, :], CLL[:, k, :],
                                   k == 0, k == KKV - 1)
                    last.then_inc(s_pe, 1)
                    if t == 0 and j == 1:
                        pe.wait_ge(s_acc, SQ0[N_LQ + 1])
                        token_squares(acc, 0)
                    if t == 1 and j == 1:
                        spread(1, ps[4], RA)
                    if t > 0 and j % 2 == 0:
                        h = 2 * (t - 1) + j // 2
                        turn(AUX_V + h, M0["UKV"] + 2 * h + 1)
            for t in range(6):
                tile_ready(T0["UQ"] + t)
                for j in range(2):
                    M = M0["UQ"] + 2 * t + j
                    bank_free(M)
                    for k in range(KQ):
                        if t == 0 and j == 0:
                            pe.wait_ge(s_ll, KKV + k + 1)
                        last = dot(ps[M % 4][:, :], T0["UQ"] + t, KQ * j + k, XH[:, k, :], XL[:, k, :],
                                   k == 0, k == KQ - 1)
                    last.then_inc(s_pe, 1)
                    if t == 0:
                        h = HEADS - 2 + j
                        turn(AUX_V + h, M0["UKV"] + 2 * h + 1)

            pe.wait_ge(s_qk, 1 + HEADS // 2)
            pe.wait_ge(s_ev, M0["WO"])
            pe.wait_ge(s_auxev, AUX_V + HEADS)
            pe.wait_ge(s_m16, 3)
            for a in range(BLOCKS_A + 4):
                if a < BLOCKS_A:
                    h, qb = a // 4, a % 4
                    L, half = (qb + 1) * P, h % 2 * HD
                    bank = ps[SB[a % 4]]
                    if a >= 4:
                        pe.wait_ge(s_p, a - 3)
                    mm(bank[:, 0:L], QN[:, h, qb * P:L], KN[:, h, 0:L], start=True, stop=False)
                    mm(bank[:, L - P:L], mask16[:, 0, :], mask16[:, 1, :], start=False, stop=False,
                       skip_group_check=True)
                    mm(bank[:, 0:L], QR[half:half + HD, h // 2, qb * P:L], KR[half:half + HD, 0:L],
                       start=False, stop=True).then_inc(s_s, 1)
                b = a - 2
                if 0 <= b < BLOCKS_A:
                    pe.wait_ge(s_pn, b + 1)
                    if b >= 2:
                        pe.wait_ge(s_ptc, b - 1)
                    for kb in range(b % 4 + 1):
                        last = nc.tensor.transpose(ps[6 + b % 2][:, kb * P:(kb + 1) * P],
                                                   PB[b % 4][:, kb * P:(kb + 1) * P], cc("ident"))
                    last.then_inc(s_pt, 1)
                b = a - 4
                if 0 <= b:
                    h, qb = b // 4, b % 4
                    pe.wait_ge(s_ptc, b + 1)
                    if qb == 0 and h >= 2:
                        pe.wait_ge(s_ol, h - 1)
                    for kb in range(qb + 1):
                        last = mm(ps[h % 2][:, qb * P:(qb + 1) * P], VT[:, h, kb * P:(kb + 1) * P],
                                  AT[:, b % 2, kb * P:(kb + 1) * P], start=kb == 0, stop=kb == qb)
                    last.then_inc(s_pv, 1)
            out_product("WO", (OH, OL), lambda k: pe.wait_ge(s_ol, k + 1))
            up(1, "UP1", E_F1, N_F1)
            down(1, "DN1")

            pe.wait_ge(s_acc, SQ0[N_FIN + 1])
            token_squares(acc, 0)
            pe.wait_ge(s_acc2, KD + 2)
            token_squares(rbl, 4)
            spread(2, ps[4], RA)
            spread(3, ps[7], RB)
            n_in = 22

            def gated():
                pe.wait_ge(s_ya, 1)
                for c in range(A_W // P):
                    for n in range(4):
                        last = nc.tensor.transpose(ps[2 + c][:, n * P:(n + 1) * P], YA[:, n, c * P:(c + 1) * P],
                                                   cc("ident"))
                    last.then_inc(s_aux, 1)

            def stick(b):
                late = b < BESIDE
                if b < BLOCKS_B:
                    h, kb = STEPS_B[b]
                    N, half = S - kb * P, h % 2 * HD
                    old = max((c for c in range(b) if z_bank(c) == z_bank(b)), default=-1)
                    if old >= 0:
                        pe.wait_ge(s_zb, old + 1)
                    mm(ps[z_bank(b)][:, 0:N], FT[half:half + HD, 9 + h // 2, kb * P:(kb + 1) * P],
                       FT[half:half + HD, 6 + h // 2, kb * P:S], start=True, stop=True)
                    mm(ps[z_bank(b)][:, 0:P], mask16[:, 0, :], mask16[:, 2, :], start=False, stop=True,
                       skip_group_check=True).then_inc(s_z, 1)
                for c in range(max(0, b - 3 - (b <= BESIDE)), min(b - 2 - late, BLOCKS_B)):
                    suffix_sums(c)
                for c in range(max(0, b - 5 - (b <= BESIDE)), b - 4 - late):
                    values(c)

            def suffix_sums(c):
                h, kb = STEPS_B[c]
                bank, sp, last_c = ps[BANK_R[h % 2]], SP[:, c % 8, :], before_b(c)
                pe.wait_ge(s_sp, c + 1)
                if last_c is not None:
                    pe.wait_ge(s_wa, last_c + 1)
                elif c == 0:
                    pe.wait_ge(s_auxev, AUX_YA)
                mid = (kb + 1) * P
                if kb < 3:
                    mm(bank[:, mid:S], cc("strict"), SP[:, last_c % 8, mid:S], start=False, stop=True,
                       skip_group_check=True)
                    mm(bank[:, mid:S], cc("tri"), sp[:, mid:S], start=False, stop=True, skip_group_check=True)
                mm(bank[:, kb * P:mid], cc("tri"), sp[:, kb * P:mid], start=True, stop=True,
                   skip_group_check=True).then_inc(s_r, 1)

            def values(c):
                h, kb = STEPS_B[c]
                half = h % 2 * HD
                pe.wait_ge(s_w, c + 1)
                if h == 2 and kb == 3:
                    pe.wait_ge(s_y2l, 2)
                mm(ps[BANK_B[h // 2]][half:half + HD, kb * P:S], BV[:, kb, h * HD:(h + 1) * HD],
                   WT[c % 3][:, 0:S - kb * P], start=kb == 3, stop=True, skip_group_check=True)\
                    .then_inc(s_bo, 1)

            def window_logits(u):
                r, half = u // 2, u % 2 * HD
                z1, z2 = ps[BANKS_Z[u % 2][0]], ps[BANKS_Z[u % 2][1]]
                mm(z1[:, :], FT[half:half + HD, 0, r::4], FT[half:half + HD, 3, :], start=True, stop=True)
                for g in (1, 2):
                    last = mm(z2[:, (g - 1) * P:g * P], FT[half:half + HD, g, r::4],
                              FT[half:half + HD, 3 + g, r::4], start=True, stop=True)
                last.then_inc(s_cz, 1)

            def second_trip(k):
                aux, M = AUX_2 + k, M0["IN2"] + k
                if k < N_TOK:
                    turn(aux, M, strided=k in (5, 6))
            for k in range(n_in):
                wide(T0["IN2"] + k, M0["IN2"] + k, before=inputs(E_M2) if k == 0 else None)
                if k >= 1:
                    second_trip(k - 1)
                if k == 12:
                    pe.wait_ge(s_ws, 1)
                    pe.wait_ge(s_vn, 1)
                    for g in range(GROUPS):
                        last = mm(MIXED[g // 2][:, (g % 2) * 256:(g % 2) * 256 + 256]
                                  .rearrange("p (n c) -> p n c", n=4),
                                  WS[:, g, :], VN[:, :, g * HD:(g + 1) * HD], start=True, stop=True)
                    last.then_inc(s_mixed, 1)
                if k == KEYS_AT:
                    pe.wait_ge(s_ev, M0["IN2"] + KEYS_AT)
                if k >= KEYS_AT:
                    stick(k - KEYS_AT)
            stick(BESIDE)
            stick(BESIDE + 1)
            pe.wait_ge(s_ev, M0["IN2"] + n_in)
            gated()
            for b in range(BESIDE + 2, BLOCKS_B + 5):
                if b == BLOCKS_B:
                    pe.wait_ge(s_qk, 1 + HEADS // 2 + 2 * (C_W // P))
                    pe.wait_ge(s_zb, BLOCKS_B)
                    window_logits(0)
                if b == BLOCKS_B + 1:
                    pe.wait_ge(s_y2l, 4)
                    window_logits(1)
                stick(b)

            def window_turn(b):
                pe.wait_ge(s_cn, b + 1)
                if b >= 1:
                    pe.wait_ge(s_cc, b)
                for n in range(6):
                    last = nc.tensor.transpose(ps[BANKS_T[n // 4]][:, n % 4 * P:(n % 4 + 1) * P],
                                               PC[b % 3][:, n * P:(n + 1) * P], cc("ident"))
                last.then_inc(s_ct, 1)

            def window_values(b):
                r, half = b // 2, b % 2 * HD
                pe.wait_ge(s_cc, b + 1)
                if b % 2 == 0:
                    pe.wait_ge(s_y2l, 4 + r)
                dst = ps[BANK_C[r % 2]]
                for kb in range(4):
                    mm(dst[half:half + HD, 0:P], CV0[:, kb, half:half + HD], PCT[b % 2][:, kb * P:(kb + 1) * P],
                       start=kb == 0, stop=kb == 3)
                for g in (1, 2):
                    last = mm(dst[half:half + HD, g * P:(g + 1) * P],
                              CV12[:, r, (g - 1) * P + half:(g - 1) * P + half + HD],
                              PCT[b % 2][:, (3 + g) * P:(4 + g) * P], start=True, stop=True)
                last.then_inc(s_co, 1)

            window_turn(0)
            for u in range(2, 8 + 3):
                if u < 8:
                    pe.wait_ge(s_cm, u - 1)
                    window_logits(u)
                if 2 < u < 10:
                    window_turn(u - 2)
                if u > 2:
                    window_values(u - 3)
            out_product("OUT2", (XH, XL), lambda k: pe.wait_ge(s_y2l, 5 if k < 5 else 9))
            pe.wait_ge(s_acc, SQ0[N_F2 + 1])
            token_squares(acc, 0)
            spread(4, ps[4], RA)
            up(2, "UP2", E_F2, None)
            down(2, "DN2")
            pe.wait_ge(s_acc, SQ0[N_END + 1])
            token_squares(acc, 0)
            spread(5, ps[4], RA)


def constants():
    C = const_layout()
    i = np.arange(P)
    c = np.zeros((P, C["width"]), np.float32)

    def put(name, a):
        c[:, C[name][0]:C[name][0] + C[name][1]] = a
    put("ident", i[:, None] == i[None, :])
    put("ones", 1.0)
    put("tri", i[:, None] >= i[None, :])
    put("causal_neg", np.where(i[None, :] <= i[:, None], 0.0, NEG))
    put("strict", i[:, None] < i[None, :])
    put("strict_neg", np.where(i[:, None] < i[None, :], 0.0, NEG))
    inv = (1.0 / (np.float32(THETA) ** (np.arange(0, ROPE, 2, dtype=np.float32) / np.float32(ROPE)))).astype(np.float32)
    ang = np.arange(S, dtype=np.float32)[:, None] * inv[None, :]
    row = i % 32
    sign = np.where(i % 64 < 32, 1.0, -1.0).astype(np.float32)
    rope = np.stack([np.cos(ang).T[row], np.sin(ang).T[row] * sign[:, None]]).astype(np.float32)
    inv2 = (np.float32(THETA) ** (-np.arange(0, HD, 2, dtype=np.float32) / np.float32(HD))).astype(np.float32)
    mask1 = np.zeros((P, 4, S), np.float32)
    k = np.arange(S)
    for r in range(4):
        q = r + 4 * i
        d = q[:, None] - k[None, :]
        mask1[:, r, :] = np.where((d >= 0) & (d < N_OFFSETS), 0.0, NEG)
    d = i[:, None] - i[None, :]
    mask2 = np.concatenate([np.where(d >= 0, 0.0, NEG), np.where((d >= 0) & (d % 4 == 0), 0.0, NEG)], 1)
    return c, rope, mask1, mask2.astype(np.float32), inv2[row][:, None], sign[:, None]


def kernel(**inputs):
    import concourse.bacc as _bacc
    from concourse.bass_utils import run_bass_kernel_spmd as _run

    a = {k: np.asarray(v) for k, v in inputs.items()}
    const, rope, mask1, mask2, inv2, sign = constants()

    def chunks(v):
        v = v.reshape(-1, P)
        return v.T

    V = vec_layout()
    parts = {
        "a_mix": chunks(a["a_mix_norm"]), "a_conv": chunks(a["a_conv"]), "b_mix": chunks(a["b_mix_norm"]),
        "q_norm": chunks(a["b_q_norm"]), "kv_in": chunks(a["kv_in_norm"]), "kv_norm": chunks(a["kv_norm"]),
        "ffn_norm0": chunks(a["ffn_norm"][0]), "ffn_norm1": chunks(a["ffn_norm"][1]),
        "ffn_conv0": chunks(a["ffn_conv"][0]), "ffn_conv1": chunks(a["ffn_conv"][1]),
        "final": chunks(a["final_norm"]), "b_ada": chunks(a["b_ada_2"]),
        "g_mix": chunks(a["g_mix_2"]), "g_ffn": chunks(a["g_ffn_2"]), "ffn_conv2": chunks(a["conv_w_2"]),
        "conv_b": chunks(a["conv_b_2"]), "g_final": chunks(a["g_final_2"]), "b_sp": a["b_sp_2"][0].T,
        "inv_freq": inv2, "sin_sign": sign,
    }
    vec = np.ascontiguousarray(np.concatenate([parts[n] for n in V if n != "width"], axis=1))
    assert vec.shape == (P, V["width"])

    def tiles(w, cols=None):
        w = w if cols is None else w[:, cols]
        kc, n = w.shape[0] // P, w.shape[1] // P
        t = w.reshape(kc, P, n, P).transpose(2, 0, 1, 3)
        if kc > BLK:
            pad = -kc % BLK
            t = np.concatenate([t, np.zeros((n, pad, P, P), t.dtype)], axis=1)
        t = t.reshape(-1, BLK, P, P).transpose(0, 2, 1, 3)
        return t.reshape(-1, P, TILE)

    def interleave(*starts):
        firsts, n = starts[:-1], starts[-1]
        return np.concatenate([np.arange(f + j * P, f + (j + 1) * P) for j in range(n) for f in firsts])

    hw = np.arange(NOPE + ROPE)
    uq_cols = np.concatenate([h * (NOPE + ROPE) + hw[NOPE:] for h in range(HEADS)]
                             + [h * (NOPE + ROPE) + hw[:NOPE] for h in range(HEADS)])
    dkv_cols = np.concatenate([np.arange(KV_LORA + ROPE), KV_LORA + np.arange(ROPE)])
    offs = np.cumsum([0, A_W, A_W, B_W, B_W, B_W, C_W, C_W, C_W])
    a_u, a_v, b_q, b_k, b_v, c_q, c_k, c_v = [np.arange(offs[i], offs[i + 1]) for i in range(8)]
    in2_cols = np.concatenate([a_v, a_u, c_v, b_v, b_q, b_k, c_q, c_k])
    up_cols = interleave(0, D_FF, FF)
    w_all = np.ascontiguousarray(np.concatenate([
        tiles(a["a_w_in"][0], interleave(D, 2 * D, KD)), tiles(a["a_w_in"][0], np.arange(D)),
        tiles(a["a_w_out"][0]), tiles(a["ffn_w_up"][0], up_cols), tiles(a["ffn_w_down"][0]),
        tiles(a["w_dkv"], dkv_cols), tiles(a["b_w_dq"][0]), tiles(a["w_ukv"]), tiles(a["b_w_uq"][0], uq_cols),
        tiles(a["b_w_o"][0]), tiles(a["ffn_w_up"][1], up_cols), tiles(a["ffn_w_down"][1]),
        tiles(a["w_in_2"][0], in2_cols), tiles(a["w_out_2"][0]), tiles(a["w_up_2"][0], up_cols),
        tiles(a["w_down_2"][0]),
    ]))
    assert len(w_all) == len(schedule()[2])
    arrays = {
        "w_tiles": w_all, "ada_tiles": np.ascontiguousarray(a["w_ada_2"][0].T).reshape(6 * KD, P, D),
        "c_in": np.ascontiguousarray(np.broadcast_to(a["c_2"][0], (P, D))),
        "x_in": np.ascontiguousarray(a["x"][0].T.reshape(KD, P, S).transpose(1, 0, 2)),
        "vec_in": vec, "const_in": const, "rope_in": rope, "mask1_in": mask1, "mask2_in": mask2,
        "gsgu_in": np.ascontiguousarray(np.broadcast_to(a["g_sgu_2"][0], (P, A_W))),
        "wsp_in": np.ascontiguousarray(a["w_sp_2"][0].transpose(2, 0, 1)),
        "pos_in": np.ascontiguousarray(np.broadcast_to(a["positions_2"][0], (P, S))),
    }
    nc = _bacc.Bacc("TRN2", target_bir_lowering=False, num_devices=1)
    aps = {n: nc.dram_tensor(n, v.shape, mybir.dt.from_np(v.dtype), kind="ExternalInput").ap()
           for n, v in arrays.items()}
    out = nc.dram_tensor("out_x", (P, KD, S), F32, kind="ExternalOutput").ap()
    build(nc, out=out, **aps)
    r = _run(nc, [arrays], core_ids=[0])
    got = r.results[0]["out_x"]
    return np.ascontiguousarray(got.transpose(1, 0, 2).reshape(D, S).T)[None]
```
